# Optimizing a Trainium2 kernel written in Bass

```python
import jax, jax.numpy as jnp
from jax import lax
import numpy as np

D_MODEL = 1024
BATCH = 1
SEQ = 256
DEPTH = 2

CTX_LEN = 256
GRID_W = 64
ROPE_BASE = 10000.0
NORM_EPS = 1e-6
LN_EPS = 1e-5
NEG_INF = -1e30
N_MOD = 9
FFN_RES = 0.5
D_FF = 2816

A_HEADS = 8
A_KV_HEADS = 2
A_HEAD_DIM = 64
A_WINDOW = 128
A_BLOCK = 128
B_CH = 512
B_KERNEL = 31
A_Q_W = A_HEADS * A_HEAD_DIM
A_KV_W = A_KV_HEADS * A_HEAD_DIM
AB_IN_W = A_Q_W + 2 * A_KV_W + 2 * B_CH
AB_OUT_W = A_Q_W + B_CH

C_HEADS = 8
C_Q_LORA = 256
C_KV_LORA = 256
C_NOPE = 128
C_ROPE = 64
C_V = 128
C_BLOCK = 128

kernel_name = "hybrid_prefix_dit_macaron_block"

def rms_norm(x, g):
    xf = x.astype(jnp.float32)
    y = xf * lax.rsqrt(jnp.mean(xf * xf, axis=-1, keepdims=True) + NORM_EPS)
    return (y * g.astype(jnp.float32)).astype(x.dtype)

def layer_norm(x, g, b):
    xf = x.astype(jnp.float32)
    mu = jnp.mean(xf, axis=-1, keepdims=True)
    xc = xf - mu
    var = jnp.mean(xc * xc, axis=-1, keepdims=True)
    y = xc * lax.rsqrt(var + LN_EPS) * g.astype(jnp.float32) + b.astype(jnp.float32)
    return y.astype(x.dtype)

def modulate(xn, shift, scale):
    return xn * (1 + scale) + shift

def axial_rope_tables(rows, d_rot):
    t = jnp.arange(rows * GRID_W)
    row = (t // GRID_W).astype(jnp.float32)
    col = (t % GRID_W).astype(jnp.float32)
    d_axis = d_rot // 2
    inv_freq = ROPE_BASE ** (-jnp.arange(0, d_axis, 2, dtype=jnp.float32) / d_axis)
    ang_r = row[:, None] * inv_freq
    ang_c = col[:, None] * inv_freq
    ang = jnp.concatenate([ang_r, ang_r, ang_c, ang_c], axis=-1)
    return jnp.cos(ang), jnp.sin(ang)

def apply_rope(x, cos, sin):
    d = x.shape[-1]
    xr = x.reshape(x.shape[:-1] + (2, 2, d // 4))
    rot = jnp.stack([-xr[..., 1, :], xr[..., 0, :]], axis=-2).reshape(x.shape)
    cos = cos[:, None, :].astype(x.dtype)
    sin = sin[:, None, :].astype(x.dtype)
    return x * cos + rot * sin

def swiglu(h, w_in, w_out):
    g, u = jnp.split(h @ w_in, 2, axis=-1)
    return (jax.nn.silu(g) * u) @ w_out

def ffn_sublayer(x, g, shift, scale, gate, w_in, w_out):
    return x + FFN_RES * gate * swiglu(modulate(rms_norm(x, g), shift, scale), w_in, w_out)

def softmax_with_sink(s, sink):
    s_all = jnp.concatenate([s, jnp.broadcast_to(sink, s.shape[:-1] + (1,))], axis=-1)
    return jax.nn.softmax(s_all, axis=-1)[..., :-1]

def attend(q, k, v, ok, sink, scale):
    s = jnp.einsum('bqhgd,bkhd->bhgqk', q, k).astype(jnp.float32) * scale
    if ok is not None:
        s = jnp.where(ok, s, NEG_INF)
    if sink is not None:
        p = softmax_with_sink(s, sink[None, :, :, None, None])
    else:
        p = jax.nn.softmax(s, axis=-1)
    o = jnp.einsum('bhgqk,bkhd->bqhgd', p.astype(v.dtype), v)
    return o.reshape(o.shape[:2] + (-1,))

def window_gqa(q, k, v, kc, vc, sink, scale):
    B, S = q.shape[:2]
    nb = S // A_BLOCK
    L = kc.shape[1]
    pad = ((0, 0), (A_BLOCK, A_BLOCK), (0, 0), (0, 0))
    k_pad = jnp.pad(k, pad)
    v_pad = jnp.pad(v, pad)
    ctx_ok = jnp.ones((A_BLOCK, L), dtype=bool)

    def block(n):
        start = n * A_BLOCK
        q_n = lax.dynamic_slice_in_dim(q, start, A_BLOCK, axis=1)
        k_n = jnp.concatenate([lax.dynamic_slice_in_dim(k_pad, start, 3 * A_BLOCK, axis=1), kc], axis=1)
        v_n = jnp.concatenate([lax.dynamic_slice_in_dim(v_pad, start, 3 * A_BLOCK, axis=1), vc], axis=1)
        q_pos = start + jnp.arange(A_BLOCK)
        k_pos = start - A_BLOCK + jnp.arange(3 * A_BLOCK)
        near = ((jnp.abs(q_pos[:, None] - k_pos[None, :]) <= A_WINDOW)
                & (k_pos >= 0)[None, :] & (k_pos < S)[None, :])
        ok = jnp.concatenate([near, ctx_ok], axis=1)
        return attend(q_n, k_n, v_n, ok, sink, scale)

    o = lax.map(block, jnp.arange(nb))
    return jnp.moveaxis(o, 0, 1).reshape(B, S, -1)

def conformer_conv(u, w_dw, b_dw, ln_g, ln_b):
    a, g = jnp.split(u, 2, axis=-1)
    y = a * jax.nn.sigmoid(g)
    y = lax.conv_general_dilated(
        y, w_dw[:, None, :].astype(y.dtype), window_strides=(1,),
        padding=[(B_KERNEL // 2, B_KERNEL // 2)],
        dimension_numbers=('NWC', 'WIO', 'NWC'),
        feature_group_count=y.shape[-1]) + b_dw
    return jax.nn.silu(layer_norm(y, ln_g, ln_b))

def ab_mixer(xm, hm, w_in, sink, w_dw, b_dw, ln_g, ln_b, w_out, rope, ctx_out):
    B, S, _ = xm.shape
    L = hm.shape[1]
    G = A_HEADS // A_KV_HEADS
    sink = sink.astype(jnp.float32).reshape(A_KV_HEADS, G)
    scale = A_HEAD_DIM ** -0.5
    i_k = A_Q_W
    i_v = i_k + A_KV_W
    i_u = i_v + A_KV_W
    px = xm @ w_in
    ph = hm @ w_in
    qx = apply_rope(px[..., :i_k].reshape(B, S, A_HEADS, A_HEAD_DIM), *rope)
    qx = qx.reshape(B, S, A_KV_HEADS, G, A_HEAD_DIM)
    kx = apply_rope(px[..., i_k:i_v].reshape(B, S, A_KV_HEADS, A_HEAD_DIM), *rope)
    vx = px[..., i_v:i_u].reshape(B, S, A_KV_HEADS, A_HEAD_DIM)
    kh = ph[..., i_k:i_v].reshape(B, L, A_KV_HEADS, A_HEAD_DIM)
    vh = ph[..., i_v:i_u].reshape(B, L, A_KV_HEADS, A_HEAD_DIM)
    ax = window_gqa(qx, kx, vx, kh, vh, sink, scale)
    bx = conformer_conv(px[..., i_u:], w_dw, b_dw, ln_g, ln_b)
    ox = jnp.concatenate([ax, bx], axis=-1) @ w_out
    if not ctx_out:
        return ox, None
    qh = ph[..., :i_k].reshape(B, L, A_KV_HEADS, G, A_HEAD_DIM)
    ah = attend(qh, kh, vh, None, sink, scale)
    bh = conformer_conv(ph[..., i_u:], w_dw, b_dw, ln_g, ln_b)
    oh = jnp.concatenate([ah, bh], axis=-1) @ w_out
    return ox, oh

def mla_q(h, w_dq, g_q, w_uq, rope):
    B, N, _ = h.shape
    cq = rms_norm(h @ w_dq, g_q)
    q = (cq @ w_uq).reshape(B, N, C_HEADS, C_NOPE + C_ROPE)
    q_nope, q_rope = q[..., :C_NOPE], q[..., C_NOPE:]
    if rope is not None:
        q_rope = apply_rope(q_rope, *rope)
    return jnp.concatenate([q_nope, q_rope], axis=-1)

def mla_kv(h, w_dkv, g_kv, w_uk, w_uv, rope):
    B, N, _ = h.shape
    ckv_kr = h @ w_dkv
    ckv = rms_norm(ckv_kr[..., :C_KV_LORA], g_kv)
    k_rope = ckv_kr[..., C_KV_LORA:][:, :, None, :]
    if rope is not None:
        k_rope = apply_rope(k_rope, *rope)
    k_nope = (ckv @ w_uk).reshape(B, N, C_HEADS, C_NOPE)
    v = (ckv @ w_uv).reshape(B, N, C_HEADS, C_V)
    k = jnp.concatenate([k_nope, jnp.broadcast_to(k_rope, (B, N, C_HEADS, C_ROPE))], axis=-1)
    return k, v

def mla_mixer(xm, hm, w_dq, g_q, w_uq, w_dkv, g_kv, w_uk, w_uv, w_o, rope, ctx_out):
    B, S, _ = xm.shape
    nb = S // C_BLOCK
    scale = (C_NOPE + C_ROPE) ** -0.5
    qx = mla_q(xm, w_dq, g_q, w_uq, rope)
    kx, vx = mla_kv(xm, w_dkv, g_kv, w_uk, w_uv, rope)
    kh, vh = mla_kv(hm, w_dkv, g_kv, w_uk, w_uv, None)
    k_all = jnp.concatenate([kx, kh], axis=1)
    v_all = jnp.concatenate([vx, vh], axis=1)

    def block(n):
        q_n = lax.dynamic_slice_in_dim(qx, n * C_BLOCK, C_BLOCK, axis=1)[:, :, :, None, :]
        return attend(q_n, k_all, v_all, None, None, scale)

    o = lax.map(block, jnp.arange(nb))
    ox = jnp.moveaxis(o, 0, 1).reshape(B, S, -1) @ w_o
    if not ctx_out:
        return ox, None
    qh = mla_q(hm, w_dq, g_q, w_uq, None)
    oh = attend(qh[:, :, :, None, :], kh, vh, None, None, scale) @ w_o
    return ox, oh

def setup_inputs(seed: int = 0) -> dict:
    key = jax.random.key(seed)
    ks = jax.random.split(key, 32)
    f32 = jnp.float32
    n_even = (DEPTH + 1) // 2
    n_odd = DEPTH // 2

    def w(k, shape, fan_in, gain=1.0):
        return jax.random.normal(k, shape, f32) * (gain * fan_in ** -0.5)

    def ones_noise(k, shape):
        return 1.0 + 0.02 * jax.random.normal(k, shape, f32)

    def small(k, shape):
        return 0.02 * jax.random.normal(k, shape, f32)

    return {
        "x": jax.random.normal(ks[0], (BATCH, SEQ, D_MODEL), f32),
        "c": jax.random.normal(ks[1], (BATCH, D_MODEL), f32),
        "ctx": jax.random.normal(ks[2], (BATCH, CTX_LEN, D_MODEL), f32),
        "c_ctx": jax.random.normal(ks[3], (D_MODEL,), f32),
        "w_mod": w(ks[4], (DEPTH, D_MODEL, N_MOD * D_MODEL), D_MODEL, 0.5),
        "b_mod": small(ks[5], (DEPTH, N_MOD * D_MODEL)),
        "g_norm": ones_noise(ks[6], (DEPTH, 3, D_MODEL)),
        "ffn_w_in": w(ks[7], (DEPTH, 2, D_MODEL, 2 * D_FF), D_MODEL),
        "ffn_w_out": w(ks[8], (DEPTH, 2, D_FF, D_MODEL), D_FF),
        "ab_w_in": w(ks[9], (n_even, D_MODEL, AB_IN_W), D_MODEL),
        "a_sink": 0.5 * jax.random.normal(ks[10], (n_even, A_HEADS), f32),
        "b_w_dw": w(ks[11], (n_even, B_KERNEL, B_CH), B_KERNEL),
        "b_b_dw": small(ks[12], (n_even, B_CH)),
        "b_ln_g": ones_noise(ks[13], (n_even, B_CH)),
        "b_ln_b": small(ks[14], (n_even, B_CH)),
        "ab_w_out": w(ks[15], (n_even, AB_OUT_W, D_MODEL), AB_OUT_W),
        "c_w_dq": w(ks[16], (n_odd, D_MODEL, C_Q_LORA), D_MODEL),
        "c_g_q": ones_noise(ks[17], (n_odd, C_Q_LORA)),
        "c_w_uq": w(ks[18], (n_odd, C_Q_LORA, C_HEADS * (C_NOPE + C_ROPE)), C_Q_LORA),
        "c_w_dkv": w(ks[19], (n_odd, D_MODEL, C_KV_LORA + C_ROPE), D_MODEL),
        "c_g_kv": ones_noise(ks[20], (n_odd, C_KV_LORA)),
        "c_w_uk": w(ks[21], (n_odd, C_KV_LORA, C_HEADS * C_NOPE), C_KV_LORA),
        "c_w_uv": w(ks[22], (n_odd, C_KV_LORA, C_HEADS * C_V), C_KV_LORA),
        "c_w_o": w(ks[23], (n_odd, C_HEADS * C_V, D_MODEL), C_HEADS * C_V),
        "g_final": ones_noise(ks[24], (D_MODEL,)),
    }

def reference(x, c, ctx, c_ctx, w_mod, b_mod, g_norm, ffn_w_in, ffn_w_out,
              ab_w_in, a_sink, b_w_dw, b_b_dw, b_ln_g, b_ln_b, ab_w_out,
              c_w_dq, c_g_q, c_w_uq, c_w_dkv, c_g_kv, c_w_uk, c_w_uv, c_w_o, g_final):
    rows = x.shape[1] // GRID_W
    rope_a = axial_rope_tables(rows, A_HEAD_DIM)
    rope_c = axial_rope_tables(rows, C_ROPE)
    silu_c = jax.nn.silu(c)
    silu_cc = jax.nn.silu(c_ctx)
    h = ctx
    for i in range(DEPTH):
        last = i == DEPTH - 1
        j = i // 2
        mx = jnp.split((silu_c @ w_mod[i] + b_mod[i])[:, None, :], N_MOD, axis=-1)
        mc = jnp.split((silu_cc @ w_mod[i] + b_mod[i])[None, None, :], N_MOD, axis=-1)
        x = ffn_sublayer(x, g_norm[i, 0], mx[0], mx[1], mx[2], ffn_w_in[i, 0], ffn_w_out[i, 0])
        h = ffn_sublayer(h, g_norm[i, 0], mc[0], mc[1], mc[2], ffn_w_in[i, 0], ffn_w_out[i, 0])
        xm = modulate(rms_norm(x, g_norm[i, 1]), mx[3], mx[4])
        hm = modulate(rms_norm(h, g_norm[i, 1]), mc[3], mc[4])
        if i % 2 == 0:
            ox, oh = ab_mixer(xm, hm, ab_w_in[j], a_sink[j], b_w_dw[j], b_b_dw[j],
                              b_ln_g[j], b_ln_b[j], ab_w_out[j], rope_a, not last)
        else:
            ox, oh = mla_mixer(xm, hm, c_w_dq[j], c_g_q[j], c_w_uq[j], c_w_dkv[j], c_g_kv[j],
                               c_w_uk[j], c_w_uv[j], c_w_o[j], rope_c, not last)
        x = x + mx[5] * ox
        x = ffn_sublayer(x, g_norm[i, 2], mx[6], mx[7], mx[8], ffn_w_in[i, 1], ffn_w_out[i, 1])
        if not last:
            h = h + mc[5] * oh
            h = ffn_sublayer(h, g_norm[i, 2], mc[6], mc[7], mc[8], ffn_w_in[i, 1], ffn_w_out[i, 1])
    return rms_norm(x, g_final)


_drawn_inputs = setup_inputs


def setup_inputs(seed=0):
    import zlib

    import numpy as np

    out = dict(_drawn_inputs(seed))
    spreads = {}
    factors = {'b_mod': 2.697,
     'g_norm': 8.0,
     'a_sink': 8.0,
     'b_b_dw': 28.725,
     'b_ln_g': 37.213,
     'b_ln_b': 41.964,
     'c_g_q': 8.0,
     'c_g_kv': 22.354,
     'g_final': 23.341}
    for name, (base, spread) in spreads.items():
        noise = np.random.default_rng([zlib.crc32(name.encode()), seed]).standard_normal(out[name].shape)
        drawn = base * np.exp(spread * noise) if base else spread * noise
        out[name] = __import__('jax').numpy.asarray(drawn.astype(out[name].dtype))
    for name, factor in factors.items():
        out[name] = (out[name] * factor).astype(out[name].dtype)
    return out
```

```python
from contextlib import ExitStack

import numpy as np

import concourse.bass as bass
from concourse import mybir

P = 128
D = 1024
DT = D // P
LAT, CTX = 256, 256
TOK = LAT + CTX
D_FF = 2816
GROUPS = (8, 8, 6)
SLAB = 2048
HALF = SLAB // 2
HEADS = 8
A_DIM, A_KV, B_CH, TAPS = 64, 2, 512, 31
CT = B_CH // P
PAD = TAPS // 2
NOPE, ROPE, C_V, LORA = 128, 64, 128, 256
N_MOD = 9
MODT = N_MOD * DT
GRID_W = 64
NORM_EPS, LN_EPS = 1e-6, 1e-5
NEG = -1e30

FFN_SLABS = sum(g + 4 for g in GROUPS)
W_FFN0 = 0
W_AB = W_FFN0 + FFN_SLABS
W_FFN1 = W_AB + 7 + 4
W_FFN2 = W_FFN1 + FFN_SLABS
W_MLA = W_FFN2 + FFN_SLABS
W_FFN3 = W_MLA + 6 + 4
N_SLABS = W_FFN3 + FFN_SLABS
FFN_W = (W_FFN0, W_FFN1, W_FFN2, W_FFN3)
FFN_STEPS = sum(GROUPS)
FFN_OUTS = 4 * len(GROUPS)
B_FFN = (0, FFN_OUTS + 4, 2 * FFN_OUTS + 4, 3 * FFN_OUTS + 8)
B_AB = FFN_OUTS
B_MLA = 3 * FFN_OUTS + 4

MOD_FIRST = 2 * DT

NORMS = ("ffn0", "ab", "ln", "ffn1", "ffn2", "mla", "cq", "ckv", "ffn3", "final")
NORM_TILES = {"ln": 4, "cq": 2, "ckv": 2}
CALL = {n: i for i, n in enumerate(NORMS)}
NORM_BASE = {}
_n = 0
for _name in NORMS:
    NORM_BASE[_name] = _n
    _n += NORM_TILES.get(_name, DT)
RES = {"ffn0": 0, "ab": 1, "ffn1": 2, "ffn2": 3, "mla": 4, "ffn3": 5, "final": 6}

V_G, V_BMOD, V_GF = 0, 48, 48 + 2 * MODT
V_BDW = V_GF + DT
V_LNG = V_BDW + CT
V_LNB = V_LNG + CT
V_GQ = V_LNB + CT
V_GKV = V_GQ + 2
V_SINK = V_GKV + 2
V_WDW = V_SINK + HEADS
N_VEC = V_WDW + CT * TAPS
C_ID, C_MASK, C_COS, C_SIN = 0, P, 3 * P, 3 * P + LAT
N_CONST = C_SIN + LAT


def build(nc, tokens, cond, vecs, consts, wmod, wstream, out):
    F32, F32R, I32 = mybir.dt.float32, mybir.dt.float32r, mybir.dt.int32
    ALU, ACT, AX = mybir.AluOpType, mybir.ActivationFunctionType, mybir.AxisListType
    ds = bass.ds

    with ExitStack() as ctx:
        def sb(name, shape, dt=F32, where=ctx):
            return where.enter_context(nc.sbuf_tensor(name, shape, dt))

        def sem(name):
            return ctx.enter_context(nc.semaphore(name))

        xT = sb("xT", [P, DT, TOK])
        a_hi = sb("a_hi", [P, DT, TOK], F32R)
        a_lo = sb("a_lo", [P, DT, TOK], F32R)
        h_hi = sb("h_hi", [P, 8, TOK], F32R)
        h_lo = sb("h_lo", [P, 8, TOK], F32R)
        raw = sb("raw", [P, 2, SLAB])
        w_hi = sb("w_hi", [P, 2, SLAB], F32R)
        w_lo = sb("w_lo", [P, 2, SLAB], F32R)
        o_tok = sb("o_tok", [P, 2048])
        work = sb("work", [P, 4, TOK])
        sq = sb("sq", [P, 2, TOK])
        ss = sb("ss", [P, 2, TOK])
        diag = sb("diag", [P, 4, P])
        ones = sb("ones", [P, P])
        cst = sb("cst", [P, N_CONST])
        ident_r = sb("ident_r", [P, P], F32R)
        mask_r = sb("mask_r", [P, 2, P], F32R)
        vec = sb("vec", [P, N_VEC])
        modc = sb("modc", [P, 2, 2 * MODT])
        stage = sb("stage", [P, 2, 4])
        shift = sb("shift", [P, 6, 2, DT])
        scale = sb("scale", [P, 6, 2, DT])
        gate = sb("gate", [P, 6, 2, DT])
        mtmp = sb("mtmp", [P, 2, DT])
        nsink = sb("nsink", [P, HEADS])
        smax = sb("smax", [P, 32])
        nmax = sb("nmax", [P, 32])
        den = sb("den", [P, 32])
        esink = sb("esink", [P, 32])
        rinv = sb("rinv", [P, 32])
        rv = sb("rv", [P, 4])
        ri = sb("ri", [P, 4], I32)
        ry = sb("ry", [P, 4])
        rt = sb("rt", [P, 4])
        with ExitStack() as first:
            mring = sb("mring", [P, 4, D], where=first)
            cb = sb("cb", [P, 2, D], where=first)
            unread = sb("unread", [P, D], mybir.dt.bfloat16, where=first)
            ypad = sb("ypad", [P, CT, 2, LAT + 2 * PAD], where=first)
            conv = sb("conv", [P, CT, TOK], where=first)
        q_hi = sb("q_hi", [P, 7, TOK], F32R)
        q_lo = sb("q_lo", [P, 7, TOK], F32R)
        l_hi = sb("l_hi", [P, 3, TOK], F32R)
        l_lo = sb("l_lo", [P, 3, TOK], F32R)
        ident = cst[:, C_ID:C_ID + P]
        cos, sin = cst[:, C_COS:C_COS + LAT], cst[:, C_SIN:C_SIN + LAT]
        xn, full = work[:, 0:2], work[:, 2:4]
        sil, prod = work[:, 0:2], work[:, 2:4]
        probs = work[:, 0:3]
        ps = [ctx.enter_context(nc.psum_tensor(f"ps{i}", [P, 512], F32)) for i in range(8)]
        OUTB = 4
        S_BANK, PT_BANK, O_BANK, LN_BANK, NORM_BANK = (1, 4, 5), (6, 7), (0, 3), 2, 6

        in_tok = sem("in_tok")
        in_cond = sem("in_cond")
        in_small = sem("in_small")
        raw_loaded = [sem(f"raw_loaded{i}") for i in range(2)]
        hi_ready = sem("hi_ready")
        lo_ready = sem("lo_ready")
        slab_done = sem("slab_done")
        mod_loaded = [sem(f"mod_loaded{i}") for i in range(4)]
        mod_first = sem("mod_first")
        mod_dots = sem("mod_dots")
        mod_cols = sem("mod_cols")
        cond_ready = sem("cond_ready")
        gp_const = sem("gp_const")
        act_const = sem("act_const")
        chain = sem("chain")
        sq_ready = [sem(f"sq_ready{i}") for i in range(2)]
        ss_sum = [sem(f"ss_sum{i}") for i in range(2)]
        colsum = sem("colsum")
        diag_ready = sem("diag_ready")
        rstd_bc = sem("rstd_bc")
        xn_ready = sem("xn_ready")
        nhi_ready = sem("nhi_ready")
        normed = sem("normed")
        pair_free = sem("pair_free")
        sil_ready = sem("sil_ready")
        hhi_ready = sem("hhi_ready")
        hid_ready = sem("hid_ready")
        tile0_done = sem("tile0_done")
        out_free = [sem(f"out_free{i}") for i in range(2)]
        glu_sig = sem("glu_sig")
        glu_done = sem("glu_done")
        conv_op = sem("conv_op")
        step_done = sem("step_done")
        rope_ctx = sem("rope_ctx")
        rope_full = sem("rope_full")
        piece_hi = sem("piece_hi")
        piece_lo = sem("piece_lo")
        scores_done = sem("scores_done")
        nmax_ready = sem("nmax_ready")
        exp_done = sem("exp_done")
        sink_done = sem("sink_done")
        pt_done = sem("pt_done")
        pt_hi = sem("pt_hi")
        pt_lo = sem("pt_lo")
        pv_done = sem("pv_done")
        o_done = sem("o_done")
        ot_done = sem("ot_done")
        ot_hi = sem("ot_hi")
        ot_lo = sem("ot_lo")
        ln_sum = sem("ln_sum")
        ln_mean = sem("ln_mean")
        ln_cent = sem("ln_cent")
        stat_sq = sem("stat_sq")
        stat_add = sem("stat_add")
        stat_ready = sem("stat_ready")
        lat_copy = sem("lat_copy")
        y_ready = sem("y_ready")
        stored = sem("stored")

        def cols(hi, lo, i, a=0, b=TOK):
            return hi[:, i, a:b], lo[:, i, a:b]

        AB_PIECES = []
        for t in range(4):
            AB_PIECES.append((ps[t % 2 + 2 * (t // 2 % 2)], *cols(h_hi, h_lo, t), ((0, LAT),),
                              (slab_done, W_AB + 5 + t // 2)))
        AB_PIECES.append((ps[0], *cols(h_hi, h_lo, 4), ((0, LAT),), (step_done, 1)))
        AB_PIECES.append((ps[1], *cols(h_hi, h_lo, 5), (), (slab_done, W_AB + 7)))
        MLA_STEPS = [[("kr", 0)], [("q", 0), ("q", 1)], [("q", 2), ("q", 3)], [("q", 4), ("q", 5)]]
        MLA_STEPS += [[("kn", 2 * i), ("kn", 2 * i + 1)] for i in range(4)]
        MLA_STEPS += [[("v", 2 * i), ("v", 2 * i + 1)] for i in range(4)]
        MLA_SIGNAL, n_step = [], 1
        for i in range(len(MLA_STEPS)):
            ends = {1: W_MLA + 3, 3: W_MLA + 4, 7: W_MLA + 5, 11: W_MLA + 6}.get(i)
            if ends is None:
                n_step += 1
                MLA_SIGNAL.append((step_done, n_step))
            else:
                MLA_SIGNAL.append((slab_done, ends))
        MLA_PIECES, MLA_PIECES_BY = [], []
        for i, parts in enumerate(MLA_STEPS):
            for t, (kind, n) in enumerate(parts):
                bank = ps[2 * (i % 2) + t]
                if kind == "kr":
                    piece = (bank, *cols(q_hi, q_lo, 6), ((0, LAT),), MLA_SIGNAL[i])
                elif kind == "q":
                    piece = (bank, *cols(q_hi, q_lo, n), ((0, LAT), (LAT, TOK)) if n >= 4 else (), MLA_SIGNAL[i])
                elif kind == "kn":
                    piece = (bank, *cols(a_hi, a_lo, n), (), MLA_SIGNAL[i])
                else:
                    piece = (bank, *cols(h_hi, h_lo, n), (), MLA_SIGNAL[i])
                MLA_PIECES.append(piece)
            MLA_PIECES_BY.append(len(AB_PIECES) + len(MLA_PIECES))
        N_AB = len(AB_PIECES)
        ROPE_INDEX = {}
        CTX_INDEX = {}
        for j, p in enumerate(AB_PIECES + MLA_PIECES):
            if p[3]:
                ROPE_INDEX[j] = len(ROPE_INDEX)
                if len(p[3]) == 1:
                    CTX_INDEX[j] = len(CTX_INDEX)

        AB_UNITS = [(h, qt) for h in range(HEADS) for qt in range(4)]
        MLA_UNITS = [(h, qt) for h in range(HEADS) for qt in range(2)]

        block = ctx.enter_context(nc.Block())

        @block.sync
        def _(sp):
            def slab(w, slot, wait=None):
                if wait is not None:
                    sp.wait_ge(lo_ready, wait)
                sp.dma_start(raw[:, slot], wstream[ds(w, 1)].rearrange("a p n -> p (a n)")) \
                  .then_inc(raw_loaded[slot], 16)

            def mod_tile(n, slot, wait=None):
                if wait is not None:
                    sp.wait_ge(mod_dots, wait)
                sp.dma_start(mring[:, slot], wmod[ds(n, 1)].rearrange("a p n -> p (a n)")) \
                  .then_inc(mod_loaded[slot], 16)

            sp.dma_start(cb[:], cond.partition_broadcast(P)).then_inc(in_cond, 16)
            for n in range(4):
                mod_tile(n, n)
            sp.dma_start(vec[:], vecs).then_inc(in_small, 16)
            sp.dma_start(xT[:], tokens).then_inc(in_tok, 16)
            with sp.Fori(0, MOD_FIRST - 7, 4) as n:
                for j in range(4):
                    mod_tile(n + (4 + j), j, n + (j + 1))
            sp.dma_start(cst[:], consts).then_inc(in_small, 16)
            for w in range(2):
                slab(w, w)
            for w in range(2, 4):
                slab(w, w % 2, w - 1)
            for j in range(4):
                mod_tile(MOD_FIRST + j, j, MOD_FIRST + j - 3)

            def both(w0, n0, turns):
                with sp.Fori(0, turns) as i:
                    for j in range(2):
                        for k in range(2):
                            n = i * 4 + (n0 + 2 * j + k)
                            mod_tile(n, 2 * j + k, n - 3)
                        w = i * 2 + (w0 + j)
                        slab(w, (w0 + j) % 2, w - 1)

            both(4, MOD_FIRST + 4, 17)
            for w in range(38, W_FFN1 + 4):
                slab(w, w % 2, w - 1)
            left = 2 * MODT - (MOD_FIRST + 4 + 68)
            both(W_FFN1 + 4, MOD_FIRST + 4 + 68, left // 4)
            w1 = W_FFN1 + 4 + left // 2
            with sp.Fori(w1, w1 + (N_SLABS - w1) // 2 * 2 - 1, 2) as w:
                for j in range(2):
                    slab(w + j, (w1 + j) % 2, w + (j - 1))
            if (N_SLABS - w1) % 2:
                slab(N_SLABS - 1, (N_SLABS - 1) % 2, N_SLABS - 2)
            for k in range(DT):
                sp.wait_ge(y_ready, k + 1)
                sp.dma_start(out[:, k], o_tok[:, k * LAT:(k + 1) * LAT]).then_inc(stored, 16)
            sp.wait_ge(stored, 16 * DT)

        @block.gpsimd
        def _(pool):
            pool.memset(ones[:], 1.0).then_inc(gp_const, 1)
            pool.memset(ypad[:], 0.0).then_inc(gp_const, 1)

            def split_lo(w, slot):
                pool.wait_ge(hi_ready, w + 1)
                pool.tensor_tensor(w_lo[:, slot], raw[:, slot], w_hi[:, slot].bitcast(F32),
                                   ALU.subtract).then_inc(lo_ready, 1)

            with pool.Fori(0, N_SLABS // 2 * 2 - 1, 2) as w:
                for j in range(2):
                    split_lo(w + j, j)
            if N_SLABS % 2:
                split_lo(N_SLABS - 1, 0)

        @block.scalar
        def _(act):
            def split_hi(w, slot, base, i=None):
                value = 16 * (base // 2 + 1)
                act.wait_ge(raw_loaded[slot], value if i is None else i * 16 + value)
                act.activation(w_hi[:, slot], raw[:, slot], ACT.Copy).then_inc(hi_ready, 1)

            def squares(n, sl, t, nt, i=None):
                k = sl if i is None else i + sl
                act.wait_ge(ss_sum[t], k + (5 * n + 1 if t else 4 * n))
                m = 2 * sl + t if i is None else i * 2 + (2 * sl + t)
                src = xT[:, m, 0:nt] if i is None else xT[:, ds(m, 1), 0:nt].rearrange("p a n -> p (a n)")
                act.activation(sq[:, t, 0:nt], src, ACT.Square).then_inc(sq_ready[t], 1)

            def norm_apply(name, tiles, emit):
                base = NORM_BASE[name]
                for k in range(tiles):
                    act.wait_ge(xn_ready, base + k + 1)
                    if k >= 2:
                        act.wait_ge(normed, base + k - 1)
                    emit(k)

            def modulated(name, s, nt):
                streams = nt // LAT

                def emit(k):
                    for dst in (full[:, k % 2], a_hi[:, k]):
                        for v in range(streams):
                            c = slice(v * LAT, (v + 1) * LAT)
                            last = act.activation(dst[:, c], xn[:, k % 2, c], ACT.Identity,
                                                  bias=shift[:, s, v, k:k + 1], scale=scale[:, s, v, k:k + 1])
                    last.then_inc(nhi_ready, 1)
                norm_apply(name, DT, emit)

            def ffn(s, name, nt, next_norm):
                modulated(name, (0, 2, 3, 5)[s], nt)
                w, f, b = FFN_W[s], s * FFN_STEPS, B_FFN[s]
                for g, size in enumerate(GROUPS):
                    with act.Fori(0, size - 1, 2) as i:
                        for j in range(2):
                            act.wait_ge(slab_done, i + (w + j + 1))
                            act.activation(sil[:, (f + j) % 2, 0:nt], ps[2 * ((f + j) % 2)][:, 0:nt],
                                           ACT.Silu).then_inc(sil_ready, 1)
                            act.wait_ge(pair_free, i + (f + j + 3))
                            act.activation(h_hi[:, ds(i + j, 1), 0:nt].rearrange("p a n -> p (a n)"),
                                           prod[:, (f + j) % 2, 0:nt], ACT.Copy).then_inc(hhi_ready, 1)
                            act.wait_ge(raw_loaded[(w + j) % 2], i * 8 + 16 * ((w + j + 2) // 2 + 1))
                            act.activation(w_hi[:, (w + j) % 2], raw[:, (w + j) % 2],
                                           ACT.Copy).then_inc(hi_ready, 1)
                    w, f = w + size, f + size
                    last = g == len(GROUPS) - 1

                    def out_step(j, i=None, split=True):
                        k = (lambda x: x) if i is None else (lambda x: i + x)
                        if last:
                            for t in range(2):
                                act.wait_ge(out_free[t], k(b + j + 3))
                                squares(RES[next_norm], j, t, nt, i)
                        if split:
                            act.wait_ge(slab_done, k(w + j + 1))
                            value = 16 * ((w + j + 2) // 2 + 1)
                            act.wait_ge(raw_loaded[(w + j) % 2], value if i is None else i * 8 + value)
                            act.activation(w_hi[:, (w + j) % 2], raw[:, (w + j) % 2],
                                           ACT.Copy).then_inc(hi_ready, 1)
                    if w + 4 == N_SLABS:
                        for j in range(4):
                            out_step(j, split=j < 2)
                    else:
                        with act.Fori(0, 3, 2) as i:
                            for j in range(2):
                                out_step(j, i)
                    w, b = w + 4, b + 4

            def pieces(j, piece, base_wait=None):
                src, hi, _, runs, (s, value) = piece
                act.wait_ge(s, value)
                if runs:
                    r = ROPE_INDEX[j]
                    if len(runs) == 1:
                        if j >= 2:
                            act.wait_ge(piece_lo, j - 1)
                        act.activation(full[:, r % 2, LAT:TOK], src[:, LAT:TOK], ACT.Copy).then_inc(rope_ctx, 1)
                    act.wait_ge(rope_full, r + 1)
                    act.activation(hi, full[:, r % 2], ACT.Copy).then_inc(piece_hi, 1)
                else:
                    act.activation(hi, src[:], ACT.Copy).then_inc(piece_hi, 1)

            def attention(units, u0, sink, factor, pt_dst, n_keys):
                for i in range(len(units) + 2):
                    if i < len(units):
                        h, qt = units[i]
                        u = u0 + i
                        nk = n_keys(qt)
                        act.wait_ge(nmax_ready, u + 1)
                        if i >= 3:
                            act.wait_ge(pt_done, u - 2)
                        act.activation(probs[:, i % 3, TOK - nk:TOK], ps[S_BANK[i % 3]][:, TOK - nk:TOK], ACT.Exp,
                                       bias=nmax[:, i:i + 1], scale=factor,
                                       accum_out=den[:, i:i + 1]).then_inc(exp_done, 1)
                        if sink:
                            act.activation(esink[:, i:i + 1], vec[:, V_SINK + h:V_SINK + h + 1], ACT.Exp,
                                           bias=nmax[:, i:i + 1]).then_inc(sink_done, 1)
                    if i >= 2:
                        e = i - 2
                        u = u0 + e
                        nk = n_keys(units[e][1])
                        act.wait_ge(pt_done, u + 1)
                        if e >= 2:
                            act.wait_ge(pv_done, u - 1)
                        act.activation(pt_dst[:, e % 2, TOK - nk:TOK], ps[PT_BANK[e % 2]][:, TOK - nk:TOK],
                                       ACT.Copy).then_inc(pt_hi, 1)

            def turned(tiles, base, nt):
                for c in range(tiles):
                    act.wait_ge(ot_done, base + c + 1)
                    act.activation(a_hi[:, c, 0:nt], ps[PT_BANK[c % 2]][:, 0:nt], ACT.Copy).then_inc(ot_hi, 1)

            def mixer_out(w, b, nt, next_norm):
                for j in range(4):
                    for t in range(2):
                        act.wait_ge(out_free[t], b + j + 3)
                        squares(RES[next_norm], j, t, nt)
                    act.wait_ge(slab_done, w + j + 1)
                    split_hi(w + j + 2, (w + j) % 2, w + j + 2)

            act.wait_ge(in_cond, 16)
            act.activation(cb[:], cb[:], ACT.Silu).then_inc(cond_ready, 1)
            act.wait_ge(in_tok, 16)
            for sl in range(4):
                for t in range(2):
                    squares(0, sl, t, TOK)
            act.wait_ge(in_small, 32)
            act.activation(ident_r[:], ident, ACT.Copy).then_inc(act_const, 1)
            act.activation(mask_r[:], cst[:, C_MASK:C_MASK + 2 * P].rearrange("p (a n) -> p a n", a=2),
                           ACT.Copy).then_inc(act_const, 1)
            split_hi(0, 0, 0)
            split_hi(1, 1, 1)
            ffn(0, "ffn0", TOK, "ab")

            modulated("ab", 1, TOK)
            w = W_AB
            for c in range(CT):
                act.wait_ge(slab_done, w + c + 1)
                if c >= 2:
                    act.wait_ge(glu_done, c - 1)
                act.activation(sil[:, c % 2], ps[2 * (c % 2) + 1][:], ACT.Sigmoid).then_inc(glu_sig, 1)
                split_hi(w + c + 2, (w + c) % 2, w + c + 2)
            for j in range(N_AB):
                pieces(j, AB_PIECES[j])
                if j in (1, 3, 5):
                    x = w + 4 + j // 2
                    split_hi(x + 2, x % 2, x + 2)
            attention(AB_UNITS, 0, True, A_DIM ** -0.5, h_hi[:, 6:8], lambda qt: TOK if qt < 2 else CTX)
            turned(4, 0, TOK)
            for c in range(CT):
                act.wait_ge(ln_cent, c + 1)
                if c >= 2:
                    act.wait_ge(stat_add, 1)
                act.activation(sq[:, c % 2], conv[:, c], ACT.Square).then_inc(stat_sq, 1)

            def ln_emit(k):
                act.activation(full[:, k % 2], xn[:, k % 2], ACT.Silu, bias=vec[:, V_LNB + k:V_LNB + k + 1],
                               scale=vec[:, V_LNG + k:V_LNG + k + 1])
                act.activation(a_hi[:, 4 + k], xn[:, k % 2], ACT.Silu, bias=vec[:, V_LNB + k:V_LNB + k + 1],
                               scale=vec[:, V_LNG + k:V_LNG + k + 1]).then_inc(nhi_ready, 1)
            norm_apply("ln", CT, ln_emit)
            mixer_out(W_AB + 7, B_AB, TOK, "ffn1")

            ffn(1, "ffn1", TOK, "ffn2")
            ffn(2, "ffn2", TOK, "mla")

            modulated("mla", 4, TOK)
            w = W_MLA
            for i, nt in ((0, LAT), (1, TOK)):
                act.wait_ge(slab_done, w + i + 1)
                for t in range(2):
                    dst = o_tok[:, t * LAT:(t + 1) * LAT] if i == 0 else o_tok[:, (1 + t) * TOK:(2 + t) * TOK]
                    act.activation(dst, ps[2 * i + t][:, 0:nt], ACT.Copy).then_inc(lat_copy, 1)
                    if i:
                        act.wait_ge(stat_ready, 1)
                    act.activation(sq[:, t, 0:nt], ps[2 * i + t][:, 0:nt], ACT.Square).then_inc(stat_sq, 1)
                split_hi(w + i + 2, (w + i) % 2, w + i + 2)

            def lora_emit(g, nt, dst):
                def emit(k):
                    gcol = vec[:, g + k:g + k + 1]
                    act.activation(full[:, k % 2, 0:nt], xn[:, k % 2, 0:nt], ACT.Copy, scale=gcol)
                    act.activation(dst(k), xn[:, k % 2, 0:nt], ACT.Copy, scale=gcol).then_inc(nhi_ready, 1)
                return emit
            norm_apply("cq", 2, lora_emit(V_GQ, LAT, lambda k: l_hi[:, 0, k * LAT:(k + 1) * LAT]))
            norm_apply("ckv", 2, lora_emit(V_GKV, TOK, lambda k: l_hi[:, 1 + k]))
            act.wait_ge(normed, NORM_BASE["ckv"] + 2)
            j = N_AB
            for i, parts in enumerate(MLA_STEPS):
                for _ in parts:
                    pieces(j, MLA_PIECES[j - N_AB])
                    j += 1
                if MLA_SIGNAL[i][0] is slab_done:
                    x = MLA_SIGNAL[i][1] - 1
                    split_hi(x + 2, x % 2, x + 2)
            attention(MLA_UNITS, len(AB_UNITS), False, (NOPE + ROPE) ** -0.5, l_hi[:, 0:2], lambda qt: TOK)
            turned(DT, 4, LAT)
            mixer_out(W_MLA + 6, B_MLA, LAT, "ffn3")

            ffn(3, "ffn3", LAT, "final")
            base = NORM_BASE["final"]
            for k in range(DT):
                act.wait_ge(xn_ready, base + k + 1)
                act.activation(o_tok[:, k * LAT:(k + 1) * LAT], xn[:, k % 2, 0:LAT], ACT.Copy,
                               scale=vec[:, V_GF + k:V_GF + k + 1]).then_inc(y_ready, 1)

        @block.vector
        def _(dve):
            count = [0]

            def link(ins):
                count[0] += 1
                ins.then_inc(chain, 1)
                dve.wait_ge(chain, count[0])

            def mod_dot(slot, value, n):
                dve.wait_ge(mod_loaded[slot], value)
                dve.wait_ge(mod_first, n + 1)
                dve.tensor_tensor_reduce(unread[:], mring[:, slot], cb[:, 0], 1.0, 0.0,
                                         ALU.mult, ALU.add, stage[:, 0, slot:slot + 1]).then_inc(mod_first, 1)
                dve.tensor_tensor_reduce(mring[:, slot], mring[:, slot], cb[:, 1], 1.0, 0.0, ALU.mult, ALU.add,
                                         stage[:, 1, slot:slot + 1]).then_inc(mod_dots, 1)

            def mod_store(n, done):
                dve.wait_ge(mod_dots, done)
                dve.tensor_copy(modc[:, :, ds(n, 4)], stage[:]).then_inc(mod_cols, 4)
                dve.wait_ge(mod_cols, done)

            def finalize(layer, place, parts=("shift", "scale", "gate")):
                s = 3 * layer + place
                base = layer * MODT + place * 3 * DT

                def summed(dst, c):
                    b = vec[:, V_BMOD + base + c * DT:V_BMOD + base + (c + 1) * DT]
                    return dve.tensor_tensor(dst, modc[:, :, base + c * DT:base + (c + 1) * DT],
                                             b.unsqueeze(1).to_broadcast([P, 2, DT]), ALU.add)
                if "shift" in parts:
                    link(summed(shift[:, s], 0))
                if "scale" in parts:
                    link(summed(mtmp[:], 1))
                    g = vec[:, V_G + s * DT:V_G + (s + 1) * DT].unsqueeze(1).to_broadcast([P, 2, DT])
                    link(dve.scalar_tensor_tensor(out=scale[:, s], in0=mtmp[:], scalar=1.0, in1=g,
                                                  op0=ALU.add, op1=ALU.mult))
                if "gate" in parts:
                    link(summed(mtmp[:], 2))
                    link(dve.tensor_scalar(gate[:, s], mtmp[:], 1.0 if place == 1 else 0.5, None, ALU.mult))

            def zero_sum(n):
                dve.memset(ss[:, 0], 0.0).then_inc(ss_sum[1], 1)

            def add_square(n, sl, t, nt, i=None):
                k = (lambda x: x) if i is None else (lambda x: i + x)
                dve.wait_ge(sq_ready[t], k(4 * n + sl + 1))
                if t:
                    dve.wait_ge(ss_sum[0], k(4 * n + sl + 1))
                else:
                    dve.wait_ge(ss_sum[1], k(5 * n + sl + 1))
                dve.tensor_tensor(ss[:, 0, 0:nt], ss[:, 0, 0:nt], sq[:, t, 0:nt], ALU.add).then_inc(ss_sum[t], 1)

            def rsqrt(name, bank, nt, inv_n, eps):
                c = nt // P
                dve.wait_ge(colsum, CALL[name] + 1)
                link(dve.tensor_scalar(rv[:, 0:c], ps[bank][:, 0:c], inv_n, eps, ALU.mult, ALU.add))
                link(dve.tensor_scalar(ri[:, 0:c], rv[:, 0:c].bitcast(I32), 1, None, ALU.logical_shift_right))
                link(dve.tensor_scalar(ri[:, 0:c], ri[:, 0:c], -1.0, float(0x5F3759DF), ALU.mult, ALU.add))
                y = ri[:, 0:c].bitcast(F32)
                for _ in range(3):
                    link(dve.scalar_tensor_tensor(out=rt[:, 0:c], in0=y, scalar=-0.5, in1=y,
                                                  op0=ALU.mult, op1=ALU.mult))
                    link(dve.tensor_tensor(rt[:, 0:c], rt[:, 0:c], rv[:, 0:c], ALU.mult))
                    link(dve.scalar_tensor_tensor(out=ry[:, 0:c], in0=rt[:, 0:c], scalar=1.5, in1=y,
                                                  op0=ALU.add, op1=ALU.mult))
                    y = ry[:, 0:c]
                dve.tensor_tensor(diag[:, 0:c], ident.unsqueeze(1).to_broadcast([P, c, P]),
                                  ry[:, 0:c].unsqueeze(2).to_broadcast([P, c, P]), ALU.mult).then_inc(diag_ready, 1)

            def norm_apply(name, bank, tiles, nt, src, dst_hi, dst_lo):
                base = NORM_BASE[name]
                dve.wait_ge(rstd_bc, CALL[name] + 1)
                for k in range(tiles + 1):
                    if k < tiles:
                        dve.tensor_tensor(xn[:, k % 2, 0:nt], src(k), ps[bank][:, 0:nt],
                                          ALU.mult).then_inc(xn_ready, 1)
                    if k >= 1:
                        e = k - 1
                        dve.wait_ge(nhi_ready, base + e + 1)
                        dve.tensor_tensor(dst_lo(e), full[:, e % 2, 0:nt], dst_hi(e).bitcast(F32),
                                          ALU.subtract).then_inc(normed, 1)

            def residual_norm(name, nt):
                rsqrt(name, NORM_BANK, nt, 1.0 / D, NORM_EPS)
                norm_apply(name, NORM_BANK, DT, nt, lambda k: xT[:, k, 0:nt], lambda k: a_hi[:, k, 0:nt],
                           lambda k: a_lo[:, k, 0:nt])

            def out_tiles(s, b, w, j, nt, i=None):
                k = (lambda x: x) if i is None else (lambda x: i + x)
                for t in range(2):
                    dve.wait_ge(*((slab_done, k(w + j + 1)) if t else (tile0_done, k(b + j + 1))))
                    bank = ps[OUTB + 2 * ((b + j) % 2) + t]
                    m = 2 * j + t if i is None else i * 2 + (2 * j + t)
                    for v in range(nt // LAT):
                        c = slice(v * LAT, (v + 1) * LAT)
                        if i is None:
                            x, g = xT[:, m, c], gate[:, s, v, m:m + 1]
                        else:
                            x, g = xT[:, ds(m, 1), c].rearrange("p a n -> p (a n)"), gate[:, s, v, ds(m, 1)]
                        last = dve.scalar_tensor_tensor(out=x, in0=bank[:, c], scalar=g, in1=x,
                                                        op0=ALU.mult, op1=ALU.add)
                    last.then_inc(out_free[t], 1)

            def ffn(s, name, nt, next_norm, mods=0, n0=0, after_first=None):
                residual_norm(name, nt)
                sub = (0, 2, 3, 5)[s]
                w, f, b = FFN_W[s], s * FFN_STEPS, B_FFN[s]
                phase = 0
                for g, size in enumerate(GROUPS):
                    with dve.Fori(0, size - 1, 2) as i:
                        for j in range(2):
                            slot = (f + j) % 2
                            dve.wait_ge(sil_ready, i + (f + j + 1))
                            dve.tensor_tensor(prod[:, slot, 0:nt], sil[:, slot, 0:nt], ps[2 * slot + 1][:, 0:nt],
                                              ALU.mult).then_inc(pair_free, 1)
                            if phase < mods:
                                mod_dot(2 * j, i * 8 + 16 * (n0 // 4 + 1), i * 2 + (n0 + 2 * j))
                            dve.wait_ge(hhi_ready, i + (f + j + 1))
                            hi = h_hi[:, ds(i + j, 1), 0:nt].rearrange("p a n -> p (a n)").bitcast(F32)
                            lo = h_lo[:, ds(i + j, 1), 0:nt].rearrange("p a n -> p (a n)")
                            dve.tensor_tensor(lo, prod[:, slot, 0:nt], hi, ALU.subtract).then_inc(hid_ready, 1)
                            if phase < mods:
                                mod_dot(2 * j + 1, i * 8 + 16 * (n0 // 4 + 1), i * 2 + (n0 + 2 * j + 1))
                        if phase < mods:
                            mod_store(i * 2 + n0, i * 2 + (n0 + 4))
                    if phase < mods:
                        n0 += 2 * size
                    phase += 1
                    w, f = w + size, f + size
                    if g == 0 and after_first is not None:
                        after_first(n0)
                    last = g == len(GROUPS) - 1
                    if last:
                        zero_sum(RES[next_norm])
                    with dve.Fori(0, 3, 2) as i:
                        for j in range(2):
                            out_tiles(sub, b, w, j, nt, i)
                            if phase < mods:
                                mod_dot(2 * j, i * 8 + 16 * (n0 // 4 + 1), i * 2 + (n0 + 2 * j))
                            if last:
                                add_square(RES[next_norm], j, 0, nt, i)
                                add_square(RES[next_norm], j, 1, nt, i)
                            if phase < mods:
                                mod_dot(2 * j + 1, i * 8 + 16 * (n0 // 4 + 1), i * 2 + (n0 + 2 * j + 1))
                        if phase < mods:
                            mod_store(i * 2 + n0, i * 2 + (n0 + 4))
                    if phase < mods:
                        n0 += 8
                    phase += 1
                    w, b = w + 4, b + 4
                return n0

            def rotate(src, dst):
                sw, t1, t2 = sq[:, 0, 0:LAT], sq[:, 0, LAT:TOK], sq[:, 1, 0:LAT]
                dve.stream_shuffle(sw, src, [(i + 16) % 32 for i in range(32)])
                link(dve.tensor_tensor(t1, src, cos, ALU.mult))
                link(dve.tensor_tensor(t2, sw, sin, ALU.mult))
                return dve.tensor_tensor(dst, t1, t2, ALU.add)

            def pieces(j, piece):
                src, hi, lo, runs, (s, value) = piece
                dve.wait_ge(s, value)
                if runs:
                    r = ROPE_INDEX[j]
                    if len(runs) == 1:
                        dve.wait_ge(rope_ctx, CTX_INDEX[j] + 1)
                    for n, (c0, c1) in enumerate(runs):
                        ins = rotate(src[:, c0:c1], full[:, r % 2, c0:c1])
                        if n == len(runs) - 1:
                            ins.then_inc(rope_full, 1)
                        else:
                            link(ins)
                    whole = full[:, r % 2]
                else:
                    whole = src[:]
                dve.wait_ge(piece_hi, j + 1)
                dve.tensor_tensor(lo, whole, hi.bitcast(F32), ALU.subtract).then_inc(piece_lo, 1)

            def conv_taps(first, last):
                for step in range(first, min(last, 2 * TAPS)):
                    pair, tap = divmod(step, TAPS)
                    for t in range(2):
                        c = 2 * pair + t
                        x = ypad[:, c, :, tap:tap + LAT]
                        acc = conv[:, c].rearrange("p (v n) -> p v n", v=2)
                        col = vec[:, V_WDW + c * TAPS + tap:V_WDW + c * TAPS + tap + 1]
                        n = 2 * step + t
                        if tap == 0:
                            ins = dve.tensor_scalar(acc, x, col, vec[:, V_BDW + c:V_BDW + c + 1],
                                                    ALU.mult, ALU.add)
                        else:
                            dve.wait_ge(conv_op, n - 1)
                            ins = dve.scalar_tensor_tensor(out=acc, in0=x, scalar=col, in1=acc,
                                                           op0=ALU.mult, op1=ALU.add)
                        ins.then_inc(conv_op, 1)

            def attention(units, u0, sink, factor, pt_hi_buf, pt_lo_buf, n_keys, o_slice, dv, beside=None):
                for i in range(len(units) + 3):
                    if i < len(units):
                        h, qt = units[i]
                        nk = n_keys(qt)
                        dve.wait_ge(scores_done, u0 + i + 1)
                        link(dve.tensor_reduce(smax[:, i:i + 1], ps[S_BANK[i % 3]][:, TOK - nk:TOK], AX.X, ALU.max))
                        if sink:
                            ins = dve.tensor_scalar(nmax[:, i:i + 1], smax[:, i:i + 1], -factor, nsink[:, h:h + 1],
                                                    ALU.mult, ALU.min)
                        else:
                            ins = dve.tensor_scalar(nmax[:, i:i + 1], smax[:, i:i + 1], -factor, None, ALU.mult)
                        ins.then_inc(nmax_ready, 1)
                    if beside is not None and i < len(units):
                        beside(i)
                    if 2 <= i < len(units) + 2:
                        e = i - 2
                        nk = n_keys(units[e][1])
                        dve.wait_ge(pt_hi, u0 + e + 1)
                        dve.tensor_tensor(pt_lo_buf[:, e % 2, TOK - nk:TOK], ps[PT_BANK[e % 2]][:, TOK - nk:TOK],
                                          pt_hi_buf[:, e % 2, TOK - nk:TOK].bitcast(F32),
                                          ALU.subtract).then_inc(pt_lo, 1)
                    if i >= 3:
                        e = i - 3
                        h, qt = units[e]
                        total = den[:, e:e + 1]
                        dve.wait_ge(exp_done, u0 + e + 1)
                        if sink:
                            dve.wait_ge(sink_done, u0 + e + 1)
                            link(dve.tensor_tensor(den[:, e:e + 1], den[:, e:e + 1], esink[:, e:e + 1], ALU.add))
                        link(dve.reciprocal(rinv[:, e:e + 1], total))
                        dve.wait_ge(pv_done, u0 + e + 1)
                        dve.tensor_scalar(o_slice(h, qt), ps[O_BANK[e % 2]][:, 0:dv], rinv[:, e:e + 1], None,
                                          ALU.mult).then_inc(o_done, 1)

            def turned(tiles, base, nt):
                for c in range(tiles):
                    dve.wait_ge(ot_hi, base + c + 1)
                    dve.tensor_tensor(a_lo[:, c, 0:nt], ps[PT_BANK[c % 2]][:, 0:nt],
                                      a_hi[:, c, 0:nt].bitcast(F32), ALU.subtract).then_inc(ot_lo, 1)

            def mixer_out(s, w, b, nt, next_norm):
                zero_sum(RES[next_norm])
                for j in range(4):
                    out_tiles(s, b, w, j, nt)
                    add_square(RES[next_norm], j, 0, nt)
                    add_square(RES[next_norm], j, 1, nt)

            dve.memset(rt[:], 0.0).then_inc(out_free[0], 2)
            dve.memset(mtmp[:], 0.0).then_inc(out_free[1], 2)
            dve.memset(rinv[:], 0.0).then_inc(pair_free, 2)
            dve.memset(unread[:], 0.0).then_inc(mod_first, 1)
            dve.wait_ge(cond_ready, 1)
            with dve.Fori(0, MOD_FIRST - 3, 4) as n:
                for j in range(4):
                    mod_dot(j, n * 4 + 16, n + j)
                mod_store(n, n + 4)
            dve.wait_ge(in_small, 32)
            dve.wait_ge(mod_cols, MOD_FIRST)
            finalize(0, 0, ("shift", "scale"))
            link(dve.tensor_scalar(nsink[:], vec[:, V_SINK:V_SINK + HEADS], -1.0, None, ALU.mult))
            zero_sum(0)
            for sl in range(4):
                add_square(0, sl, 0, TOK)
                add_square(0, sl, 1, TOK)

            def first_gate(n):
                dve.wait_ge(mod_cols, n)
                finalize(0, 0, ("gate",))
            n0 = ffn(0, "ffn0", TOK, "ab", 6, MOD_FIRST, first_gate)
            dve.wait_ge(mod_cols, n0)
            finalize(0, 1)
            finalize(0, 2)

            residual_norm("ab", TOK)
            dve.wait_ge(gp_const, 2)
            for c in range(CT):
                dve.wait_ge(glu_sig, c + 1)
                dve.tensor_tensor(ypad[:, c, :, PAD:PAD + LAT], ps[2 * (c % 2)][:].rearrange("p (v n) -> p v n", v=2),
                                  sil[:, c % 2].rearrange("p (v n) -> p v n", v=2), ALU.mult).then_inc(glu_done, 1)
                if c in (1, 3):
                    dve.wait_ge(glu_done, c + 1)
                if c >= 1:
                    conv_taps(8 * (c - 1), 8 * c)
            for j in range(N_AB):
                pieces(j, AB_PIECES[j])
                if j in (1, 3):
                    conv_taps(24 + 2 * (j - 1), 28 + 2 * (j - 1))
            attention(AB_UNITS, 0, True, A_DIM ** -0.5, h_hi[:, 6:8], h_lo[:, 6:8],
                      lambda qt: TOK if qt < 2 else CTX,
                      lambda h, qt: o_tok[:, qt * 512 + h * A_DIM:qt * 512 + (h + 1) * A_DIM], A_DIM,
                      lambda i: conv_taps(32 + i, 33 + i))
            dve.wait_ge(conv_op, 4 * TAPS)
            link(dve.tensor_tensor(ss[:, 0], conv[:, 0], conv[:, 1], ALU.add))
            link(dve.tensor_tensor(ss[:, 1], conv[:, 2], conv[:, 3], ALU.add))
            dve.tensor_tensor(ss[:, 0], ss[:, 0], ss[:, 1], ALU.add).then_inc(ln_sum, 1)
            turned(4, 0, TOK)
            dve.wait_ge(ln_mean, 1)
            for c in range(CT):
                dve.scalar_tensor_tensor(out=conv[:, c], in0=ps[LN_BANK][:], scalar=-1.0 / B_CH, in1=conv[:, c],
                                         op0=ALU.mult, op1=ALU.add).then_inc(ln_cent, 1)
            dve.wait_ge(stat_sq, 2)
            dve.tensor_tensor(ss[:, 0], sq[:, 0], sq[:, 1], ALU.add).then_inc(stat_add, 1)
            dve.wait_ge(stat_sq, 4)
            link(dve.tensor_tensor(ss[:, 1], sq[:, 0], sq[:, 1], ALU.add))
            dve.wait_ge(stat_add, 1)
            dve.tensor_tensor(ss[:, 0], ss[:, 0], ss[:, 1], ALU.add).then_inc(stat_add, 1)
            rsqrt("ln", LN_BANK, TOK, 1.0 / B_CH, LN_EPS)
            norm_apply("ln", LN_BANK, CT, TOK, lambda k: conv[:, k], lambda k: a_hi[:, 4 + k], lambda k: a_lo[:, 4 + k])
            mixer_out(1, W_AB + 7, B_AB, TOK, "ffn1")

            n0 = ffn(1, "ffn1", TOK, "ffn2", 5, n0)
            assert n0 == 2 * MODT
            dve.wait_ge(mod_cols, n0)
            for place in range(3):
                finalize(1, place)
            ffn(2, "ffn2", TOK, "mla")

            residual_norm("mla", TOK)
            for i, nt in ((0, LAT), (1, TOK)):
                dve.wait_ge(stat_sq, CT + 2 * i + 2)
                dve.tensor_tensor(ss[:, i, 0:nt], sq[:, 0, 0:nt], sq[:, 1, 0:nt], ALU.add).then_inc(stat_ready, 1)
            rsqrt("cq", NORM_BANK, LAT, 1.0 / LORA, NORM_EPS)
            dve.wait_ge(lat_copy, 2)
            norm_apply("cq", NORM_BANK, 2, LAT, lambda k: o_tok[:, k * LAT:(k + 1) * LAT],
                       lambda k: l_hi[:, 0, k * LAT:(k + 1) * LAT], lambda k: l_lo[:, 0, k * LAT:(k + 1) * LAT])
            rsqrt("ckv", NORM_BANK + 1, TOK, 1.0 / LORA, NORM_EPS)
            dve.wait_ge(lat_copy, 4)
            norm_apply("ckv", NORM_BANK + 1, 2, TOK, lambda k: o_tok[:, (1 + k) * TOK:(2 + k) * TOK],
                       lambda k: l_hi[:, 1 + k], lambda k: l_lo[:, 1 + k])
            for j in range(len(MLA_PIECES)):
                pieces(N_AB + j, MLA_PIECES[j])
            attention(MLA_UNITS, len(AB_UNITS), False, (NOPE + ROPE) ** -0.5, l_hi[:, 0:2], l_lo[:, 0:2],
                      lambda qt: TOK, lambda h, qt: o_tok[:, qt * 1024 + h * C_V:qt * 1024 + (h + 1) * C_V], C_V)
            turned(DT, 4, LAT)
            mixer_out(4, W_MLA + 6, B_MLA, LAT, "ffn3")

            ffn(3, "ffn3", LAT, "final")
            rsqrt("final", NORM_BANK, LAT, 1.0 / D, NORM_EPS)
            dve.wait_ge(rstd_bc, CALL["final"] + 1)
            for k in range(DT):
                if k >= 2:
                    dve.wait_ge(y_ready, k - 1)
                dve.tensor_tensor(xn[:, k % 2, 0:LAT], xT[:, k, 0:LAT], ps[NORM_BANK][:, 0:LAT],
                                  ALU.mult).then_inc(xn_ready, 1)

        @block.tensor
        def _(pe):
            def passes(dst, lhs_hi, lhs_lo, rhs_hi, rhs_lo, start, stop):
                pe.matmul(dst, lhs_lo, rhs_hi, start=start, stop=False, skip_group_check=True)
                pe.matmul(dst, lhs_hi, rhs_lo, start=False, stop=False, skip_group_check=True)
                return pe.matmul(dst, lhs_hi, rhs_hi, start=False, stop=stop, skip_group_check=True)

            def weights(slot, c0, n=P):
                return w_hi[:, slot, c0:c0 + n], w_lo[:, slot, c0:c0 + n]

            def two_tiles(slot, banks, nt, name=None):
                for k in range(DT):
                    if name is not None:
                        pe.wait_ge(normed, NORM_BASE[name] + k + 1)
                    for t in range(2):
                        last = passes(ps[banks[t]][:, 0:nt], *weights(slot, t * HALF + k * P),
                                      a_hi[:, k, 0:nt], a_lo[:, k, 0:nt], k == 0, k == DT - 1)
                return last

            def token_sum(name, bank, sums, nt):
                for c in range(nt // P):
                    last = pe.matmul(ps[bank][:, c:c + 1], sums[:, c * P:(c + 1) * P], ones[:, 0:1],
                                     start=True, stop=True)
                last.then_inc(colsum, 1)
                pe.wait_ge(diag_ready, CALL[name] + 1)
                pe.matmul(ps[bank][:, 0:nt], ones[:], diag[:].rearrange("p a n -> p (a n)")[:, 0:nt],
                          start=True, stop=True).then_inc(rstd_bc, 1)

            def residual_norm(name, nt):
                n = RES[name]
                pe.wait_ge(ss_sum[1], 5 * n + 5)
                token_sum(name, NORM_BANK, ss[:, 0], nt)

            def out_slab(b, slot, j, kt, hi, lo, nt, w, i=None, waits=None):
                k0 = (lambda x: x) if i is None else (lambda x: i + x)
                pe.wait_ge(lo_ready, k0(w + j + 1))
                for t in range(2):
                    pe.wait_ge(out_free[t], k0(b + j + 1))
                    for k in range(kt):
                        if waits is not None and t == 0:
                            waits(k)
                        last = passes(ps[OUTB + 2 * ((b + j) % 2) + t][:, 0:nt],
                                      *weights(slot, (t * kt + k) * P), hi[:, k, 0:nt], lo[:, k, 0:nt],
                                      k == 0, k == kt - 1)
                    last.then_inc(slab_done if t else tile0_done, 1)

            def ffn(s, name, nt):
                residual_norm(name, nt)
                w, f, b = FFN_W[s], s * FFN_STEPS, B_FFN[s]
                for g, size in enumerate(GROUPS):
                    with pe.Fori(0, size - 1, 2) as i:
                        for j in range(2):
                            pe.wait_ge(lo_ready, i + (w + j + 1))
                            pe.wait_ge(pair_free, i + (f + j + 1))
                            p = (f + j) % 2
                            two_tiles((w + j) % 2, (2 * p, 2 * p + 1), nt,
                                      name if g == 0 and j == 0 else None).then_inc(slab_done, 1)
                    w, f = w + size, f + size

                    def hidden(k, f=f, size=size):
                        if k >= size - 2:
                            pe.wait_ge(hid_ready, f - size + k + 1)
                    with pe.Fori(0, 3, 2) as i:
                        for j in range(2):
                            out_slab(b, (w + j) % 2, j, size, h_hi, h_lo, nt, w, i, hidden if j == 0 else None)
                    w, b = w + 4, b + 4

            def attention(units, u0, chunks, mask, v, pt_buf, n_keys, dv):
                for i in range(len(units) + 3):
                    if i < len(units):
                        h, qt = units[i]
                        nk = n_keys(qt)
                        bank = ps[S_BANK[i % 3]]
                        if i >= 3:
                            pe.wait_ge(exp_done, u0 + i - 2)
                        parts = chunks(h, qt, TOK - nk)
                        for n, part in enumerate(parts):
                            last = passes(bank[:, TOK - nk:TOK], *part, n == 0, n == len(parts) - 1)
                        if mask and qt < 2:
                            c0 = P * (1 - qt)
                            last = pe.matmul(bank[:, c0:c0 + P], ident_r[:], mask_r[:, qt],
                                             start=False, stop=True, skip_group_check=True)
                        last.then_inc(scores_done, 1)
                    if 2 <= i < len(units) + 2:
                        e = i - 2
                        pe.wait_ge(exp_done, u0 + e + 1)
                        if e >= 2:
                            pe.wait_ge(pt_lo, u0 + e - 1)
                        for kt in range((TOK - n_keys(units[e][1])) // P, 4):
                            last = pe.transpose(ps[PT_BANK[e % 2]][:, kt * P:(kt + 1) * P],
                                                probs[:, e % 3, kt * P:(kt + 1) * P], ident)
                        last.then_inc(pt_done, 1)
                    if i >= 3:
                        e = i - 3
                        h, qt = units[e]
                        pe.wait_ge(pt_lo, u0 + e + 1)
                        if e >= 2:
                            pe.wait_ge(o_done, u0 + e - 1)
                        k0 = (TOK - n_keys(qt)) // P
                        for kt in range(k0, 4):
                            last = passes(ps[O_BANK[e % 2]][:, 0:dv], *[x[:, e % 2, kt * P:(kt + 1) * P] for x in pt_buf],
                                          *v(h, kt), kt == k0, kt == 3)
                        last.then_inc(pv_done, 1)

            def turn(tiles, base, qts, stride):
                for c in range(tiles):
                    if c >= 2:
                        pe.wait_ge(ot_lo, base + c - 1)
                    for qt in range(qts):
                        last = pe.transpose(ps[PT_BANK[c % 2]][:, qt * P:(qt + 1) * P],
                                            o_tok[:, qt * stride + c * P:qt * stride + (c + 1) * P], ident)
                    last.then_inc(ot_done, 1)

            pe.wait_ge(gp_const, 1)
            pe.wait_ge(act_const, 2)
            ffn(0, "ffn0", TOK)

            residual_norm("ab", TOK)
            w = W_AB
            for c in range(6):
                pe.wait_ge(lo_ready, w + c + 1)
                if 2 <= c < 6:
                    pe.wait_ge(glu_done, c - 1)
                two_tiles((w + c) % 2, (2 * (c % 2), 2 * (c % 2) + 1), TOK,
                          "ab" if c == 0 else None).then_inc(slab_done, 1)
            pe.wait_ge(lo_ready, w + 7)
            pe.wait_ge(piece_lo, 2)
            slot = (w + 6) % 2
            for k in range(DT):
                last = passes(ps[0][:], *weights(slot, k * P), a_hi[:, k], a_lo[:, k], k == 0, k == DT - 1)
            last.then_inc(step_done, 1)
            for kt in range(4):
                for k in range(DT):
                    last = passes(ps[1][:, kt * P:(kt + 1) * P], a_hi[:, k, kt * P:(kt + 1) * P],
                                  a_lo[:, k, kt * P:(kt + 1) * P], *weights(slot, HALF + k * P),
                                  k == 0, k == DT - 1)
            last.then_inc(slab_done, 1)
            pe.wait_ge(piece_lo, N_AB)

            def ab_chunks(h, qt, k0):
                r = slice(A_DIM * (h // 4), A_DIM * (h // 4 + 1))
                q = [x[r, h % 4, qt * P:(qt + 1) * P] for x in (h_hi, h_lo)]
                return [(*q, h_hi[r, 4, k0:TOK], h_lo[r, 4, k0:TOK])]

            def ab_v(h, kt):
                c = kt * P + (h // 4) * A_DIM
                return h_hi[:, 5, c:c + A_DIM], h_lo[:, 5, c:c + A_DIM]
            attention(AB_UNITS, 0, ab_chunks, True, ab_v, (h_hi[:, 6:8], h_lo[:, 6:8]),
                      lambda qt: TOK if qt < 2 else CTX, A_DIM)
            pe.wait_ge(ln_sum, 1)
            pe.matmul(ps[LN_BANK][:], ones[:], ss[:, 0], start=True, stop=True).then_inc(ln_mean, 1)
            pe.wait_ge(o_done, len(AB_UNITS))
            turn(4, 0, 4, 512)
            pe.wait_ge(stat_add, 2)
            token_sum("ln", LN_BANK, ss[:, 0], TOK)

            def mixer_out(b, w, nt, inputs):
                for j in range(4):
                    out_slab(b, (w + j) % 2, j, DT, a_hi, a_lo, nt, w, None, inputs if j == 0 else None)

            def ab_inputs(k):
                if k < 4:
                    pe.wait_ge(ot_lo, k + 1)
                else:
                    pe.wait_ge(normed, NORM_BASE["ln"] + k - 3)
            mixer_out(B_AB, W_AB + 7, TOK, ab_inputs)
            ffn(1, "ffn1", TOK)
            ffn(2, "ffn2", TOK)

            residual_norm("mla", TOK)
            w = W_MLA
            pe.wait_ge(lo_ready, w + 1)
            two_tiles(w % 2, (0, 1), LAT, "mla").then_inc(slab_done, 1)
            pe.wait_ge(lo_ready, w + 2)
            two_tiles((w + 1) % 2, (2, 3), TOK).then_inc(slab_done, 1)
            pe.wait_ge(lo_ready, w + 3)
            pe.wait_ge(stat_ready, 1)
            pe.wait_ge(lat_copy, 2)
            slot = (w + 2) % 2
            for k in range(DT):
                last = passes(ps[0][:], *weights(slot, k * P), a_hi[:, k], a_lo[:, k], k == 0, k == DT - 1)
            last.then_inc(step_done, 1)
            token_sum("cq", NORM_BANK, ss[:, 0], LAT)
            pe.wait_ge(stat_ready, 2)
            token_sum("ckv", NORM_BANK + 1, ss[:, 1], TOK)
            pe.wait_ge(normed, NORM_BASE["cq"] + 2)
            pe.wait_ge(lat_copy, 4)

            def queries(i, slot, c0):
                for t in range(4):
                    for k in range(2):
                        c = k * LAT
                        last = passes(ps[2 * (i % 2) + t // 2][:, (t % 2) * LAT:(t % 2 + 1) * LAT],
                                      *weights(slot, c0 + (2 * t + k) * P), l_hi[:, 0, c:c + LAT],
                                      l_lo[:, 0, c:c + LAT], k == 0, k == 1)
                return last

            def step(i, emit):
                if i >= 2:
                    pe.wait_ge(piece_lo, MLA_PIECES_BY[i - 2])
                emit().then_inc(MLA_SIGNAL[i][0], 1)

            step(1, lambda: queries(1, slot, HALF))
            pe.wait_ge(lo_ready, w + 4)
            step(2, lambda: queries(2, (w + 3) % 2, 0))
            step(3, lambda: queries(3, (w + 3) % 2, HALF))
            pe.wait_ge(normed, NORM_BASE["ckv"] + 2)
            pe.wait_ge(lo_ready, w + 5)

            def nope_keys(i):
                def emit():
                    for t in range(2):
                        m = 2 * (i - 4) + t
                        for k in range(2):
                            last = passes(ps[2 * (i % 2) + t][:], *weights((w + 4) % 2, (2 * m + k) * P),
                                          l_hi[:, 1 + k], l_lo[:, 1 + k], k == 0, k == 1)
                    return last
                return emit

            def values(i):
                def emit():
                    kt = i - 8
                    for t in range(2):
                        for k in range(2):
                            last = passes(ps[2 * (i % 2) + t][:], l_hi[:, 1 + k, kt * P:(kt + 1) * P],
                                          l_lo[:, 1 + k, kt * P:(kt + 1) * P],
                                          *weights((w + 5) % 2, k * D + t * 512, 512), k == 0, k == 1)
                    return last
                return emit
            for i in range(4, 8):
                step(i, nope_keys(i))
            pe.wait_ge(lo_ready, w + 6)
            for i in range(8, 12):
                step(i, values(i))
            pe.wait_ge(piece_lo, N_AB + len(MLA_PIECES))

            def mla_chunks(h, qt, k0):
                n, c = h // 2, (h % 2) * LAT + qt * P
                r = slice(ROPE * (h % 2), ROPE * (h % 2 + 1))
                tile = h // 2
                rn, rc = 4 + tile // 2, (tile % 2) * LAT + qt * P
                return [(q_hi[:, n, c:c + P], q_lo[:, n, c:c + P], a_hi[:, h], a_lo[:, h]),
                        (q_hi[r, rn, rc:rc + P], q_lo[r, rn, rc:rc + P], q_hi[r, 6], q_lo[r, 6])]

            def mla_v(h, kt):
                n, c = 2 * kt + h // 4, (h % 4) * C_V
                return h_hi[:, n, c:c + C_V], h_lo[:, n, c:c + C_V]
            attention(MLA_UNITS, len(AB_UNITS), mla_chunks, False, mla_v, (l_hi[:, 0:2], l_lo[:, 0:2]),
                      lambda qt: TOK, C_V)
            pe.wait_ge(o_done, len(AB_UNITS) + len(MLA_UNITS))
            turn(DT, 4, 2, 1024)
            mixer_out(B_MLA, W_MLA + 6, LAT, lambda k: pe.wait_ge(ot_lo, 4 + k + 1))
            ffn(3, "ffn3", LAT)
            residual_norm("final", LAT)


def _tiles(w, rows, width):
    k, m = w.shape
    return w.reshape(rows, P, m // width, width).transpose(2, 1, 0, 3)


def _ffn_slabs(w_in, w_out):
    n = D_FF // P
    gate_up = _tiles(w_in, DT, P).reshape(2, n, P, HALF)
    w_out = _tiles(w_out, n, P)
    slabs, at = [], 0
    for size in GROUPS:
        slabs.append(gate_up[:, at:at + size].transpose(1, 2, 0, 3).reshape(size, P, SLAB))
        part = w_out[:, :, at:at + size].reshape(4, 2, P, size * P).transpose(0, 2, 1, 3).reshape(4, P, 2 * size * P)
        if part.shape[2] < SLAB:
            part = np.concatenate([part, np.zeros((4, P, SLAB - part.shape[2]), part.dtype)], axis=2)
        slabs.append(part)
        at += size
    return slabs


def _pairs(w, rows):
    t = _tiles(w, rows, P)
    return t.reshape(t.shape[0] // 2, 2, P, rows * P).transpose(0, 2, 1, 3).reshape(-1, P, 2 * rows * P)


def _stream(ffn_w_in, ffn_w_out, ab_w_in, ab_w_out, c_w_dq, c_w_uq, c_w_dkv, c_w_uk, c_w_uv, c_w_o):
    aq, akv = HEADS * A_DIM, A_KV * A_DIM
    wq = ab_w_in[:, :aq].reshape(D, 2, 4, A_DIM).transpose(0, 2, 1, 3).reshape(D, aq)
    wa, wg = ab_w_in[:, aq + 2 * akv:aq + 2 * akv + B_CH], ab_w_in[:, aq + 2 * akv + B_CH:]
    wconv = np.concatenate([wa.reshape(D, CT, 1, P), wg.reshape(D, CT, 1, P)], axis=2).reshape(D, 2 * B_CH)
    wab = np.concatenate([wconv, wq, ab_w_in[:, aq:aq + 2 * akv]], axis=1)
    uq = c_w_uq.reshape(LORA, HEADS, NOPE + ROPE)
    uq = np.concatenate([uq[:, :, :NOPE].reshape(LORA, -1), uq[:, :, NOPE:].reshape(LORA, -1)], axis=1)
    uq = _tiles(uq, 2, P).transpose(1, 0, 2, 3).reshape(P, 3 * HALF)
    kr = np.concatenate([c_w_dkv[:, LORA:], c_w_dkv[:, LORA:]], axis=1)
    kr = _tiles(kr, DT, P).reshape(P, HALF)
    mla = [_pairs(c_w_dq, DT), _pairs(c_w_dkv[:, :LORA], DT),
           np.concatenate([kr, uq[:, :HALF]], axis=1)[None], uq[:, HALF:][None],
           _tiles(c_w_uk, 2, P).transpose(1, 0, 2, 3).reshape(1, P, SLAB),
           c_w_uv.reshape(2, P, D).transpose(1, 0, 2).reshape(1, P, SLAB),
           _pairs(c_w_o, DT)]
    slabs = (_ffn_slabs(ffn_w_in[0, 0], ffn_w_out[0, 0]) + [_pairs(wab, DT), _pairs(ab_w_out, DT)]
             + _ffn_slabs(ffn_w_in[0, 1], ffn_w_out[0, 1]) + _ffn_slabs(ffn_w_in[1, 0], ffn_w_out[1, 0])
             + mla + _ffn_slabs(ffn_w_in[1, 1], ffn_w_out[1, 1]))
    return np.concatenate(slabs, axis=0)


def _columns(a):
    return a.reshape(-1, P).T


def _constants():
    q, k = np.arange(P)[:, None], np.arange(P)[None, :]
    mask0 = np.where(k <= q, 0.0, NEG)
    mask1 = np.where(q <= k, 0.0, NEG)
    t = np.arange(LAT)
    half = ROPE // 2
    inv = (np.float32(10000.0) ** (-np.arange(0, half, 2, dtype=np.float32) / np.float32(half))).astype(np.float32)
    row = (t // GRID_W).astype(np.float32)[:, None] * inv
    col = (t % GRID_W).astype(np.float32)[:, None] * inv
    ang = np.concatenate([row, row, col, col], axis=1).astype(np.float32)
    sign = np.tile(np.concatenate([-np.ones(half // 2), np.ones(half // 2)]), 2)
    cos, sin = np.cos(ang).T, (np.sin(ang) * sign).T
    c = np.concatenate([np.eye(P), mask0, mask1, np.tile(cos, (2, 1)), np.tile(sin, (2, 1))], axis=1)
    return np.ascontiguousarray(c, dtype=np.float32)


def kernel(x, c, ctx, c_ctx, w_mod, b_mod, g_norm, ffn_w_in, ffn_w_out, ab_w_in, a_sink, b_w_dw, b_b_dw,
           b_ln_g, b_ln_b, ab_w_out, c_w_dq, c_g_q, c_w_uq, c_w_dkv, c_g_kv, c_w_uk, c_w_uv, c_w_o, g_final):
    import concourse.bacc as bacc
    from concourse.bass_utils import run_bass_kernel_spmd

    (x, c, ctx, c_ctx, w_mod, b_mod, g_norm, ffn_w_in, ffn_w_out, ab_w_in, a_sink, b_w_dw, b_b_dw, b_ln_g, b_ln_b,
     ab_w_out, c_w_dq, c_g_q, c_w_uq, c_w_dkv, c_g_kv, c_w_uk, c_w_uv, c_w_o, g_final) = (
        np.asarray(a) for a in (x, c, ctx, c_ctx, w_mod, b_mod, g_norm, ffn_w_in, ffn_w_out, ab_w_in, a_sink, b_w_dw,
                                b_b_dw, b_ln_g, b_ln_b, ab_w_out, c_w_dq, c_g_q, c_w_uq, c_w_dkv, c_g_kv, c_w_uk,
                                c_w_uv, c_w_o, g_final))
    tokens = np.concatenate([x[0], ctx[0]], axis=0).T.reshape(DT, P, TOK).transpose(1, 0, 2)
    taps = b_w_dw[0].reshape(TAPS, CT, P).transpose(2, 1, 0).reshape(P, CT * TAPS)
    vecs = np.concatenate([_columns(g_norm), _columns(b_mod), _columns(g_final), _columns(b_b_dw), _columns(b_ln_g),
                           _columns(b_ln_b), _columns(c_g_q), _columns(c_g_kv),
                           np.broadcast_to(a_sink, (P, HEADS)), taps], axis=1)
    arrays = {
        "tokens": tokens,
        "cond": np.stack([c[0], c_ctx]),
        "vecs": vecs,
        "consts": _constants(),
        "wmod": w_mod.transpose(0, 2, 1).reshape(2 * MODT, P, D),
        "wstream": _stream(ffn_w_in, ffn_w_out, ab_w_in[0], ab_w_out[0], c_w_dq[0], c_w_uq[0], c_w_dkv[0], c_w_uk[0],
                           c_w_uv[0], c_w_o[0]),
    }
    arrays = {k: np.ascontiguousarray(a) for k, a in arrays.items()}
    nc = bacc.Bacc("TRN2", target_bir_lowering=False, num_devices=1)
    args = [nc.dram_tensor(k, a.shape, mybir.dt.from_np(a.dtype), kind="ExternalInput").ap()
            for k, a in arrays.items()]
    out = nc.dram_tensor("out", [P, DT, LAT], mybir.dt.float32, kind="ExternalOutput").ap()
    build(nc, *args, out)
    result = run_bass_kernel_spmd(nc, [arrays], core_ids=[0]).results[0]["out"]
    return np.ascontiguousarray(result.transpose(2, 1, 0).reshape(LAT, D))[None]
```

```python
from contextlib import ExitStack

import numpy as np

import concourse.bass as bass
from concourse import mybir

P = 128
D = 1024
DT = D // P
LAT, CTX = 256, 256
TOK = LAT + CTX
D_FF = 2816
GROUPS = (8, 8, 6)
SLAB = 2048
HALF = SLAB // 2
HEADS = 8
A_DIM, A_KV, B_CH, TAPS = 64, 2, 512, 31
CT = B_CH // P
PAD = TAPS // 2
NOPE, ROPE, C_V, LORA = 128, 64, 128, 256
N_MOD = 9
MODT = N_MOD * DT
GRID_W = 64
NORM_EPS, LN_EPS = 1e-6, 1e-5
NEG = -1e30

FFN_SLABS = sum(g + 4 for g in GROUPS)
W_FFN0 = 0
W_AB = W_FFN0 + FFN_SLABS
W_FFN1 = W_AB + 7 + 4
W_FFN2 = W_FFN1 + FFN_SLABS
W_MLA = W_FFN2 + FFN_SLABS
W_FFN3 = W_MLA + 6 + 4
N_SLABS = W_FFN3 + FFN_SLABS
FFN_W = (W_FFN0, W_FFN1, W_FFN2, W_FFN3)
FFN_STEPS = sum(GROUPS)
FFN_OUTS = 4 * len(GROUPS)
B_FFN = (0, FFN_OUTS + 4, 2 * FFN_OUTS + 4, 3 * FFN_OUTS + 8)
B_AB = FFN_OUTS
B_MLA = 3 * FFN_OUTS + 4

MOD_FIRST = 2 * DT

NORMS = ("ffn0", "ab", "ln", "ffn1", "ffn2", "mla", "cq", "ckv", "ffn3", "final")
NORM_TILES = {"ln": 4, "cq": 2, "ckv": 2}
CALL = {n: i for i, n in enumerate(NORMS)}
NORM_BASE = {}
_n = 0
for _name in NORMS:
    NORM_BASE[_name] = _n
    _n += NORM_TILES.get(_name, DT)
RES = {"ffn0": 0, "ab": 1, "ffn1": 2, "ffn2": 3, "mla": 4, "ffn3": 5, "final": 6}

V_G, V_BMOD, V_GF = 0, 48, 48 + 2 * MODT
V_BDW = V_GF + DT
V_LNG = V_BDW + CT
V_LNB = V_LNG + CT
V_GQ = V_LNB + CT
V_GKV = V_GQ + 2
V_SINK = V_GKV + 2
V_WDW = V_SINK + HEADS
N_VEC = V_WDW + CT * TAPS
C_ID, C_MASK, C_COS, C_SIN = 0, P, 3 * P, 3 * P + LAT
N_CONST = C_SIN + LAT


def build(nc, tokens, cond, vecs, consts, wmod, wstream, out):
    F32, F32R, I32 = mybir.dt.float32, mybir.dt.float32r, mybir.dt.int32
    ALU, ACT, AX = mybir.AluOpType, mybir.ActivationFunctionType, mybir.AxisListType
    ds = bass.ds

    with ExitStack() as ctx:
        def sb(name, shape, dt=F32, where=ctx):
            return where.enter_context(nc.sbuf_tensor(name, shape, dt))

        def sem(name):
            return ctx.enter_context(nc.semaphore(name))

        xT = sb("xT", [P, DT, TOK])
        a_hi = sb("a_hi", [P, DT, TOK], F32R)
        a_lo = sb("a_lo", [P, DT, TOK], F32R)
        h_hi = sb("h_hi", [P, 8, TOK], F32R)
        h_lo = sb("h_lo", [P, 8, TOK], F32R)
        raw = sb("raw", [P, 2, SLAB])
        w_hi = sb("w_hi", [P, 2, SLAB], F32R)
        w_lo = sb("w_lo", [P, 2, SLAB], F32R)
        spare = sb("spare", [P, 2048])
        work = sb("work", [P, 4, TOK])
        with ExitStack() as norms:
            sq = sb("sq", [P, 2, TOK], where=norms)
            ss = sb("ss", [P, 2, TOK], where=norms)
        pt_hi1 = sb("pt_hi1", [P, 2, TOK], F32R)
        pt_lo1 = sb("pt_lo1", [P, 2, TOK], F32R)
        diag = sb("diag", [P, 4, P])
        rdiag = sb("rdiag", [P, 2, 2, P])
        ones = sb("ones", [P, P])
        cst = sb("cst", [P, N_CONST])
        ident_r = sb("ident_r", [P, P], F32R)
        mask_r = sb("mask_r", [P, 2, P], F32R)
        vec = sb("vec", [P, N_VEC])
        modc = sb("modc", [P, 2, 2 * MODT])
        stage = sb("stage", [P, 2, 4])
        shift = sb("shift", [P, 6, 2, DT])
        scale = sb("scale", [P, 6, 2, DT])
        gate = sb("gate", [P, 6, 2, DT])
        mtmp = sb("mtmp", [P, 2, DT])
        nsink = sb("nsink", [P, HEADS])
        smax = sb("smax", [P, 32])
        nmax = sb("nmax", [P, 32])
        den = sb("den", [P, 32])
        esink = sb("esink", [P, 32])
        rinv = sb("rinv", [P, 32])
        rv = sb("rv", [P, 4])
        ri = sb("ri", [P, 4], I32)
        ry = sb("ry", [P, 4])
        rt = sb("rt", [P, 4])
        tick = sb("tick", [P, N_SLABS - W_FFN3])
        with ExitStack() as first:
            mring = sb("mring", [P, 4, D], where=first)
            cb = sb("cb", [P, 2, D], where=first)
            unread = sb("unread", [P, D], mybir.dt.bfloat16, where=first)
            ypad = sb("ypad", [P, CT, 2, LAT + 2 * PAD], where=first)
        q_hi = sb("q_hi", [P, 7, TOK], F32R)
        q_lo = sb("q_lo", [P, 7, TOK], F32R)
        l_hi = sb("l_hi", [P, 3, TOK], F32R)
        l_lo = sb("l_lo", [P, 3, TOK], F32R)
        conv = spare[:].rearrange("p (c n) -> p c n", c=CT)
        ident = cst[:, C_ID:C_ID + P]
        cos, sin = cst[:, C_COS:C_COS + LAT], cst[:, C_SIN:C_SIN + LAT]
        xn, full = work[:, 0:2], work[:, 2:4]
        sil, prod = work[:, 0:2], work[:, 2:4]
        probs = work[:, 0:3]
        AB_PT = [(x[:, 4:6], x[:, 6:8]) for x in (a_hi, a_lo)]
        MLA_PT = [(l_hi[:, 0:2], pt_hi1[:]), (l_lo[:, 0:2], pt_lo1[:])]
        ps = [ctx.enter_context(nc.psum_tensor(f"ps{i}", [P, 512], F32)) for i in range(8)]
        OUTB = 4
        S_BANK, PT_BANK, O_BANK, LN_BANK, NORM_BANK = (1, 4, 5), (6, 7), (0, 3), 2, 6

        in_tok = sem("in_tok")
        in_cond = sem("in_cond")
        in_small = sem("in_small")
        raw_loaded = [sem(f"raw_loaded{i}") for i in range(2)]
        hi_ready = sem("hi_ready")
        lo_ready = sem("lo_ready")
        lo2_ready = sem("lo2_ready")
        both_split = sem("both_split")
        slab_done = sem("slab_done")
        mod_loaded = [sem(f"mod_loaded{i}") for i in range(4)]
        mod_first = sem("mod_first")
        mod_dots = sem("mod_dots")
        mod_cols = sem("mod_cols")
        cond_ready = sem("cond_ready")
        gp_const = sem("gp_const")
        act_const = sem("act_const")
        chain = sem("chain")
        sq_ready = [sem(f"sq_ready{i}") for i in range(2)]
        ss_sum = [sem(f"ss_sum{i}") for i in range(2)]
        colsum = sem("colsum")
        diag_ready = sem("diag_ready")
        rstd_bc = sem("rstd_bc")
        xn_ready = sem("xn_ready")
        nhi_ready = sem("nhi_ready")
        normed = sem("normed")
        pair_free = sem("pair_free")
        sil_ready = sem("sil_ready")
        hhi_ready = sem("hhi_ready")
        hid_ready = sem("hid_ready")
        tile0_done = sem("tile0_done")
        out_free = [sem(f"out_free{i}") for i in range(2)]
        glu_sig = sem("glu_sig")
        glu_done = sem("glu_done")
        conv_op = sem("conv_op")
        tap_first = sem("tap_first")
        tap_prod = sem("tap_prod")
        tap_add = sem("tap_add")
        step_done = sem("step_done")
        rope_ctx = sem("rope_ctx")
        rope_full = sem("rope_full")
        piece_hi = sem("piece_hi")
        piece_lo = sem("piece_lo")
        scores_done = sem("scores_done")
        nmax_ready = sem("nmax_ready")
        exp_done = sem("exp_done")
        sink_done = sem("sink_done")
        pt_done = sem("pt_done")
        pt_hi = sem("pt_hi")
        pt_lo = sem("pt_lo")
        pv_done = sem("pv_done")
        rdiag_ready = sem("rdiag_ready")
        v_copy = sem("v_copy")
        ot_hi = sem("ot_hi")
        ot_lo = sem("ot_lo")
        ln_sum = sem("ln_sum")
        ln_mean = sem("ln_mean")
        ln_cent = sem("ln_cent")
        stat_sq = sem("stat_sq")
        stat_add = sem("stat_add")
        stat_ready = sem("stat_ready")
        lat_copy = sem("lat_copy")
        y_ready = sem("y_ready")
        stored = sem("stored")

        CONV_ADDS = 2 * (TAPS - 1)

        def tap_slot(n):
            return (ss[:, 0], ss[:, 1], diag[:].rearrange("p a n -> p (a n)"))[n % 3]

        def cols(hi, lo, i, a=0, b=TOK):
            return hi[:, i, a:b], lo[:, i, a:b]

        AB_PIECES = []
        for t in range(4):
            AB_PIECES.append((ps[t % 2 + 2 * (t // 2 % 2)], *cols(h_hi, h_lo, t), ((0, LAT),),
                              (slab_done, W_AB + 5 + t // 2)))
        AB_PIECES.append((ps[0], *cols(h_hi, h_lo, 4), ((0, LAT),), (step_done, 1)))
        AB_PIECES.append((ps[2], *cols(h_hi, h_lo, 5), (), (step_done, 2)))
        MLA_STEPS = [[("kr", 0)], [("q", 0), ("q", 1)], [("q", 2), ("q", 3)], [("q", 4), ("q", 5)]]
        MLA_STEPS += [[("kn", 2 * i), ("kn", 2 * i + 1)] for i in range(4)]
        MLA_STEPS += [[("v", 2 * i), ("v", 2 * i + 1)] for i in range(4)]
        MLA_SIGNAL, n_step = [], 2
        for i in range(len(MLA_STEPS)):
            ends = {1: W_MLA + 3, 3: W_MLA + 4, 7: W_MLA + 5, 11: W_MLA + 6}.get(i)
            if ends is None:
                n_step += 1
                MLA_SIGNAL.append((step_done, n_step))
            else:
                MLA_SIGNAL.append((slab_done, ends))
        MLA_PIECES, MLA_PIECES_BY = [], []
        for i, parts in enumerate(MLA_STEPS):
            for t, (kind, n) in enumerate(parts):
                bank = ps[2 * (i % 2) + t]
                if kind == "kr":
                    piece = (bank, *cols(q_hi, q_lo, 6), ((0, LAT),), MLA_SIGNAL[i])
                elif kind == "q":
                    piece = (bank, *cols(q_hi, q_lo, n), ((0, LAT), (LAT, TOK)) if n >= 4 else (), MLA_SIGNAL[i])
                elif kind == "kn":
                    piece = (bank, *cols(a_hi, a_lo, n), (), MLA_SIGNAL[i])
                else:
                    piece = (bank, *cols(h_hi, h_lo, n), (), MLA_SIGNAL[i])
                MLA_PIECES.append(piece)
            MLA_PIECES_BY.append(len(AB_PIECES) + len(MLA_PIECES))
        N_AB = len(AB_PIECES)
        ROPE_INDEX = {}
        CTX_INDEX = {}
        for j, p in enumerate(AB_PIECES + MLA_PIECES):
            if p[3]:
                ROPE_INDEX[j] = len(ROPE_INDEX)
                if len(p[3]) == 1:
                    CTX_INDEX[j] = len(CTX_INDEX)

        def units(order):
            found, at = [], 0
            for h, qts in order:
                found.append((h, qts, at))
                at += len(qts)
            return found

        LATE = HEADS // 2
        AB_UNITS = units([(h, qts) for t in range(LATE) for qts in (((0, 0),), ((1, 0),), ((2, LAT), (3, LAT)))
                          for h in (t, t + LATE)])
        MLA_UNITS = units([(h, ((qt, 0),)) for h in range(HEADS) for qt in range(2)])
        AB_PAIRS = len(AB_UNITS) // 2
        LN_UNIT = 17

        def spans(qts):
            n = TOK // len(qts)
            return [(qt, key0, i * n, n) for i, (qt, key0) in enumerate(qts)]

        def pt_unit(buf, e, qts):
            pair = buf[e // 2 % 2].rearrange("p a n -> p (a n)")
            return pair.rearrange("p (k u n) -> p k u n", u=2, n=len(qts) * P)[:, :, e % 2]

        def pt_bank(e, qts):
            return ps[PT_BANK[e % 2]][:].rearrange("p (k n) -> p k n", n=len(qts) * P)

        def ab_out(buf, p):
            c, which = p // 3, p % 3
            n = P if which < 2 else 2 * P
            return [(slice(A_DIM * u, A_DIM * (u + 1)), slice(u * n, (u + 1) * n),
                     buf[A_DIM * u:A_DIM * (u + 1), c, which * P:which * P + n]) for u in range(2)]

        def mla_out(buf, p):
            return [(slice(0, P), slice(0, LAT), buf[:, p, 0:LAT])]

        block = ctx.enter_context(nc.Block())

        @block.sync
        def _(sp):
            def slab(w, slot, wait=None):
                if wait is not None:
                    sp.wait_ge(lo_ready, wait)
                sp.dma_start(raw[:, slot], wstream[ds(w, 1)].rearrange("a p n -> p (a n)")) \
                  .then_inc(raw_loaded[slot], 16)

            def mod_tile(n, slot, wait=None):
                if wait is not None:
                    sp.wait_ge(mod_dots, wait)
                sp.dma_start(mring[:, slot], wmod[ds(n, 1)].rearrange("a p n -> p (a n)")) \
                  .then_inc(mod_loaded[slot], 16)

            sp.dma_start(cb[:], cond.partition_broadcast(P)).then_inc(in_cond, 16)
            for n in range(4):
                mod_tile(n, n)
            sp.dma_start(vec[:], vecs).then_inc(in_small, 16)
            sp.dma_start(xT[:], tokens).then_inc(in_tok, 16)
            with sp.Fori(0, MOD_FIRST - 7, 4) as n:
                for j in range(4):
                    mod_tile(n + (4 + j), j, n + (j + 1))
            sp.dma_start(cst[:], consts).then_inc(in_small, 16)
            for w in range(2):
                slab(w, w)
            for w in range(2, 4):
                slab(w, w % 2, w - 1)
            for j in range(4):
                mod_tile(MOD_FIRST + j, j, MOD_FIRST + j - 3)

            def both(w0, n0, turns):
                with sp.Fori(0, turns) as i:
                    for j in range(2):
                        for k in range(2):
                            n = i * 4 + (n0 + 2 * j + k)
                            mod_tile(n, 2 * j + k, n - 3)
                        w = i * 2 + (w0 + j)
                        slab(w, (w0 + j) % 2, w - 1)

            both(4, MOD_FIRST + 4, 17)
            for w in range(38, W_FFN1 + 4):
                slab(w, w % 2, w - 1)
            left = 2 * MODT - (MOD_FIRST + 4 + 68)
            both(W_FFN1 + 4, MOD_FIRST + 4 + 68, left // 4)
            w1 = W_FFN1 + 4 + left // 2
            def only(w0, w2, last_ffn=False):
                with sp.Fori(w0, w2 - 1, 2) as w:
                    for j in range(2):
                        if last_ffn:
                            sp.wait_ge(both_split, w + (j - 1 - W_FFN3))
                            slab(w + j, (w0 + j) % 2)
                        else:
                            slab(w + j, (w0 + j) % 2, w + (j - 1))

            assert (w1 - W_FFN3) % 2 == 0
            only(w1, W_FFN3 + 2)
            only(W_FFN3 + 2, N_SLABS, True)
            for k in range(DT):
                sp.wait_ge(y_ready, k + 1)
                sp.dma_start(out[:, k], spare[:, k * LAT:(k + 1) * LAT]).then_inc(stored, 16)
            sp.wait_ge(stored, 16 * DT)

        @block.gpsimd
        def _(pool):
            pool.memset(ones[:], 1.0).then_inc(gp_const, 1)
            pool.memset(ypad[:], 0.0).then_inc(gp_const, 1)

            def split_lo(w, slot, width=SLAB):
                pool.wait_ge(hi_ready, w + 1)
                pool.tensor_tensor(w_lo[:, slot, 0:width], raw[:, slot, 0:width],
                                   w_hi[:, slot, 0:width].bitcast(F32), ALU.subtract).then_inc(lo_ready, 1)

            def add_taps(first, last):
                for n in range(first, last):
                    if n < 2:
                        pool.wait_ge(tap_first, n + 1)
                    pool.wait_ge(tap_prod, n + 1)
                    if n >= 2:
                        pool.wait_ge(tap_add, n - 1)
                    pool.tensor_tensor(conv[:, n % 2], conv[:, n % 2], tap_slot(n), ALU.add).then_inc(tap_add, 1)

            def loop(first, end):
                with pool.Fori(first, end - 1, 2) as w:
                    for j in range(2):
                        split_lo(w + j, (first + j) % 2)

            loop(0, W_AB + 2)
            for c in range(7):
                split_lo(W_AB + 2 + c, (W_AB + c) % 2)
                if c >= 2:
                    add_taps(10 * (c - 2) // 2, 10 * (c - 1) // 2)
            add_taps(25, CONV_ADDS)
            loop(W_AB + 9, W_FFN3)
            with pool.Fori(W_FFN3, N_SLABS - 1, 2) as w:
                for j in range(2):
                    split_lo(w + j, (W_FFN3 + j) % 2, HALF)
                    pool.wait_ge(lo2_ready, w + (j + 1 - W_FFN3))
                    pool.tensor_tensor(tick[:, ds(w + (j - W_FFN3), 1)], ones[:, 0:1], ones[:, 0:1],
                                       ALU.add).then_inc(both_split, 1)

        @block.scalar
        def _(act):
            def split_hi(w, slot, base, i=None):
                value = 16 * (base // 2 + 1)
                act.wait_ge(raw_loaded[slot], value if i is None else i * 16 + value)
                act.activation(w_hi[:, slot], raw[:, slot], ACT.Copy).then_inc(hi_ready, 1)

            def squares(n, sl, t, nt, i=None):
                k = sl if i is None else i + sl
                act.wait_ge(ss_sum[t], k + (5 * n + 1 if t else 4 * n))
                m = 2 * sl + t if i is None else i * 2 + (2 * sl + t)
                src = xT[:, m, 0:nt] if i is None else xT[:, ds(m, 1), 0:nt].rearrange("p a n -> p (a n)")
                act.activation(sq[:, t, 0:nt], src, ACT.Square).then_inc(sq_ready[t], 1)

            def norm_apply(name, tiles, emit):
                base = NORM_BASE[name]
                for k in range(tiles):
                    act.wait_ge(xn_ready, base + k + 1)
                    if k >= 2:
                        act.wait_ge(normed, base + k - 1)
                    emit(k)

            def modulated(name, s, nt):
                streams = nt // LAT

                def emit(k):
                    for dst in (full[:, k % 2], a_hi[:, k]):
                        for v in range(streams):
                            c = slice(v * LAT, (v + 1) * LAT)
                            last = act.activation(dst[:, c], xn[:, k % 2, c], ACT.Identity,
                                                  bias=shift[:, s, v, k:k + 1], scale=scale[:, s, v, k:k + 1])
                    last.then_inc(nhi_ready, 1)
                norm_apply(name, DT, emit)

            def ffn(s, name, nt, next_norm):
                modulated(name, (0, 2, 3, 5)[s], nt)
                w, f, b = FFN_W[s], s * FFN_STEPS, B_FFN[s]
                for g, size in enumerate(GROUPS):
                    with act.Fori(0, size - 1, 2) as i:
                        for j in range(2):
                            act.wait_ge(slab_done, i + (w + j + 1))
                            act.wait_ge(raw_loaded[(w + j) % 2], i * 8 + 16 * ((w + j + 2) // 2 + 1))
                            act.activation(w_hi[:, (w + j) % 2], raw[:, (w + j) % 2],
                                           ACT.Copy).then_inc(hi_ready, 1)
                            act.activation(sil[:, (f + j) % 2, 0:nt], ps[2 * ((f + j) % 2)][:, 0:nt],
                                           ACT.Silu).then_inc(sil_ready, 1)
                            act.wait_ge(pair_free, i + (f + j + 3))
                            act.activation(h_hi[:, ds(i + j, 1), 0:nt].rearrange("p a n -> p (a n)"),
                                           prod[:, (f + j) % 2, 0:nt], ACT.Copy).then_inc(hhi_ready, 1)
                    w, f = w + size, f + size
                    last = g == len(GROUPS) - 1

                    def out_step(j, i=None, split=True):
                        k = (lambda x: x) if i is None else (lambda x: i + x)
                        if last:
                            act.wait_ge(out_free[0], k(b + j + 3))
                            squares(RES[next_norm], j, 0, nt, i)
                        if split:
                            act.wait_ge(slab_done, k(w + j + 1))
                            value = 16 * ((w + j + 2) // 2 + 1)
                            act.wait_ge(raw_loaded[(w + j) % 2], value if i is None else i * 8 + value)
                            act.activation(w_hi[:, (w + j) % 2], raw[:, (w + j) % 2],
                                           ACT.Copy).then_inc(hi_ready, 1)
                        if last:
                            act.wait_ge(out_free[1], k(b + j + 3))
                            squares(RES[next_norm], j, 1, nt, i)
                    if w + 4 == N_SLABS:
                        for j in range(4):
                            out_step(j, split=j < 2)
                    else:
                        with act.Fori(0, 3, 2) as i:
                            for j in range(2):
                                out_step(j, i)
                    w, b = w + 4, b + 4

            def pieces(j, piece, base_wait=None):
                src, hi, _, runs, (s, value) = piece
                act.wait_ge(s, value)
                if runs:
                    r = ROPE_INDEX[j]
                    if len(runs) == 1:
                        if j >= 2:
                            act.wait_ge(piece_lo, j - 1)
                        act.activation(full[:, r % 2, LAT:TOK], src[:, LAT:TOK], ACT.Copy).then_inc(rope_ctx, 1)
                    act.wait_ge(rope_full, r + 1)
                    act.activation(hi, full[:, r % 2], ACT.Copy).then_inc(piece_hi, 1)
                else:
                    act.activation(hi, src[:], ACT.Copy).then_inc(piece_hi, 1)

            def attention(units, u0, sink, factor, pt_hi_buf, out_to, beside=None):
                for i in range(len(units) + 6):
                    if i < len(units):
                        h, qts, at = units[i]
                        u = u0 + i
                        act.wait_ge(nmax_ready, u + 1)
                        if i >= 3:
                            act.wait_ge(pt_done, u - 2)
                        for n, (_, _, c0, width) in enumerate(spans(qts)):
                            last = act.activation(probs[:, i % 3, c0:c0 + width], ps[S_BANK[i % 3]][:, c0:c0 + width],
                                                  ACT.Exp, bias=nmax[:, at + n:at + n + 1], scale=factor,
                                                  accum_out=den[:, at + n:at + n + 1])
                        last.then_inc(exp_done, 1)
                        if sink:
                            act.activation(esink[:, at:at + len(qts)], nmax[:, at:at + len(qts)], ACT.Exp,
                                           bias=vec[:, V_SINK + h:V_SINK + h + 1]).then_inc(sink_done, 1)
                    if beside is not None and i < len(units):
                        beside(i)
                    if 2 <= i < len(units) + 2:
                        e = i - 2
                        act.wait_ge(pt_done, u0 + e + 1)
                        if e >= 4:
                            act.wait_ge(pv_done, u0 // 2 + e // 2 - 1)
                        act.activation(pt_unit(pt_hi_buf, e, units[e][1]), pt_bank(e, units[e][1]),
                                       ACT.Copy).then_inc(pt_hi, 1)
                    if i >= 7 and i % 2:
                        p = (i - 7) // 2
                        act.wait_ge(pv_done, u0 // 2 + p + 1)
                        for rows, c, dst in out_to(a_hi, p):
                            last = act.activation(dst, ps[O_BANK[p % 2]][rows, c], ACT.Copy)
                        last.then_inc(ot_hi, 1)

            def mixer_out(w, b, nt, next_norm):
                for j in range(4):
                    for t in range(2):
                        act.wait_ge(out_free[t], b + j + 3)
                        squares(RES[next_norm], j, t, nt)
                    act.wait_ge(slab_done, w + j + 1)
                    split_hi(w + j + 2, (w + j) % 2, w + j + 2)

            act.wait_ge(in_cond, 16)
            act.activation(cb[:], cb[:], ACT.Silu).then_inc(cond_ready, 1)
            act.wait_ge(in_tok, 16)
            for sl in range(4):
                for t in range(2):
                    squares(0, sl, t, TOK)
            act.wait_ge(in_small, 32)
            act.activation(ident_r[:], ident, ACT.Copy).then_inc(act_const, 1)
            act.activation(mask_r[:], cst[:, C_MASK:C_MASK + 2 * P].rearrange("p (a n) -> p a n", a=2),
                           ACT.Copy).then_inc(act_const, 1)
            split_hi(0, 0, 0)
            split_hi(1, 1, 1)
            ffn(0, "ffn0", TOK, "ab")

            modulated("ab", 1, TOK)
            def tap_products(first, last):
                for n in range(first, last):
                    c, tap = n % 2, n // 2 + 1
                    if n >= 3:
                        act.wait_ge(tap_add, n - 2)
                    act.activation(tap_slot(n).rearrange("p (v n) -> p v n", v=2), ypad[:, c, :, tap:tap + LAT],
                                   ACT.Copy, scale=vec[:, V_WDW + c * TAPS + tap:V_WDW + c * TAPS + tap + 1]) \
                       .then_inc(tap_prod, 1)

            w = W_AB
            for c in range(CT):
                act.wait_ge(slab_done, w + c + 1)
                split_hi(w + c + 2, (w + c) % 2, w + c + 2)
                if c >= 2:
                    act.wait_ge(glu_done, c - 1)
                act.activation(sil[:, c % 2], ps[2 * (c % 2) + 1][:], ACT.Sigmoid).then_inc(glu_sig, 1)
                if c < 2:
                    act.wait_ge(glu_done, c + 1)
                    act.wait_ge(normed, NORM_BASE["ab"] + DT)
                    act.activation(conv[:, c].rearrange("p (v n) -> p v n", v=2), ypad[:, c, :, 0:LAT], ACT.Identity,
                                   bias=vec[:, V_BDW + c:V_BDW + c + 1],
                                   scale=vec[:, V_WDW + c * TAPS:V_WDW + c * TAPS + 1]).then_inc(tap_first, 1)
                else:
                    tap_products(5 * (c - 2), 5 * (c - 1))
            for j in range(N_AB):
                if j in (0, 2, 4):
                    x = w + 4 + j // 2
                    act.wait_ge(slab_done, x + 1)
                    split_hi(x + 2, x % 2, x + 2)
                if j == N_AB - 1:
                    act.wait_ge(slab_done, w + 7)
                    act.wait_ge(piece_lo, 4)
                    act.activation(full[:, 1], ps[1][:], ACT.Copy).then_inc(v_copy, 1)
                pieces(j, AB_PIECES[j])
                if j in (1, 3, 5):
                    tap_products(10 + 5 * (j // 2), 15 + 5 * (j // 2))

            def ab_beside(i):
                if 25 + 2 * i < CONV_ADDS:
                    tap_products(25 + 2 * i, min(27 + 2 * i, CONV_ADDS))
                if i in (LN_UNIT + 3, LN_UNIT + 4):
                    for c in (0, 1) if i == LN_UNIT + 3 else (2, 3):
                        act.wait_ge(ln_cent, c + 1)
                        if c >= 2:
                            act.wait_ge(stat_add, 1)
                        act.activation(sq[:, c % 2], conv[:, c], ACT.Square).then_inc(stat_sq, 1)
            attention(AB_UNITS, 0, True, A_DIM ** -0.5, AB_PT[0], ab_out, ab_beside)

            def ln_emit(k):
                for dst in (full[:, k % 2], a_hi[:, 4 + k]):
                    last = act.activation(dst, xn[:, k % 2], ACT.Silu, bias=vec[:, V_LNB + k:V_LNB + k + 1],
                                          scale=vec[:, V_LNG + k:V_LNG + k + 1])
                last.then_inc(nhi_ready, 1)
            norm_apply("ln", CT, ln_emit)
            mixer_out(W_AB + 7, B_AB, TOK, "ffn1")

            ffn(1, "ffn1", TOK, "ffn2")
            ffn(2, "ffn2", TOK, "mla")

            modulated("mla", 4, TOK)
            w = W_MLA
            for i, nt in ((0, LAT), (1, TOK)):
                act.wait_ge(slab_done, w + i + 1)
                for t in range(2):
                    dst = spare[:, t * LAT:(t + 1) * LAT] if i == 0 else spare[:, (1 + t) * TOK:(2 + t) * TOK]
                    act.activation(dst, ps[2 * i + t][:, 0:nt], ACT.Copy).then_inc(lat_copy, 1)
                    if i:
                        act.wait_ge(stat_ready, 1)
                    act.activation(sq[:, t, 0:nt], ps[2 * i + t][:, 0:nt], ACT.Square).then_inc(stat_sq, 1)
                split_hi(w + i + 2, (w + i) % 2, w + i + 2)

            def lora_emit(g, nt, dst):
                def emit(k):
                    gcol = vec[:, g + k:g + k + 1]
                    act.activation(full[:, k % 2, 0:nt], xn[:, k % 2, 0:nt], ACT.Copy, scale=gcol)
                    act.activation(dst(k), xn[:, k % 2, 0:nt], ACT.Copy, scale=gcol).then_inc(nhi_ready, 1)
                return emit
            norm_apply("cq", 2, lora_emit(V_GQ, LAT, lambda k: l_hi[:, 0, k * LAT:(k + 1) * LAT]))
            norm_apply("ckv", 2, lora_emit(V_GKV, TOK, lambda k: l_hi[:, 1 + k]))
            act.wait_ge(normed, NORM_BASE["ckv"] + 2)
            j = N_AB
            for i, parts in enumerate(MLA_STEPS):
                for _ in parts:
                    pieces(j, MLA_PIECES[j - N_AB])
                    j += 1
                if MLA_SIGNAL[i][0] is slab_done:
                    x = MLA_SIGNAL[i][1] - 1
                    split_hi(x + 2, x % 2, x + 2)
            attention(MLA_UNITS, len(AB_UNITS), False, (NOPE + ROPE) ** -0.5, MLA_PT[0], mla_out)
            mixer_out(W_MLA + 6, B_MLA, LAT, "ffn3")

            ffn(3, "ffn3", LAT, "final")
            base = NORM_BASE["final"]
            for k in range(DT):
                act.wait_ge(xn_ready, base + k + 1)
                act.activation(spare[:, k * LAT:(k + 1) * LAT], xn[:, k % 2, 0:LAT], ACT.Copy,
                               scale=vec[:, V_GF + k:V_GF + k + 1]).then_inc(y_ready, 1)

        @block.vector
        def _(dve):
            count = [0]

            def link(ins):
                count[0] += 1
                ins.then_inc(chain, 1)
                dve.wait_ge(chain, count[0])

            def mod_dot(slot, value, n):
                dve.wait_ge(mod_loaded[slot], value)
                dve.wait_ge(mod_first, n + 1)
                dve.tensor_tensor_reduce(unread[:], mring[:, slot], cb[:, 0], 1.0, 0.0,
                                         ALU.mult, ALU.add, stage[:, 0, slot:slot + 1]).then_inc(mod_first, 1)
                dve.tensor_tensor_reduce(mring[:, slot], mring[:, slot], cb[:, 1], 1.0, 0.0, ALU.mult, ALU.add,
                                         stage[:, 1, slot:slot + 1]).then_inc(mod_dots, 1)

            def mod_store(n, done):
                dve.wait_ge(mod_dots, done)
                dve.tensor_copy(modc[:, :, ds(n, 4)], stage[:]).then_inc(mod_cols, 4)
                dve.wait_ge(mod_cols, done)

            def finalize(layer, place, parts=("shift", "scale", "gate")):
                s = 3 * layer + place
                base = layer * MODT + place * 3 * DT

                def summed(dst, c):
                    b = vec[:, V_BMOD + base + c * DT:V_BMOD + base + (c + 1) * DT]
                    return dve.tensor_tensor(dst, modc[:, :, base + c * DT:base + (c + 1) * DT],
                                             b.unsqueeze(1).to_broadcast([P, 2, DT]), ALU.add)
                if "shift" in parts:
                    link(summed(shift[:, s], 0))
                if "scale" in parts:
                    link(summed(mtmp[:], 1))
                    g = vec[:, V_G + s * DT:V_G + (s + 1) * DT].unsqueeze(1).to_broadcast([P, 2, DT])
                    link(dve.scalar_tensor_tensor(out=scale[:, s], in0=mtmp[:], scalar=1.0, in1=g,
                                                  op0=ALU.add, op1=ALU.mult))
                if "gate" in parts:
                    link(summed(mtmp[:], 2))
                    link(dve.tensor_scalar(gate[:, s], mtmp[:], 1.0 if place == 1 else 0.5, None, ALU.mult))

            def zero_sum(n):
                dve.memset(ss[:, 0], 0.0).then_inc(ss_sum[1], 1)

            def add_square(n, sl, t, nt, i=None):
                k = (lambda x: x) if i is None else (lambda x: i + x)
                dve.wait_ge(sq_ready[t], k(4 * n + sl + 1))
                if t:
                    dve.wait_ge(ss_sum[0], k(4 * n + sl + 1))
                else:
                    dve.wait_ge(ss_sum[1], k(5 * n + sl + 1))
                dve.tensor_tensor(ss[:, 0, 0:nt], ss[:, 0, 0:nt], sq[:, t, 0:nt], ALU.add).then_inc(ss_sum[t], 1)

            def rsqrt(name, bank, nt, inv_n, eps):
                c = nt // P
                dve.wait_ge(colsum, CALL[name] + 1)
                link(dve.tensor_scalar(rv[:, 0:c], ps[bank][:, 0:c], inv_n, eps, ALU.mult, ALU.add))
                link(dve.tensor_scalar(ri[:, 0:c], rv[:, 0:c].bitcast(I32), 1, None, ALU.logical_shift_right))
                link(dve.tensor_scalar(ri[:, 0:c], ri[:, 0:c], -1.0, float(0x5F3759DF), ALU.mult, ALU.add))
                y = ri[:, 0:c].bitcast(F32)
                for _ in range(3):
                    link(dve.scalar_tensor_tensor(out=rt[:, 0:c], in0=y, scalar=-0.5, in1=y,
                                                  op0=ALU.mult, op1=ALU.mult))
                    link(dve.tensor_tensor(rt[:, 0:c], rt[:, 0:c], rv[:, 0:c], ALU.mult))
                    link(dve.scalar_tensor_tensor(out=ry[:, 0:c], in0=rt[:, 0:c], scalar=1.5, in1=y,
                                                  op0=ALU.add, op1=ALU.mult))
                    y = ry[:, 0:c]
                dve.tensor_tensor(diag[:, 0:c], ident.unsqueeze(1).to_broadcast([P, c, P]),
                                  ry[:, 0:c].unsqueeze(2).to_broadcast([P, c, P]), ALU.mult).then_inc(diag_ready, 1)

            def norm_apply(name, bank, tiles, nt, src, dst_hi, dst_lo):
                base = NORM_BASE[name]
                dve.wait_ge(rstd_bc, CALL[name] + 1)
                for k in range(tiles + 1):
                    if k < tiles:
                        dve.tensor_tensor(xn[:, k % 2, 0:nt], src(k), ps[bank][:, 0:nt],
                                          ALU.mult).then_inc(xn_ready, 1)
                    if k >= 1:
                        e = k - 1
                        dve.wait_ge(nhi_ready, base + e + 1)
                        dve.tensor_tensor(dst_lo(e), full[:, e % 2, 0:nt], dst_hi(e).bitcast(F32),
                                          ALU.subtract).then_inc(normed, 1)

            def residual_norm(name, nt):
                rsqrt(name, NORM_BANK, nt, 1.0 / D, NORM_EPS)
                norm_apply(name, NORM_BANK, DT, nt, lambda k: xT[:, k, 0:nt], lambda k: a_hi[:, k, 0:nt],
                           lambda k: a_lo[:, k, 0:nt])

            def out_tiles(s, b, w, j, nt, i=None):
                k = (lambda x: x) if i is None else (lambda x: i + x)
                for t in range(2):
                    dve.wait_ge(*((slab_done, k(w + j + 1)) if t else (tile0_done, k(b + j + 1))))
                    bank = ps[OUTB + 2 * ((b + j) % 2) + t]
                    m = 2 * j + t if i is None else i * 2 + (2 * j + t)
                    for v in range(nt // LAT):
                        c = slice(v * LAT, (v + 1) * LAT)
                        if i is None:
                            x, g = xT[:, m, c], gate[:, s, v, m:m + 1]
                        else:
                            x, g = xT[:, ds(m, 1), c].rearrange("p a n -> p (a n)"), gate[:, s, v, ds(m, 1)]
                        last = dve.scalar_tensor_tensor(out=x, in0=bank[:, c], scalar=g, in1=x,
                                                        op0=ALU.mult, op1=ALU.add)
                    last.then_inc(out_free[t], 1)

            def split_lo2(w, slot, i=None):
                dve.wait_ge(hi_ready, w + 1 if i is None else i + (w + 1))
                dve.tensor_tensor(w_lo[:, slot, HALF:SLAB], raw[:, slot, HALF:SLAB],
                                  w_hi[:, slot, HALF:SLAB].bitcast(F32), ALU.subtract).then_inc(lo2_ready, 1)

            def ffn(s, name, nt, next_norm, mods=0, n0=0, after_first=None):
                residual_norm(name, nt)
                sub = (0, 2, 3, 5)[s]
                w, f, b = FFN_W[s], s * FFN_STEPS, B_FFN[s]
                phase = 0
                for g, size in enumerate(GROUPS):
                    with dve.Fori(0, size - 1, 2) as i:
                        for j in range(2):
                            slot = (f + j) % 2
                            if w >= W_FFN3:
                                split_lo2(w + j + 2, (w + j) % 2, i)
                            dve.wait_ge(sil_ready, i + (f + j + 1))
                            dve.tensor_tensor(prod[:, slot, 0:nt], sil[:, slot, 0:nt], ps[2 * slot + 1][:, 0:nt],
                                              ALU.mult).then_inc(pair_free, 1)
                            if phase < mods:
                                mod_dot(2 * j, i * 8 + 16 * (n0 // 4 + 1), i * 2 + (n0 + 2 * j))
                            dve.wait_ge(hhi_ready, i + (f + j + 1))
                            hi = h_hi[:, ds(i + j, 1), 0:nt].rearrange("p a n -> p (a n)").bitcast(F32)
                            lo = h_lo[:, ds(i + j, 1), 0:nt].rearrange("p a n -> p (a n)")
                            dve.tensor_tensor(lo, prod[:, slot, 0:nt], hi, ALU.subtract).then_inc(hid_ready, 1)
                            if phase < mods:
                                mod_dot(2 * j + 1, i * 8 + 16 * (n0 // 4 + 1), i * 2 + (n0 + 2 * j + 1))
                        if phase < mods:
                            mod_store(i * 2 + n0, i * 2 + (n0 + 4))
                    if phase < mods:
                        n0 += 2 * size
                    phase += 1
                    w, f = w + size, f + size
                    if g == 0 and after_first is not None:
                        after_first(n0)
                    last = g == len(GROUPS) - 1
                    if last:
                        zero_sum(RES[next_norm])
                    if w + 4 == N_SLABS:
                        for j in range(4):
                            out_tiles(sub, b, w, j, nt)
                            if j < 2:
                                split_lo2(w + j + 2, (w + j) % 2)
                            add_square(RES[next_norm], j, 0, nt)
                            add_square(RES[next_norm], j, 1, nt)
                        continue
                    with dve.Fori(0, 3, 2) as i:
                        for j in range(2):
                            out_tiles(sub, b, w, j, nt, i)
                            if w >= W_FFN3:
                                split_lo2(w + j + 2, (w + j) % 2, i)
                            if phase < mods:
                                mod_dot(2 * j, i * 8 + 16 * (n0 // 4 + 1), i * 2 + (n0 + 2 * j))
                            if last:
                                add_square(RES[next_norm], j, 0, nt, i)
                                add_square(RES[next_norm], j, 1, nt, i)
                            if phase < mods:
                                mod_dot(2 * j + 1, i * 8 + 16 * (n0 // 4 + 1), i * 2 + (n0 + 2 * j + 1))
                        if phase < mods:
                            mod_store(i * 2 + n0, i * 2 + (n0 + 4))
                    if phase < mods:
                        n0 += 8
                    phase += 1
                    w, b = w + 4, b + 4
                return n0

            def rotate(src, dst):
                sw, t1, t2 = sq[:, 0, 0:LAT], sq[:, 0, LAT:TOK], sq[:, 1, 0:LAT]
                dve.stream_shuffle(sw, src, [(i + 16) % 32 for i in range(32)])
                link(dve.tensor_tensor(t1, src, cos, ALU.mult))
                link(dve.tensor_tensor(t2, sw, sin, ALU.mult))
                return dve.tensor_tensor(dst, t1, t2, ALU.add)

            def pieces(j, piece):
                src, hi, lo, runs, (s, value) = piece
                dve.wait_ge(s, value)
                if runs:
                    r = ROPE_INDEX[j]
                    if len(runs) == 1:
                        dve.wait_ge(rope_ctx, CTX_INDEX[j] + 1)
                    for n, (c0, c1) in enumerate(runs):
                        ins = rotate(src[:, c0:c1], full[:, r % 2, c0:c1])
                        if n == len(runs) - 1:
                            ins.then_inc(rope_full, 1)
                        else:
                            link(ins)
                    whole = full[:, r % 2]
                else:
                    whole = src[:]
                dve.wait_ge(piece_hi, j + 1)
                dve.tensor_tensor(lo, whole, hi.bitcast(F32), ALU.subtract).then_inc(piece_lo, 1)

            def conv_taps(first, last):
                for tap in range(first, last):
                    for c in (2, 3):
                        x = ypad[:, c, :, tap:tap + LAT]
                        acc = conv[:, c].rearrange("p (v n) -> p v n", v=2)
                        col = vec[:, V_WDW + c * TAPS + tap:V_WDW + c * TAPS + tap + 1]
                        if tap == 0:
                            ins = dve.tensor_scalar(acc, x, col, vec[:, V_BDW + c:V_BDW + c + 1],
                                                    ALU.mult, ALU.add)
                        else:
                            dve.wait_ge(conv_op, 2 * tap + c - 3)
                            ins = dve.scalar_tensor_tensor(out=acc, in0=x, scalar=col, in1=acc,
                                                           op0=ALU.mult, op1=ALU.add)
                        ins.then_inc(conv_op, 1)

            def attention(units, u0, sink, factor, pt_hi_buf, pt_lo_buf, out_to, beside=None):
                for i in range(len(units) + 6):
                    if i < len(units):
                        h, qts, at = units[i]
                        b = slice(at, at + len(qts))
                        dve.wait_ge(scores_done, u0 + i + 1)
                        link(dve.tensor_reduce(smax[:, b], ps[S_BANK[i % 3]][:].rearrange("p (b n) -> p b n", b=len(qts)),
                                               AX.X, ALU.max))
                        if sink:
                            ins = dve.tensor_scalar(nmax[:, b], smax[:, b], -factor, nsink[:, h:h + 1],
                                                    ALU.mult, ALU.min)
                        else:
                            ins = dve.tensor_scalar(nmax[:, b], smax[:, b], -factor, None, ALU.mult)
                        ins.then_inc(nmax_ready, 1)
                    if 1 <= i < len(units) + 1:
                        e = i - 1
                        h, qts, at = units[e]
                        b = slice(at, at + len(qts))
                        dve.wait_ge(exp_done, u0 + e + 1)
                        if sink:
                            dve.wait_ge(sink_done, u0 + e + 1)
                            link(dve.tensor_tensor(den[:, b], den[:, b], esink[:, b], ALU.add))
                        link(dve.reciprocal(rinv[:, b], den[:, b]))
                        if e >= 2:
                            dve.wait_ge(pt_done, u0 + e - 1)
                        for n in range(len(qts)):
                            last = dve.tensor_scalar(rdiag[:, e % 2, n], ident, rinv[:, at + n:at + n + 1], None,
                                                     ALU.mult)
                        last.then_inc(rdiag_ready, 1)
                    if beside is not None and i < len(units):
                        beside(i)
                    if 3 <= i < len(units) + 3:
                        e = i - 3
                        qts = units[e][1]
                        dve.wait_ge(pt_hi, u0 + e + 1)
                        dve.tensor_tensor(pt_unit(pt_lo_buf, e, qts), pt_bank(e, qts),
                                          pt_unit(pt_hi_buf, e, qts).bitcast(F32), ALU.subtract).then_inc(pt_lo, 1)
                    if i >= 7 and i % 2:
                        p = (i - 7) // 2
                        dve.wait_ge(ot_hi, u0 // 2 + p + 1)
                        for (rows, c, lo), (_, _, hi) in zip(out_to(a_lo, p), out_to(a_hi, p)):
                            last = dve.tensor_tensor(lo, ps[O_BANK[p % 2]][rows, c], hi.bitcast(F32), ALU.subtract)
                        last.then_inc(ot_lo, 1)

            def mixer_out(s, w, b, nt, next_norm):
                zero_sum(RES[next_norm])
                for j in range(4):
                    out_tiles(s, b, w, j, nt)
                    if w + j + 2 >= W_FFN3:
                        split_lo2(w + j + 2, (w + j) % 2)
                    add_square(RES[next_norm], j, 0, nt)
                    add_square(RES[next_norm], j, 1, nt)

            dve.memset(rt[:], 0.0).then_inc(out_free[0], 2)
            dve.memset(mtmp[:], 0.0).then_inc(out_free[1], 2)
            dve.memset(rinv[:], 0.0).then_inc(pair_free, 2)
            dve.memset(unread[:], 0.0).then_inc(mod_first, 1)
            dve.wait_ge(cond_ready, 1)
            with dve.Fori(0, MOD_FIRST - 3, 4) as n:
                for j in range(4):
                    mod_dot(j, n * 4 + 16, n + j)
                mod_store(n, n + 4)
            dve.wait_ge(in_small, 32)
            dve.wait_ge(mod_cols, MOD_FIRST)
            finalize(0, 0, ("shift", "scale"))
            link(dve.tensor_scalar(nsink[:], vec[:, V_SINK:V_SINK + HEADS], -1.0, None, ALU.mult))
            zero_sum(0)
            for sl in range(4):
                add_square(0, sl, 0, TOK)
                add_square(0, sl, 1, TOK)

            def first_gate(n):
                dve.wait_ge(mod_cols, n)
                finalize(0, 0, ("gate",))
            n0 = ffn(0, "ffn0", TOK, "ab", 6, MOD_FIRST, first_gate)
            dve.wait_ge(mod_cols, n0)
            finalize(0, 1)
            finalize(0, 2)

            residual_norm("ab", TOK)
            dve.wait_ge(gp_const, 2)
            for c in range(CT):
                dve.wait_ge(glu_sig, c + 1)
                dve.tensor_tensor(ypad[:, c, :, PAD:PAD + LAT], ps[2 * (c % 2)][:].rearrange("p (v n) -> p v n", v=2),
                                  sil[:, c % 2].rearrange("p (v n) -> p v n", v=2), ALU.mult).then_inc(glu_done, 1)
            dve.wait_ge(glu_done, CT)
            conv_taps(0, 6)
            for j in range(N_AB):
                pieces(j, AB_PIECES[j])
                if j in (1, 3, 4, 5):
                    conv_taps({1: 6, 3: 11, 4: 16, 5: 19}[j], {1: 11, 3: 16, 4: 19, 5: 21}[j])

            def ab_beside(i):
                if i < 5:
                    conv_taps(21 + 2 * i, 23 + 2 * i)
                if i == LN_UNIT:
                    dve.wait_ge(conv_op, 2 * TAPS)
                    dve.wait_ge(tap_add, CONV_ADDS)
                    link(dve.tensor_tensor(ss[:, 0], conv[:, 0], conv[:, 1], ALU.add))
                    link(dve.tensor_tensor(ss[:, 1], conv[:, 2], conv[:, 3], ALU.add))
                    dve.tensor_tensor(ss[:, 0], ss[:, 0], ss[:, 1], ALU.add).then_inc(ln_sum, 1)
                if i in (LN_UNIT + 2, LN_UNIT + 3):
                    dve.wait_ge(ln_mean, 1)
                    for c in (0, 1) if i == LN_UNIT + 2 else (2, 3):
                        dve.scalar_tensor_tensor(out=conv[:, c], in0=ps[LN_BANK][:], scalar=-1.0 / B_CH,
                                                 in1=conv[:, c], op0=ALU.mult, op1=ALU.add).then_inc(ln_cent, 1)
                if i == LN_UNIT + 4:
                    dve.wait_ge(stat_sq, 2)
                    dve.tensor_tensor(ss[:, 0], sq[:, 0], sq[:, 1], ALU.add).then_inc(stat_add, 1)
                if i == LN_UNIT + 5:
                    dve.wait_ge(stat_sq, 4)
                    link(dve.tensor_tensor(ss[:, 1], sq[:, 0], sq[:, 1], ALU.add))
                    dve.wait_ge(stat_add, 1)
                    dve.tensor_tensor(ss[:, 0], ss[:, 0], ss[:, 1], ALU.add).then_inc(stat_add, 1)
                if i == LN_UNIT + 6:
                    rsqrt("ln", LN_BANK, TOK, 1.0 / B_CH, LN_EPS)
            attention(AB_UNITS, 0, True, A_DIM ** -0.5, *AB_PT, ab_out, ab_beside)
            norm_apply("ln", LN_BANK, CT, TOK, lambda k: conv[:, k], lambda k: a_hi[:, 4 + k], lambda k: a_lo[:, 4 + k])
            mixer_out(1, W_AB + 7, B_AB, TOK, "ffn1")

            n0 = ffn(1, "ffn1", TOK, "ffn2", 5, n0)
            assert n0 == 2 * MODT
            dve.wait_ge(mod_cols, n0)
            for place in range(3):
                finalize(1, place)
            ffn(2, "ffn2", TOK, "mla")

            residual_norm("mla", TOK)
            for i, nt in ((0, LAT), (1, TOK)):
                dve.wait_ge(stat_sq, CT + 2 * i + 2)
                dve.tensor_tensor(ss[:, i, 0:nt], sq[:, 0, 0:nt], sq[:, 1, 0:nt], ALU.add).then_inc(stat_ready, 1)
            rsqrt("cq", NORM_BANK, LAT, 1.0 / LORA, NORM_EPS)
            dve.wait_ge(lat_copy, 2)
            norm_apply("cq", NORM_BANK, 2, LAT, lambda k: spare[:, k * LAT:(k + 1) * LAT],
                       lambda k: l_hi[:, 0, k * LAT:(k + 1) * LAT], lambda k: l_lo[:, 0, k * LAT:(k + 1) * LAT])
            rsqrt("ckv", NORM_BANK + 1, TOK, 1.0 / LORA, NORM_EPS)
            dve.wait_ge(lat_copy, 4)
            norm_apply("ckv", NORM_BANK + 1, 2, TOK, lambda k: spare[:, (1 + k) * TOK:(2 + k) * TOK],
                       lambda k: l_hi[:, 1 + k], lambda k: l_lo[:, 1 + k])
            for j in range(len(MLA_PIECES)):
                pieces(N_AB + j, MLA_PIECES[j])
            attention(MLA_UNITS, len(AB_UNITS), False, (NOPE + ROPE) ** -0.5, *MLA_PT, mla_out)
            mixer_out(4, W_MLA + 6, B_MLA, LAT, "ffn3")

            ffn(3, "ffn3", LAT, "final")
            rsqrt("final", NORM_BANK, LAT, 1.0 / D, NORM_EPS)
            dve.wait_ge(rstd_bc, CALL["final"] + 1)
            for k in range(DT):
                if k >= 2:
                    dve.wait_ge(y_ready, k - 1)
                dve.tensor_tensor(xn[:, k % 2, 0:LAT], xT[:, k, 0:LAT], ps[NORM_BANK][:, 0:LAT],
                                  ALU.mult).then_inc(xn_ready, 1)

        @block.tensor
        def _(pe):
            def passes(dst, lhs_hi, lhs_lo, rhs_hi, rhs_lo, start, stop):
                pe.matmul(dst, lhs_lo, rhs_hi, start=start, stop=False, skip_group_check=True)
                pe.matmul(dst, lhs_hi, rhs_lo, start=False, stop=False, skip_group_check=True)
                return pe.matmul(dst, lhs_hi, rhs_hi, start=False, stop=stop, skip_group_check=True)

            def weights(slot, c0, n=P):
                return w_hi[:, slot, c0:c0 + n], w_lo[:, slot, c0:c0 + n]

            def two_tiles(slot, banks, nt, name=None):
                for k in range(DT):
                    if name is not None:
                        pe.wait_ge(normed, NORM_BASE[name] + k + 1)
                    for t in range(2):
                        last = passes(ps[banks[t]][:, 0:nt], *weights(slot, t * HALF + k * P),
                                      a_hi[:, k, 0:nt], a_lo[:, k, 0:nt], k == 0, k == DT - 1)
                return last

            def token_colsum(bank, sums, nt):
                for c in range(nt // P):
                    last = pe.matmul(ps[bank][:, c:c + 1], sums[:, c * P:(c + 1) * P], ones[:, 0:1],
                                     start=True, stop=True)
                last.then_inc(colsum, 1)

            def token_spread(name, bank, nt):
                pe.wait_ge(diag_ready, CALL[name] + 1)
                pe.matmul(ps[bank][:, 0:nt], ones[:], diag[:].rearrange("p a n -> p (a n)")[:, 0:nt],
                          start=True, stop=True).then_inc(rstd_bc, 1)

            def token_sum(name, bank, sums, nt):
                token_colsum(bank, sums, nt)
                token_spread(name, bank, nt)

            def residual_norm(name, nt):
                n = RES[name]
                pe.wait_ge(ss_sum[1], 5 * n + 5)
                token_sum(name, NORM_BANK, ss[:, 0], nt)

            def out_slab(b, slot, j, kt, hi, lo, nt, w, i=None, waits=None):
                k0 = (lambda x: x) if i is None else (lambda x: i + x)
                pe.wait_ge(lo_ready, k0(w + j + 1))
                if w >= W_FFN3:
                    pe.wait_ge(lo2_ready, k0(w + j + 1 - W_FFN3))
                for t in range(2):
                    pe.wait_ge(out_free[t], k0(b + j + 1))
                    for k in range(kt):
                        if waits is not None and t == 0:
                            waits(k)
                        last = passes(ps[OUTB + 2 * ((b + j) % 2) + t][:, 0:nt],
                                      *weights(slot, (t * kt + k) * P), hi[:, k, 0:nt], lo[:, k, 0:nt],
                                      k == 0, k == kt - 1)
                    last.then_inc(slab_done if t else tile0_done, 1)

            def ffn(s, name, nt):
                residual_norm(name, nt)
                w, f, b = FFN_W[s], s * FFN_STEPS, B_FFN[s]
                for g, size in enumerate(GROUPS):
                    with pe.Fori(0, size - 1, 2) as i:
                        for j in range(2):
                            pe.wait_ge(lo_ready, i + (w + j + 1))
                            if w >= W_FFN3:
                                pe.wait_ge(lo2_ready, i + (w + j + 1 - W_FFN3))
                            pe.wait_ge(pair_free, i + (f + j + 1))
                            p = (f + j) % 2
                            two_tiles((w + j) % 2, (2 * p, 2 * p + 1), nt,
                                      name if g == 0 and j == 0 else None).then_inc(slab_done, 1)
                    w, f = w + size, f + size

                    def hidden(k, f=f, size=size):
                        if k >= size - 4:
                            pe.wait_ge(hid_ready, f - size + k + 1)
                    with pe.Fori(0, 3, 2) as i:
                        for j in range(2):
                            out_slab(b, (w + j) % 2, j, size, h_hi, h_lo, nt, w, i, hidden if j == 0 else None)
                    w, b = w + 4, b + 4

            def attention(units, u0, chunks, mask, v, pt_buf, beside=None):
                for i in range(len(units) + 5):
                    if i < len(units):
                        h, qts, _ = units[i]
                        bank = ps[S_BANK[i % 3]]
                        if i >= 3:
                            pe.wait_ge(exp_done, u0 + i - 2)
                        for qt, key0, c0, width in spans(qts):
                            parts = chunks(h, qt, key0)
                            for n, part in enumerate(parts):
                                last = passes(bank[:, c0:c0 + width], *part, n == 0, n == len(parts) - 1)
                            if mask and qt < 2:
                                m0 = P * (1 - qt)
                                last = pe.matmul(bank[:, m0:m0 + P], ident_r[:], mask_r[:, qt],
                                                 start=False, stop=True, skip_group_check=True)
                        last.then_inc(scores_done, 1)
                    if beside is not None and i < len(units):
                        beside(i)
                    if i >= 5 and i % 2:
                        p = (i - 5) // 2
                        h, qts, _ = units[2 * p]
                        n = len(qts) * P
                        pe.wait_ge(pt_lo, u0 + 2 * p + 2)
                        if p >= 2:
                            pe.wait_ge(ot_lo, u0 // 2 + p - 1)
                        tiles = TOK // n
                        for k in range(tiles):
                            at = [x[p % 2].rearrange("p a n -> p (a n)")[:, 2 * k * n:2 * (k + 1) * n]
                                  for x in pt_buf]
                            last = passes(ps[O_BANK[p % 2]][:, 0:2 * n], *v(h, qts[0][1] // P + k), *at,
                                          k == 0, k == tiles - 1)
                        last.then_inc(pv_done, 1)
                    if 2 <= i < len(units) + 2:
                        e = i - 2
                        qts = units[e][1]
                        pe.wait_ge(rdiag_ready, u0 + e + 1)
                        if e >= 2:
                            pe.wait_ge(pt_lo, u0 + e - 1)
                        for _, _, c0, width in spans(qts):
                            b = c0 // width
                            for k in range(width // P):
                                c = (k * len(qts) + b) * P
                                last = pe.matmul(ps[PT_BANK[e % 2]][:, c:c + P],
                                                 probs[:, e % 3, c0 + k * P:c0 + (k + 1) * P], rdiag[:, e % 2, b],
                                                 start=True, stop=True)
                        last.then_inc(pt_done, 1)

            pe.wait_ge(gp_const, 1)
            pe.wait_ge(act_const, 2)
            ffn(0, "ffn0", TOK)

            residual_norm("ab", TOK)
            w = W_AB
            for c in range(6):
                pe.wait_ge(lo_ready, w + c + 1)
                if 2 <= c < 6:
                    pe.wait_ge(glu_done, c - 1)
                two_tiles((w + c) % 2, (2 * (c % 2), 2 * (c % 2) + 1), TOK,
                          "ab" if c == 0 else None).then_inc(slab_done, 1)
            pe.wait_ge(lo_ready, w + 7)
            pe.wait_ge(piece_lo, 2)
            slot = (w + 6) % 2
            for k in range(DT):
                last = passes(ps[0][:], *weights(slot, k * P), a_hi[:, k], a_lo[:, k], k == 0, k == DT - 1)
            last.then_inc(step_done, 1)
            for k in range(DT):
                last = passes(ps[1][:], *weights(slot, HALF + k * P), a_hi[:, k], a_lo[:, k], k == 0, k == DT - 1)
            last.then_inc(slab_done, 1)
            pe.wait_ge(v_copy, 1)
            for kt in range(4):
                last = pe.transpose(ps[2][:, kt * P:(kt + 1) * P], full[:, 1, kt * P:(kt + 1) * P], ident)
            last.then_inc(step_done, 1)
            pe.wait_ge(piece_lo, N_AB)

            def ab_chunks(h, qt, k0):
                r = slice(A_DIM * (h // 4), A_DIM * (h // 4 + 1))
                q = [x[r, h % 4, qt * P:(qt + 1) * P] for x in (h_hi, h_lo)]
                return [(*q, h_hi[r, 4, k0:TOK], h_lo[r, 4, k0:TOK])]

            def ab_v(h, kt):
                return h_hi[:, 5, kt * P:(kt + 1) * P], h_lo[:, 5, kt * P:(kt + 1) * P]
            def ab_beside(i):
                if i == LN_UNIT + 1:
                    pe.wait_ge(ln_sum, 1)
                    pe.matmul(ps[LN_BANK][:], ones[:], ss[:, 0], start=True, stop=True).then_inc(ln_mean, 1)
                if i == LN_UNIT + 6:
                    pe.wait_ge(stat_add, 2)
                    token_colsum(LN_BANK, ss[:, 0], TOK)
            attention(AB_UNITS, 0, ab_chunks, True, ab_v, AB_PT, ab_beside)
            token_spread("ln", LN_BANK, TOK)

            def mixer_out(b, w, nt, inputs):
                for j in range(4):
                    out_slab(b, (w + j) % 2, j, DT, a_hi, a_lo, nt, w, None, inputs if j == 0 else None)

            def ab_inputs(k):
                if k < 4:
                    pe.wait_ge(ot_lo, 3 * (k + 1))
                else:
                    pe.wait_ge(normed, NORM_BASE["ln"] + k - 3)
            mixer_out(B_AB, W_AB + 7, TOK, ab_inputs)
            ffn(1, "ffn1", TOK)
            ffn(2, "ffn2", TOK)

            residual_norm("mla", TOK)
            w = W_MLA
            pe.wait_ge(lo_ready, w + 1)
            two_tiles(w % 2, (0, 1), LAT, "mla").then_inc(slab_done, 1)
            pe.wait_ge(lo_ready, w + 2)
            two_tiles((w + 1) % 2, (2, 3), TOK).then_inc(slab_done, 1)
            pe.wait_ge(lo_ready, w + 3)
            pe.wait_ge(stat_ready, 1)
            pe.wait_ge(lat_copy, 2)
            slot = (w + 2) % 2
            for k in range(DT):
                last = passes(ps[0][:], *weights(slot, k * P), a_hi[:, k], a_lo[:, k], k == 0, k == DT - 1)
            last.then_inc(step_done, 1)
            token_sum("cq", NORM_BANK, ss[:, 0], LAT)
            pe.wait_ge(stat_ready, 2)
            token_sum("ckv", NORM_BANK + 1, ss[:, 1], TOK)
            pe.wait_ge(normed, NORM_BASE["cq"] + 2)
            pe.wait_ge(lat_copy, 4)

            def queries(i, slot, c0):
                for t in range(4):
                    for k in range(2):
                        c = k * LAT
                        last = passes(ps[2 * (i % 2) + t // 2][:, (t % 2) * LAT:(t % 2 + 1) * LAT],
                                      *weights(slot, c0 + (2 * t + k) * P), l_hi[:, 0, c:c + LAT],
                                      l_lo[:, 0, c:c + LAT], k == 0, k == 1)
                return last

            def step(i, emit):
                if i >= 2:
                    pe.wait_ge(piece_lo, MLA_PIECES_BY[i - 2])
                emit().then_inc(MLA_SIGNAL[i][0], 1)

            step(1, lambda: queries(1, slot, HALF))
            pe.wait_ge(lo_ready, w + 4)
            step(2, lambda: queries(2, (w + 3) % 2, 0))
            step(3, lambda: queries(3, (w + 3) % 2, HALF))
            pe.wait_ge(normed, NORM_BASE["ckv"] + 2)
            pe.wait_ge(lo_ready, w + 5)

            def nope_keys(i):
                def emit():
                    for t in range(2):
                        m = 2 * (i - 4) + t
                        for k in range(2):
                            last = passes(ps[2 * (i % 2) + t][:], *weights((w + 4) % 2, (2 * m + k) * P),
                                          l_hi[:, 1 + k], l_lo[:, 1 + k], k == 0, k == 1)
                    return last
                return emit

            def values(i):
                def emit():
                    kt = i - 8
                    for t in range(2):
                        for k in range(2):
                            last = passes(ps[2 * (i % 2) + t][:], l_hi[:, 1 + k, kt * P:(kt + 1) * P],
                                          l_lo[:, 1 + k, kt * P:(kt + 1) * P],
                                          *weights((w + 5) % 2, k * D + t * 512, 512), k == 0, k == 1)
                    return last
                return emit
            for i in range(4, 8):
                step(i, nope_keys(i))
            pe.wait_ge(lo_ready, w + 6)
            for i in range(8, 12):
                step(i, values(i))
            pe.wait_ge(piece_lo, N_AB + len(MLA_PIECES))

            def mla_chunks(h, qt, k0):
                n, c = h // 2, (h % 2) * LAT + qt * P
                r = slice(ROPE * (h % 2), ROPE * (h % 2 + 1))
                tile = h // 2
                rn, rc = 4 + tile // 2, (tile % 2) * LAT + qt * P
                return [(q_hi[:, n, c:c + P], q_lo[:, n, c:c + P], a_hi[:, h], a_lo[:, h]),
                        (q_hi[r, rn, rc:rc + P], q_lo[r, rn, rc:rc + P], q_hi[r, 6], q_lo[r, 6])]

            def mla_v(h, kt):
                n, c = 2 * kt + h // 4, (h % 4) * C_V
                return h_hi[:, n, c:c + C_V], h_lo[:, n, c:c + C_V]
            attention(MLA_UNITS, len(AB_UNITS), mla_chunks, False, mla_v, MLA_PT)
            mixer_out(B_MLA, W_MLA + 6, LAT, lambda k: pe.wait_ge(ot_lo, AB_PAIRS + k + 1))
            ffn(3, "ffn3", LAT)
            residual_norm("final", LAT)


def _tiles(w, rows, width):
    k, m = w.shape
    return w.reshape(rows, P, m // width, width).transpose(2, 1, 0, 3)


def _ffn_slabs(w_in, w_out):
    n = D_FF // P
    gate_up = _tiles(w_in, DT, P).reshape(2, n, P, HALF)
    w_out = _tiles(w_out, n, P)
    slabs, at = [], 0
    for size in GROUPS:
        slabs.append(gate_up[:, at:at + size].transpose(1, 2, 0, 3).reshape(size, P, SLAB))
        part = w_out[:, :, at:at + size].reshape(4, 2, P, size * P).transpose(0, 2, 1, 3).reshape(4, P, 2 * size * P)
        if part.shape[2] < SLAB:
            part = np.concatenate([part, np.zeros((4, P, SLAB - part.shape[2]), part.dtype)], axis=2)
        slabs.append(part)
        at += size
    return slabs


def _pairs(w, rows):
    t = _tiles(w, rows, P)
    return t.reshape(t.shape[0] // 2, 2, P, rows * P).transpose(0, 2, 1, 3).reshape(-1, P, 2 * rows * P)


def _stream(ffn_w_in, ffn_w_out, ab_w_in, ab_w_out, c_w_dq, c_w_uq, c_w_dkv, c_w_uk, c_w_uv, c_w_o):
    aq, akv = HEADS * A_DIM, A_KV * A_DIM
    wq = ab_w_in[:, :aq].reshape(D, 2, 4, A_DIM).transpose(0, 2, 1, 3).reshape(D, aq)
    ab_w_out = np.concatenate([ab_w_out[:aq].reshape(2, 4, A_DIM, D).transpose(1, 0, 2, 3).reshape(aq, D),
                               ab_w_out[aq:]], axis=0)
    wa, wg = ab_w_in[:, aq + 2 * akv:aq + 2 * akv + B_CH], ab_w_in[:, aq + 2 * akv + B_CH:]
    wconv = np.concatenate([wa.reshape(D, CT, 1, P), wg.reshape(D, CT, 1, P)], axis=2).reshape(D, 2 * B_CH)
    wab = np.concatenate([wconv, wq, ab_w_in[:, aq:aq + 2 * akv]], axis=1)
    uq = c_w_uq.reshape(LORA, HEADS, NOPE + ROPE)
    uq = np.concatenate([uq[:, :, :NOPE].reshape(LORA, -1), uq[:, :, NOPE:].reshape(LORA, -1)], axis=1)
    uq = _tiles(uq, 2, P).transpose(1, 0, 2, 3).reshape(P, 3 * HALF)
    kr = np.concatenate([c_w_dkv[:, LORA:], c_w_dkv[:, LORA:]], axis=1)
    kr = _tiles(kr, DT, P).reshape(P, HALF)
    mla = [_pairs(c_w_dq, DT), _pairs(c_w_dkv[:, :LORA], DT),
           np.concatenate([kr, uq[:, :HALF]], axis=1)[None], uq[:, HALF:][None],
           _tiles(c_w_uk, 2, P).transpose(1, 0, 2, 3).reshape(1, P, SLAB),
           c_w_uv.reshape(2, P, D).transpose(1, 0, 2).reshape(1, P, SLAB),
           _pairs(c_w_o, DT)]
    slabs = (_ffn_slabs(ffn_w_in[0, 0], ffn_w_out[0, 0]) + [_pairs(wab, DT), _pairs(ab_w_out, DT)]
             + _ffn_slabs(ffn_w_in[0, 1], ffn_w_out[0, 1]) + _ffn_slabs(ffn_w_in[1, 0], ffn_w_out[1, 0])
             + mla + _ffn_slabs(ffn_w_in[1, 1], ffn_w_out[1, 1]))
    return np.concatenate(slabs, axis=0)


def _columns(a):
    return a.reshape(-1, P).T


def _constants():
    q, k = np.arange(P)[:, None], np.arange(P)[None, :]
    mask0 = np.where(k <= q, 0.0, NEG)
    mask1 = np.where(q <= k, 0.0, NEG)
    t = np.arange(LAT)
    half = ROPE // 2
    inv = (np.float32(10000.0) ** (-np.arange(0, half, 2, dtype=np.float32) / np.float32(half))).astype(np.float32)
    row = (t // GRID_W).astype(np.float32)[:, None] * inv
    col = (t % GRID_W).astype(np.float32)[:, None] * inv
    ang = np.concatenate([row, row, col, col], axis=1).astype(np.float32)
    sign = np.tile(np.concatenate([-np.ones(half // 2), np.ones(half // 2)]), 2)
    cos, sin = np.cos(ang).T, (np.sin(ang) * sign).T
    c = np.concatenate([np.eye(P), mask0, mask1, np.tile(cos, (2, 1)), np.tile(sin, (2, 1))], axis=1)
    return np.ascontiguousarray(c, dtype=np.float32)


def kernel(x, c, ctx, c_ctx, w_mod, b_mod, g_norm, ffn_w_in, ffn_w_out, ab_w_in, a_sink, b_w_dw, b_b_dw,
           b_ln_g, b_ln_b, ab_w_out, c_w_dq, c_g_q, c_w_uq, c_w_dkv, c_g_kv, c_w_uk, c_w_uv, c_w_o, g_final):
    import concourse.bacc as bacc
    from concourse.bass_utils import run_bass_kernel_spmd

    (x, c, ctx, c_ctx, w_mod, b_mod, g_norm, ffn_w_in, ffn_w_out, ab_w_in, a_sink, b_w_dw, b_b_dw, b_ln_g, b_ln_b,
     ab_w_out, c_w_dq, c_g_q, c_w_uq, c_w_dkv, c_g_kv, c_w_uk, c_w_uv, c_w_o, g_final) = (
        np.asarray(a) for a in (x, c, ctx, c_ctx, w_mod, b_mod, g_norm, ffn_w_in, ffn_w_out, ab_w_in, a_sink, b_w_dw,
                                b_b_dw, b_ln_g, b_ln_b, ab_w_out, c_w_dq, c_g_q, c_w_uq, c_w_dkv, c_g_kv, c_w_uk,
                                c_w_uv, c_w_o, g_final))
    tokens = np.concatenate([x[0], ctx[0]], axis=0).T.reshape(DT, P, TOK).transpose(1, 0, 2)
    taps = b_w_dw[0].reshape(TAPS, CT, P).transpose(2, 1, 0).reshape(P, CT * TAPS)
    vecs = np.concatenate([_columns(g_norm), _columns(b_mod), _columns(g_final), _columns(b_b_dw), _columns(b_ln_g),
                           _columns(b_ln_b), _columns(c_g_q), _columns(c_g_kv),
                           np.broadcast_to(a_sink, (P, HEADS)), taps], axis=1)
    arrays = {
        "tokens": tokens,
        "cond": np.stack([c[0], c_ctx]),
        "vecs": vecs,
        "consts": _constants(),
        "wmod": w_mod.transpose(0, 2, 1).reshape(2 * MODT, P, D),
        "wstream": _stream(ffn_w_in, ffn_w_out, ab_w_in[0], ab_w_out[0], c_w_dq[0], c_w_uq[0], c_w_dkv[0], c_w_uk[0],
                           c_w_uv[0], c_w_o[0]),
    }
    arrays = {k: np.ascontiguousarray(a) for k, a in arrays.items()}
    nc = bacc.Bacc("TRN2", target_bir_lowering=False, num_devices=1)
    args = [nc.dram_tensor(k, a.shape, mybir.dt.from_np(a.dtype), kind="ExternalInput").ap()
            for k, a in arrays.items()]
    out = nc.dram_tensor("out", [P, DT, LAT], mybir.dt.float32, kind="ExternalOutput").ap()
    build(nc, *args, out)
    result = run_bass_kernel_spmd(nc, [arrays], core_ids=[0]).results[0]["out"]
    return np.ascontiguousarray(result.transpose(2, 1, 0).reshape(LAT, D))[None]
```

```python
from contextlib import ExitStack

import numpy as np

import concourse.bass as bass
from concourse import mybir

P = 128
D = 1024
DT = D // P
LAT, CTX = 256, 256
TOK = LAT + CTX
D_FF = 2816
GROUPS = (8, 8, 6)
SLAB = 2048
HALF = SLAB // 2
HEADS = 8
A_DIM, A_KV, B_CH, TAPS = 64, 2, 512, 31
CT = B_CH // P
PAD = TAPS // 2
NOPE, ROPE, C_V, LORA = 128, 64, 128, 256
N_MOD = 9
MODT = N_MOD * DT
GRID_W = 64
NORM_EPS, LN_EPS = 1e-6, 1e-5
NEG = -1e30

FFN_SLABS = sum(g + 4 for g in GROUPS)
W_FFN0 = 0
W_AB = W_FFN0 + FFN_SLABS
W_FFN1 = W_AB + 7 + 4
W_FFN2 = W_FFN1 + FFN_SLABS
W_MLA = W_FFN2 + FFN_SLABS
W_FFN3 = W_MLA + 6 + 4
N_SLABS = W_FFN3 + FFN_SLABS
FFN_W = (W_FFN0, W_FFN1, W_FFN2, W_FFN3)
FFN_STEPS = sum(GROUPS)
FFN_OUTS = 4 * len(GROUPS)
B_FFN = (0, FFN_OUTS + 4, 2 * FFN_OUTS + 4, 3 * FFN_OUTS + 8)
B_AB = FFN_OUTS
B_MLA = 3 * FFN_OUTS + 4

MOD_FIRST = 2 * DT
MOD_STEPS = FFN_SLABS - 4
MOD_PHASES = ((0, 1, 2, 3, 4), (0, 1, 2, 3, 4), (1,), ())

NORMS = ("ffn0", "ab", "ln", "ffn1", "ffn2", "mla", "cq", "ckv", "ffn3", "final")
NORM_TILES = {"ln": 4, "cq": 2, "ckv": 2}
CALL = {n: i for i, n in enumerate(NORMS)}
NORM_BASE = {}
_n = 0
for _name in NORMS:
    NORM_BASE[_name] = _n
    _n += NORM_TILES.get(_name, DT)
RES = {"ffn0": 0, "ab": 1, "ffn1": 2, "ffn2": 3, "mla": 4, "ffn3": 5, "final": 6}

V_G, V_BMOD, V_GF = 0, 48, 48 + 2 * MODT
V_BDW = V_GF + DT
V_LNG = V_BDW + CT
V_LNB = V_LNG + CT
V_GQ = V_LNB + CT
V_GKV = V_GQ + 2
V_SINK = V_GKV + 2
V_WDW = V_SINK + HEADS
N_VEC = V_WDW + CT * TAPS
C_ID, C_MASK, C_COS, C_SIN = 0, P, 3 * P, 3 * P + LAT
N_CONST = C_SIN + LAT


def build(nc, tokens, cond, cond_cols, vecs, consts, wmod, wstream, out):
    F32, F32R, I32 = mybir.dt.float32, mybir.dt.float32r, mybir.dt.int32
    ALU, ACT, AX = mybir.AluOpType, mybir.ActivationFunctionType, mybir.AxisListType
    ds = bass.ds

    with ExitStack() as ctx:
        def sb(name, shape, dt=F32, where=ctx):
            return where.enter_context(nc.sbuf_tensor(name, shape, dt))

        def sem(name):
            return ctx.enter_context(nc.semaphore(name))

        xT = sb("xT", [P, DT, TOK])
        a_hi = sb("a_hi", [P, DT, TOK], F32R)
        a_lo = sb("a_lo", [P, DT, TOK], F32R)
        h_hi = sb("h_hi", [P, 8, TOK], F32R)
        h_lo = sb("h_lo", [P, 8, TOK], F32R)
        raw = sb("raw", [P, 2, SLAB])
        w_hi = sb("w_hi", [P, 2, SLAB], F32R)
        w_lo = sb("w_lo", [P, 2, SLAB], F32R)
        spare = sb("spare", [P, 2048])
        work = sb("work", [P, 4, TOK])
        with ExitStack() as norms:
            sq = sb("sq", [P, 2, TOK], where=norms)
            ss = sb("ss", [P, 2, TOK], where=norms)
        pt_hi1 = sb("pt_hi1", [P, 2, TOK], F32R)
        pt_lo1 = sb("pt_lo1", [P, 2, TOK], F32R)
        diag = sb("diag", [P, 4, P])
        rdiag = sb("rdiag", [P, 2, 2, P])
        ones = sb("ones", [P, P])
        cst = sb("cst", [P, N_CONST])
        ident_r = sb("ident_r", [P, P], F32R)
        mask_r = sb("mask_r", [P, 2, P], F32R)
        vec = sb("vec", [P, N_VEC])
        modc = sb("modc", [P, 2, 2 * MODT])
        stage = sb("stage", [P, 2, 4])
        ccol = sb("ccol", [P, DT, 2])
        shift = sb("shift", [P, 6, 2, DT])
        scale = sb("scale", [P, 6, 2, DT])
        gate = sb("gate", [P, 6, 2, DT])
        mtmp = sb("mtmp", [P, 2, DT])
        nsink = sb("nsink", [P, HEADS])
        smax = sb("smax", [P, 32])
        nmax = sb("nmax", [P, 32])
        den = sb("den", [P, 32])
        esink = sb("esink", [P, 32])
        rinv = sb("rinv", [P, 32])
        rv = sb("rv", [P, 4])
        ri = sb("ri", [P, 4], I32)
        ry = sb("ry", [P, 4])
        rt = sb("rt", [P, 4])
        tick = sb("tick", [P, N_SLABS - W_FFN3])
        with ExitStack() as first:
            mring = sb("mring", [P, 4, D], where=first)
            cb = sb("cb", [P, 2, D], where=first)
            unread = sb("unread", [P, D], mybir.dt.bfloat16, where=first)
            ypad = sb("ypad", [P, CT, 2, LAT + 2 * PAD], where=first)
        q_hi = sb("q_hi", [P, 7, TOK], F32R)
        q_lo = sb("q_lo", [P, 7, TOK], F32R)
        l_hi = sb("l_hi", [P, 3, TOK], F32R)
        l_lo = sb("l_lo", [P, 3, TOK], F32R)
        conv = spare[:].rearrange("p (c n) -> p c n", c=CT)
        ident = cst[:, C_ID:C_ID + P]
        cos, sin = cst[:, C_COS:C_COS + LAT], cst[:, C_SIN:C_SIN + LAT]
        xn, full = work[:, 0:2], work[:, 2:4]
        sil, prod = work[:, 0:2], work[:, 2:4]
        probs = work[:, 0:3]
        v_rows = work[:, 0]
        AB_PT = [(x[:, 4:6], x[:, 6:8]) for x in (a_hi, a_lo)]
        MLA_PT = [(l_hi[:, 0:2], pt_hi1[:]), (l_lo[:, 0:2], pt_lo1[:])]
        ps = [ctx.enter_context(nc.psum_tensor(f"ps{i}", [P, 512], F32)) for i in range(8)]
        OUTB = 4
        S_BANK, PT_BANK, O_BANK, LN_BANK, NORM_BANK = (1, 4, 5), (6, 7), (0, 3), 2, 6

        in_tok = sem("in_tok")
        in_cond = sem("in_cond")
        in_rows = sem("in_rows")
        in_small = sem("in_small")
        raw_loaded = [sem(f"raw_loaded{i}") for i in range(2)]
        hi_ready = sem("hi_ready")
        lo_ready = sem("lo_ready")
        lo2_ready = sem("lo2_ready")
        both_split = sem("both_split")
        slab_done = sem("slab_done")
        mod_loaded = [sem(f"mod_loaded{i}") for i in range(4)]
        mod_first = sem("mod_first")
        mod_dots = sem("mod_dots")
        mod_cols = sem("mod_cols")
        mod_rows = sem("mod_rows")
        mod_turned = sem("mod_turned")
        cond_ready = sem("cond_ready")
        gp_const = sem("gp_const")
        act_const = sem("act_const")
        chain = sem("chain")
        sq_ready = [sem(f"sq_ready{i}") for i in range(2)]
        ss_sum = [sem(f"ss_sum{i}") for i in range(2)]
        colsum = sem("colsum")
        diag_ready = sem("diag_ready")
        rstd_bc = sem("rstd_bc")
        xn_ready = sem("xn_ready")
        nhi_ready = sem("nhi_ready")
        normed = sem("normed")
        pair_free = sem("pair_free")
        sil_ready = sem("sil_ready")
        hhi_ready = sem("hhi_ready")
        hid_ready = sem("hid_ready")
        tile0_done = sem("tile0_done")
        out_free = [sem(f"out_free{i}") for i in range(2)]
        glu_sig = sem("glu_sig")
        glu_done = sem("glu_done")
        conv_op = sem("conv_op")
        tap_first = sem("tap_first")
        tap_prod = sem("tap_prod")
        tap_add = sem("tap_add")
        step_done = sem("step_done")
        rope_ctx = sem("rope_ctx")
        rope_full = sem("rope_full")
        piece_hi = sem("piece_hi")
        piece_lo = sem("piece_lo")
        scores_done = sem("scores_done")
        nmax_ready = sem("nmax_ready")
        exp_done = sem("exp_done")
        sink_done = sem("sink_done")
        pt_done = sem("pt_done")
        pt_hi = sem("pt_hi")
        pt_lo = sem("pt_lo")
        pv_done = sem("pv_done")
        rdiag_ready = sem("rdiag_ready")
        v_copy = sem("v_copy")
        ot_hi = sem("ot_hi")
        ot_lo = sem("ot_lo")
        ln_sum = sem("ln_sum")
        ln_mean = sem("ln_mean")
        ln_cent = sem("ln_cent")
        stat_sq = sem("stat_sq")
        stat_add = sem("stat_add")
        stat_ready = sem("stat_ready")
        lat_copy = sem("lat_copy")
        y_ready = sem("y_ready")
        stored = sem("stored")

        OWN_TAPS = 12
        CONV_ADDS = 2 * TAPS - 1 - OWN_TAPS
        ADDS_AFTER = (0, 0, 4, 8, 12, 16, 20, 20)
        TAPS_AFTER = (0, 13, 26, 40, 55)
        TAPS_PIECE = (6, 0, 0, 0)

        def turns(*tiles):
            return [taps[n] for n in range(max(map(len, tiles))) for taps in tiles if n < len(taps)]

        def tile_taps(c, first=0, last=TAPS):
            return [(c, tap) for tap in range(first, last)]
        OWN = tile_taps(0, 0, 26) + turns(tile_taps(0, 26), tile_taps(2, 0, 9)) \
            + turns(tile_taps(2, 9), tile_taps(3, 0, OWN_TAPS))
        CONV_OPS = len(OWN)
        OWN_AFTER = [OWN.index((c, tap - 1)) + 1 if tap else 0 for c, tap in OWN]

        def add_tap(n):
            return (1, n + 1) if n < TAPS - 1 else (3, n - (TAPS - 1) + OWN_TAPS)

        def tap_slot(n):
            return (ss[:, 0], ss[:, 1], diag[:].rearrange("p a n -> p (a n)"))[n % 3]

        def cols(hi, lo, i, a=0, b=TOK):
            return hi[:, i, a:b], lo[:, i, a:b]

        AB_PIECES = [(ps[0], *cols(h_hi, h_lo, 4), ((0, LAT),), (step_done, 1))]
        for t in range(2):
            AB_PIECES.append((ps[2 + t], *cols(h_hi, h_lo, t), ((0, LAT),), (slab_done, W_AB + 6)))
        AB_PIECES.append((ps[6], *cols(h_hi, h_lo, 5), (), (step_done, 2)))
        for t in range(2):
            AB_PIECES.append((ps[7 * t], *cols(h_hi, h_lo, 2 + t), ((0, LAT),), (slab_done, W_AB + 7)))
        AB_EARLY = 4
        MLA_STEPS = [[("kr", 0)], [("q", 0), ("q", 1)], [("q", 2), ("q", 3)], [("q", 4), ("q", 5)]]
        MLA_STEPS += [[("kn", 2 * i), ("kn", 2 * i + 1)] for i in range(4)]
        MLA_STEPS += [[("v", 2 * i), ("v", 2 * i + 1)] for i in range(4)]
        MLA_SIGNAL, n_step = [], 2
        for i in range(len(MLA_STEPS)):
            ends = {1: W_MLA + 3, 3: W_MLA + 4, 7: W_MLA + 5, 11: W_MLA + 6}.get(i)
            if ends is None:
                n_step += 1
                MLA_SIGNAL.append((step_done, n_step))
            else:
                MLA_SIGNAL.append((slab_done, ends))
        MLA_PIECES, MLA_PIECES_BY = [], []
        for i, parts in enumerate(MLA_STEPS):
            for t, (kind, n) in enumerate(parts):
                bank = ps[2 * (i % 2) + t]
                if kind == "kr":
                    piece = (bank, *cols(q_hi, q_lo, 6), ((0, LAT),), MLA_SIGNAL[i])
                elif kind == "q":
                    piece = (bank, *cols(q_hi, q_lo, n), ((0, LAT), (LAT, TOK)) if n >= 4 else (), MLA_SIGNAL[i])
                elif kind == "kn":
                    piece = (bank, *cols(a_hi, a_lo, n), (), MLA_SIGNAL[i])
                else:
                    piece = (bank, *cols(h_hi, h_lo, n), (), MLA_SIGNAL[i])
                MLA_PIECES.append(piece)
            MLA_PIECES_BY.append(len(AB_PIECES) + len(MLA_PIECES))
        N_AB = len(AB_PIECES)
        ROPE_INDEX = {}
        CTX_INDEX = {}
        for j, p in enumerate(AB_PIECES + MLA_PIECES):
            if p[3]:
                ROPE_INDEX[j] = len(ROPE_INDEX)
                if len(p[3]) == 1:
                    CTX_INDEX[j] = len(CTX_INDEX)

        def units(order):
            found, at = [], 0
            for h, qts in order:
                found.append((h, qts, at))
                at += len(qts)
            return found

        LATE = HEADS // 2
        AB_UNITS = units([(h, qts) for t in range(LATE) for qts in (((0, 0),), ((1, 0),), ((2, LAT), (3, LAT)))
                          for h in (t, t + LATE)])
        MLA_UNITS = units([(h, ((qt, 0),)) for h in range(HEADS) for qt in range(2)])
        AB_PAIRS = len(AB_UNITS) // 2
        LN_UNIT = 15

        def spans(qts):
            n = TOK // len(qts)
            return [(qt, key0, i * n, n) for i, (qt, key0) in enumerate(qts)]

        def pt_unit(buf, e, qts):
            pair = buf[e // 2 % 2].rearrange("p a n -> p (a n)")
            return pair.rearrange("p (k u n) -> p k u n", u=2, n=len(qts) * P)[:, :, e % 2]

        def pt_bank(e, qts):
            return ps[PT_BANK[e % 2]][:].rearrange("p (k n) -> p k n", n=len(qts) * P)

        def ab_out(buf, p):
            c, which = p // 3, p % 3
            n = P if which < 2 else 2 * P
            return [(slice(A_DIM * u, A_DIM * (u + 1)), slice(u * n, (u + 1) * n),
                     buf[A_DIM * u:A_DIM * (u + 1), c, which * P:which * P + n]) for u in range(2)]

        def mla_out(buf, p):
            return [(slice(0, P), slice(0, LAT), buf[:, p, 0:LAT])]

        block = ctx.enter_context(nc.Block())

        @block.sync
        def _(sp):
            def slab(w, slot, wait=None):
                if wait is not None:
                    sp.wait_ge(lo_ready, wait)
                sp.dma_start(raw[:, slot], wstream[ds(w, 1)].rearrange("a p n -> p (a n)")) \
                  .then_inc(raw_loaded[slot], 16)

            def mod_tile(n, slot, wait=None):
                if wait is not None:
                    sp.wait_ge(mod_dots, wait)
                sp.dma_start(mring[:, slot], wmod[ds(n, 1)].rearrange("a p n -> p (a n)")) \
                  .then_inc(mod_loaded[slot], 16)

            sp.dma_start(ccol[:], cond_cols).then_inc(in_cond, 16)
            for n in range(4):
                mod_tile(n, n)
            sp.dma_start(xT[:], tokens).then_inc(in_tok, 16)
            sp.dma_start(cst[:], consts).then_inc(in_small, 16)
            sp.dma_start(vec[:], vecs).then_inc(in_small, 16)
            for n in range(4, MOD_FIRST):
                mod_tile(n, n % 4, n - 3)
                if n == MOD_FIRST - 5:
                    slab(0, 0)
            slab(1, 1)
            sp.dma_start(cb[:], cond.partition_broadcast(P)).then_inc(in_rows, 16)
            for w in range(2, 4):
                slab(w, w % 2, w - 1)
            for j in range(4):
                mod_tile(MOD_FIRST + j, j, MOD_FIRST + j - 3)

            def plain(w0, w2):
                for w in range(w0, w2):
                    slab(w, w % 2, w - 1)

            def both(w0, n0, turns):
                with sp.Fori(0, turns) as i:
                    for j in range(2):
                        for k in range(2):
                            n = i * 4 + (n0 + 2 * j + k)
                            mod_tile(n, 2 * j + k, n - 3)
                        w = i * 2 + (w0 + j)
                        slab(w, (w0 + j) % 2, w - 1)

            both(4, MOD_FIRST + 4, MOD_STEPS // 2 - 1)
            plain(W_FFN0 + 2 + MOD_STEPS, W_FFN1 + 4)
            n0 = MOD_FIRST + 2 * MOD_STEPS
            for j in range(4):
                mod_tile(n0 + j, j, n0 + j - 3)
            both(W_FFN1 + 4, n0 + 4, MOD_STEPS // 2 - 1)
            plain(W_FFN1 + 2 + MOD_STEPS, W_FFN2 + 2 + GROUPS[0])
            n0 += 2 * MOD_STEPS
            for j in range(4):
                mod_tile(n0 + j, j, n0 + j - 3)
            plain(W_FFN2 + 2 + GROUPS[0], W_FFN2 + 4 + GROUPS[0])
            for j in range(2):
                for k in range(2):
                    n = n0 + 4 + 2 * j + k
                    mod_tile(n, 2 * j + k, n - 3)
                plain(W_FFN2 + 4 + GROUPS[0] + j, W_FFN2 + 5 + GROUPS[0] + j)
            w1 = W_FFN2 + 6 + GROUPS[0]
            assert n0 + 8 == 2 * MODT

            def only(w0, w2, last_ffn=False):
                with sp.Fori(w0, w2 - 1, 2) as w:
                    for j in range(2):
                        if last_ffn:
                            sp.wait_ge(both_split, w + (j - 1 - W_FFN3))
                            slab(w + j, (w0 + j) % 2)
                        else:
                            slab(w + j, (w0 + j) % 2, w + (j - 1))

            assert (w1 - W_FFN3) % 2 == 0
            only(w1, W_FFN3 + 2)
            only(W_FFN3 + 2, N_SLABS, True)
            for k in range(DT):
                sp.wait_ge(y_ready, k + 1)
                sp.dma_start(out[:, k], spare[:, k * LAT:(k + 1) * LAT]).then_inc(stored, 16)
            sp.wait_ge(stored, 16 * DT)

        @block.gpsimd
        def _(pool):
            pool.memset(ones[:], 1.0).then_inc(gp_const, 1)
            pool.memset(ypad[:], 0.0).then_inc(gp_const, 1)

            def split_lo(w, slot, width=SLAB):
                pool.wait_ge(hi_ready, w + 1)
                pool.tensor_tensor(w_lo[:, slot, 0:width], raw[:, slot, 0:width],
                                   w_hi[:, slot, 0:width].bitcast(F32), ALU.subtract).then_inc(lo_ready, 1)

            def add_taps(first, last):
                for n in range(first, last):
                    c, tap = add_tap(n)
                    if n == 0:
                        pool.wait_ge(tap_first, 1)
                    if n == TAPS - 1:
                        pool.wait_ge(conv_op, OWN.index((3, OWN_TAPS - 1)) + 1)
                    pool.wait_ge(tap_prod, n + 1)
                    if n >= 1:
                        pool.wait_ge(tap_add, n)
                    pool.tensor_tensor(conv[:, c], conv[:, c], tap_slot(n), ALU.add).then_inc(tap_add, 1)

            def loop(first, end):
                with pool.Fori(first, end - 1, 2) as w:
                    for j in range(2):
                        split_lo(w + j, (first + j) % 2)

            loop(0, W_AB + 2)
            for c in range(7):
                split_lo(W_AB + 2 + c, (W_AB + c) % 2)
                add_taps(ADDS_AFTER[c], ADDS_AFTER[c + 1])
            add_taps(ADDS_AFTER[7], CONV_ADDS)
            loop(W_AB + 9, W_FFN3)
            with pool.Fori(W_FFN3, N_SLABS - 1, 2) as w:
                for j in range(2):
                    split_lo(w + j, (W_FFN3 + j) % 2, HALF)
                    pool.wait_ge(lo2_ready, w + (j + 1 - W_FFN3))
                    pool.tensor_tensor(tick[:, ds(w + (j - W_FFN3), 1)], ones[:, 0:1], ones[:, 0:1],
                                       ALU.add).then_inc(both_split, 1)

        @block.scalar
        def _(act):
            def split_hi(w, slot, base, i=None):
                value = 16 * (base // 2 + 1)
                act.wait_ge(raw_loaded[slot], value if i is None else i * 16 + value)
                act.activation(w_hi[:, slot], raw[:, slot], ACT.Copy).then_inc(hi_ready, 1)

            def squares(n, sl, t, nt, i=None):
                k = sl if i is None else i + sl
                act.wait_ge(ss_sum[t], k + (5 * n + 1 if t else 4 * n))
                m = 2 * sl + t if i is None else i * 2 + (2 * sl + t)
                src = xT[:, m, 0:nt] if i is None else xT[:, ds(m, 1), 0:nt].rearrange("p a n -> p (a n)")
                act.activation(sq[:, t, 0:nt], src, ACT.Square).then_inc(sq_ready[t], 1)

            def norm_apply(name, tiles, emit):
                base = NORM_BASE[name]
                for k in range(tiles):
                    act.wait_ge(xn_ready, base + k + 1)
                    if k >= 2:
                        act.wait_ge(normed, base + k - 1)
                    emit(k)

            def modulated(name, s, nt):
                streams = nt // LAT

                def emit(k):
                    for dst, those in ((full[:, k % 2], 1), (a_hi[:, k], streams)):
                        for v in range(those):
                            c = slice(v * LAT, (v + 1) * LAT)
                            last = act.activation(dst[:, c], xn[:, k % 2, c], ACT.Identity,
                                                  bias=shift[:, s, v, k:k + 1], scale=scale[:, s, v, k:k + 1])
                    last.then_inc(nhi_ready, 1)
                norm_apply(name, DT, emit)

            def ffn(s, name, nt, next_norm, after_norm=None):
                modulated(name, (0, 2, 3, 5)[s], nt)
                if after_norm is not None:
                    after_norm()
                w, f, b = FFN_W[s], s * FFN_STEPS, B_FFN[s]
                for g, size in enumerate(GROUPS):
                    with act.Fori(0, size - 1, 2) as i:
                        for j in range(2):
                            act.wait_ge(slab_done, i + (w + j + 1))
                            act.wait_ge(raw_loaded[(w + j) % 2], i * 8 + 16 * ((w + j + 2) // 2 + 1))
                            act.activation(w_hi[:, (w + j) % 2], raw[:, (w + j) % 2],
                                           ACT.Copy).then_inc(hi_ready, 1)
                            act.activation(sil[:, (f + j) % 2, 0:nt], ps[2 * ((f + j) % 2)][:, 0:nt],
                                           ACT.Silu).then_inc(sil_ready, 1)
                            act.wait_ge(pair_free, i + (f + j + 3))
                            act.activation(h_hi[:, ds(i + j, 1), 0:nt].rearrange("p a n -> p (a n)"),
                                           prod[:, (f + j) % 2, 0:nt], ACT.Copy).then_inc(hhi_ready, 1)
                    w, f = w + size, f + size
                    last = g == len(GROUPS) - 1

                    def out_step(j, i=None, split=True):
                        k = (lambda x: x) if i is None else (lambda x: i + x)
                        if last:
                            act.wait_ge(out_free[0], k(b + j + 3))
                            squares(RES[next_norm], j, 0, nt, i)
                        if split:
                            act.wait_ge(slab_done, k(w + j + 1))
                            value = 16 * ((w + j + 2) // 2 + 1)
                            act.wait_ge(raw_loaded[(w + j) % 2], value if i is None else i * 8 + value)
                            act.activation(w_hi[:, (w + j) % 2], raw[:, (w + j) % 2],
                                           ACT.Copy).then_inc(hi_ready, 1)
                        if last:
                            act.wait_ge(out_free[1], k(b + j + 3))
                            squares(RES[next_norm], j, 1, nt, i)
                    if w + 4 == N_SLABS:
                        for j in range(4):
                            out_step(j, split=j < 2)
                    else:
                        with act.Fori(0, 3, 2) as i:
                            for j in range(2):
                                out_step(j, i)
                    w, b = w + 4, b + 4

            def pieces(j, piece, base_wait=None):
                src, hi, _, runs, (s, value) = piece
                act.wait_ge(s, value)
                if runs:
                    r = ROPE_INDEX[j]
                    if len(runs) == 1:
                        if j >= 2:
                            act.wait_ge(piece_lo, j - 1)
                        act.activation(full[:, r % 2, LAT:TOK], src[:, LAT:TOK], ACT.Copy).then_inc(rope_ctx, 1)
                    act.wait_ge(rope_full, r + 1)
                    act.activation(hi, full[:, r % 2], ACT.Copy).then_inc(piece_hi, 1)
                else:
                    act.activation(hi, src[:], ACT.Copy).then_inc(piece_hi, 1)

            def attention(units, u0, sink, factor, pt_hi_buf, out_to, beside=None):
                for i in range(len(units) + 5):
                    if i < len(units):
                        h, qts, at = units[i]
                        u = u0 + i
                        act.wait_ge(nmax_ready, u + 1)
                        if i >= 3:
                            act.wait_ge(pt_done, u - 2)
                        for n, (_, _, c0, width) in enumerate(spans(qts)):
                            last = act.activation(probs[:, i % 3, c0:c0 + width], ps[S_BANK[i % 3]][:, c0:c0 + width],
                                                  ACT.Exp, bias=nmax[:, at + n:at + n + 1], scale=factor,
                                                  accum_out=den[:, at + n:at + n + 1])
                        last.then_inc(exp_done, 1)
                        if sink:
                            act.activation(esink[:, at:at + len(qts)], nmax[:, at:at + len(qts)], ACT.Exp,
                                           bias=vec[:, V_SINK + h:V_SINK + h + 1]).then_inc(sink_done, 1)
                    if beside is not None and i < len(units):
                        beside(i)
                    if 2 <= i < len(units) + 2:
                        e = i - 2
                        act.wait_ge(pt_done, u0 + e + 1)
                        if e >= 4:
                            act.wait_ge(pv_done, u0 // 2 + e // 2 - 1)
                        act.activation(pt_unit(pt_hi_buf, e, units[e][1]), pt_bank(e, units[e][1]),
                                       ACT.Copy).then_inc(pt_hi, 1)
                    if i >= 6 and i % 2 == 0:
                        p = (i - 6) // 2
                        act.wait_ge(pv_done, u0 // 2 + p + 1)
                        for rows, c, dst in out_to(a_hi, p):
                            last = act.activation(dst, ps[O_BANK[p % 2]][rows, c], ACT.Copy)
                        last.then_inc(ot_hi, 1)

            def mixer_out(w, b, nt, next_norm):
                for j in range(4):
                    for t in range(2):
                        act.wait_ge(out_free[t], b + j + 3)
                        squares(RES[next_norm], j, t, nt)
                    act.wait_ge(slab_done, w + j + 1)
                    split_hi(w + j + 2, (w + j) % 2, w + j + 2)

            act.wait_ge(in_cond, 16)
            act.activation(ccol[:], ccol[:], ACT.Silu).then_inc(cond_ready, 1)
            act.wait_ge(in_tok, 16)
            for sl in range(4):
                for t in range(2):
                    squares(0, sl, t, TOK)
            act.wait_ge(in_small, 32)
            act.activation(ident_r[:], ident, ACT.Copy).then_inc(act_const, 1)
            act.activation(mask_r[:], cst[:, C_MASK:C_MASK + 2 * P].rearrange("p (a n) -> p a n", a=2),
                           ACT.Copy).then_inc(act_const, 1)
            split_hi(0, 0, 0)
            split_hi(1, 1, 1)
            ffn(0, "ffn0", TOK, "ab", lambda: (
                act.wait_ge(in_rows, 16),
                act.activation(cb[:], cb[:], ACT.Silu).then_inc(cond_ready, 1)))

            modulated("ab", 1, TOK)
            def tap_products(first, last):
                for n in range(first, last):
                    c, tap = add_tap(n)
                    if n >= 3:
                        act.wait_ge(tap_add, n - 2)
                    act.activation(tap_slot(n).rearrange("p (v n) -> p v n", v=2), ypad[:, c, :, tap:tap + LAT],
                                   ACT.Copy, scale=vec[:, V_WDW + c * TAPS + tap:V_WDW + c * TAPS + tap + 1]) \
                       .then_inc(tap_prod, 1)

            w = W_AB
            for c in range(CT):
                act.wait_ge(slab_done, w + c + 1)
                split_hi(w + c + 2, (w + c) % 2, w + c + 2)
                if c >= 2:
                    act.wait_ge(glu_done, c - 1)
                act.activation(sil[:, c % 2], ps[2 * (c % 2) + 1][:], ACT.Sigmoid).then_inc(glu_sig, 1)
                if c == 1:
                    act.wait_ge(glu_done, c + 1)
                    act.wait_ge(normed, NORM_BASE["ab"] + DT)
                    act.activation(conv[:, c].rearrange("p (v n) -> p v n", v=2), ypad[:, c, :, 0:LAT], ACT.Identity,
                                   bias=vec[:, V_BDW + c:V_BDW + c + 1],
                                   scale=vec[:, V_WDW + c * TAPS:V_WDW + c * TAPS + 1]).then_inc(tap_first, 1)
                tap_products(ADDS_AFTER[c], ADDS_AFTER[c + 1])
            for x in (w + 4, w + 5):
                act.wait_ge(slab_done, x + 1)
                split_hi(x + 2, x % 2, x + 2)
                if x == w + 4:
                    act.wait_ge(glu_done, 3)
                    act.activation(v_rows, ps[1][:], ACT.Copy).then_inc(v_copy, 1)
                    pieces(0, AB_PIECES[0])
                    tap_products(ADDS_AFTER[4], ADDS_AFTER[5])
                else:
                    for j in range(1, AB_EARLY):
                        pieces(j, AB_PIECES[j])
                    tap_products(ADDS_AFTER[5], ADDS_AFTER[6])

            def ab_beside(i):
                if i < 2:
                    pieces(AB_EARLY + i, AB_PIECES[AB_EARLY + i])
                if i == 0:
                    split_hi(w + 8, (w + 6) % 2, w + 8)
                if i == 1:
                    act.wait_ge(piece_lo, N_AB)
                n = ADDS_AFTER[7] + 2 * i
                if n < CONV_ADDS:
                    tap_products(n, min(n + 2, CONV_ADDS))
                if i in (LN_UNIT + 3, LN_UNIT + 4):
                    for c in (0, 1) if i == LN_UNIT + 3 else (2, 3):
                        act.wait_ge(ln_cent, c + 1)
                        if c >= 2:
                            act.wait_ge(stat_add, 1)
                        act.activation(sq[:, c % 2], conv[:, c], ACT.Square).then_inc(stat_sq, 1)
            attention(AB_UNITS, 0, True, A_DIM ** -0.5, AB_PT[0], ab_out, ab_beside)

            def ln_emit(k):
                for dst in (full[:, k % 2], a_hi[:, 4 + k]):
                    last = act.activation(dst, xn[:, k % 2], ACT.Silu, bias=vec[:, V_LNB + k:V_LNB + k + 1],
                                          scale=vec[:, V_LNG + k:V_LNG + k + 1])
                last.then_inc(nhi_ready, 1)
            norm_apply("ln", CT, ln_emit)
            mixer_out(W_AB + 7, B_AB, TOK, "ffn1")

            ffn(1, "ffn1", TOK, "ffn2")
            ffn(2, "ffn2", TOK, "mla")

            modulated("mla", 4, TOK)
            w = W_MLA
            for i, nt in ((0, LAT), (1, TOK)):
                act.wait_ge(slab_done, w + i + 1)
                for t in range(2):
                    dst = spare[:, t * LAT:(t + 1) * LAT] if i == 0 else spare[:, (1 + t) * TOK:(2 + t) * TOK]
                    act.activation(dst, ps[2 * i + t][:, 0:nt], ACT.Copy).then_inc(lat_copy, 1)
                    if i:
                        act.wait_ge(stat_ready, 1)
                    act.activation(sq[:, t, 0:nt], ps[2 * i + t][:, 0:nt], ACT.Square).then_inc(stat_sq, 1)
                split_hi(w + i + 2, (w + i) % 2, w + i + 2)

            def lora_emit(g, nt, dst):
                def emit(k):
                    gcol = vec[:, g + k:g + k + 1]
                    act.activation(full[:, k % 2, 0:nt], xn[:, k % 2, 0:nt], ACT.Copy, scale=gcol)
                    act.activation(dst(k), xn[:, k % 2, 0:nt], ACT.Copy, scale=gcol).then_inc(nhi_ready, 1)
                return emit
            norm_apply("cq", 2, lora_emit(V_GQ, LAT, lambda k: l_hi[:, 0, k * LAT:(k + 1) * LAT]))
            norm_apply("ckv", 2, lora_emit(V_GKV, TOK, lambda k: l_hi[:, 1 + k]))
            act.wait_ge(normed, NORM_BASE["ckv"] + 2)
            j = N_AB
            for i, parts in enumerate(MLA_STEPS):
                for _ in parts:
                    pieces(j, MLA_PIECES[j - N_AB])
                    j += 1
                if MLA_SIGNAL[i][0] is slab_done:
                    x = MLA_SIGNAL[i][1] - 1
                    split_hi(x + 2, x % 2, x + 2)
            attention(MLA_UNITS, len(AB_UNITS), False, (NOPE + ROPE) ** -0.5, MLA_PT[0], mla_out)
            mixer_out(W_MLA + 6, B_MLA, LAT, "ffn3")

            ffn(3, "ffn3", LAT, "final")
            base = NORM_BASE["final"]
            for k in range(DT):
                act.wait_ge(xn_ready, base + k + 1)
                act.activation(spare[:, k * LAT:(k + 1) * LAT], xn[:, k % 2, 0:LAT], ACT.Copy,
                               scale=vec[:, V_GF + k:V_GF + k + 1]).then_inc(y_ready, 1)

        @block.vector
        def _(dve):
            count = [0]

            def link(ins):
                count[0] += 1
                ins.then_inc(chain, 1)
                dve.wait_ge(chain, count[0])

            def mod_dot(slot, value, n):
                dve.wait_ge(mod_loaded[slot], value)
                dve.wait_ge(mod_first, n + 1)
                dve.tensor_tensor_reduce(unread[:], mring[:, slot], cb[:, 0], 1.0, 0.0,
                                         ALU.mult, ALU.add, stage[:, 0, slot:slot + 1]).then_inc(mod_first, 1)
                dve.tensor_tensor_reduce(mring[:, slot], mring[:, slot], cb[:, 1], 1.0, 0.0, ALU.mult, ALU.add,
                                         stage[:, 1, slot:slot + 1]).then_inc(mod_dots, 1)

            def mod_store(n, done):
                dve.wait_ge(mod_dots, done)
                dve.tensor_copy(modc[:, :, ds(n, 4)], stage[:]).then_inc(mod_cols, 4)
                dve.wait_ge(mod_cols, done)

            def finalize(layer, place, parts=("shift", "scale", "gate")):
                s = 3 * layer + place
                base = layer * MODT + place * 3 * DT

                def summed(dst, c):
                    b = vec[:, V_BMOD + base + c * DT:V_BMOD + base + (c + 1) * DT]
                    return dve.tensor_tensor(dst, modc[:, :, base + c * DT:base + (c + 1) * DT],
                                             b.unsqueeze(1).to_broadcast([P, 2, DT]), ALU.add)
                if "shift" in parts:
                    link(summed(shift[:, s], 0))
                if "scale" in parts:
                    link(summed(mtmp[:], 1))
                    g = vec[:, V_G + s * DT:V_G + (s + 1) * DT].unsqueeze(1).to_broadcast([P, 2, DT])
                    link(dve.scalar_tensor_tensor(out=scale[:, s], in0=mtmp[:], scalar=1.0, in1=g,
                                                  op0=ALU.add, op1=ALU.mult))
                if "gate" in parts:
                    link(summed(mtmp[:], 2))
                    link(dve.tensor_scalar(gate[:, s], mtmp[:], 1.0 if place == 1 else 0.5, None, ALU.mult))

            def zero_sum(n):
                dve.memset(ss[:, 0], 0.0).then_inc(ss_sum[1], 1)

            def add_square(n, sl, t, nt, i=None):
                k = (lambda x: x) if i is None else (lambda x: i + x)
                dve.wait_ge(sq_ready[t], k(4 * n + sl + 1))
                if t:
                    dve.wait_ge(ss_sum[0], k(4 * n + sl + 1))
                else:
                    dve.wait_ge(ss_sum[1], k(5 * n + sl + 1))
                dve.tensor_tensor(ss[:, 0, 0:nt], ss[:, 0, 0:nt], sq[:, t, 0:nt], ALU.add).then_inc(ss_sum[t], 1)

            def rsqrt(name, bank, nt, inv_n, eps):
                c = nt // P
                dve.wait_ge(colsum, CALL[name] + 1)
                link(dve.tensor_scalar(rv[:, 0:c], ps[bank][:, 0:c], inv_n, eps, ALU.mult, ALU.add))
                link(dve.tensor_scalar(ri[:, 0:c], rv[:, 0:c].bitcast(I32), 1, None, ALU.logical_shift_right))
                link(dve.tensor_scalar(ri[:, 0:c], ri[:, 0:c], -1.0, float(0x5F3759DF), ALU.mult, ALU.add))
                y = ri[:, 0:c].bitcast(F32)
                for _ in range(3):
                    link(dve.scalar_tensor_tensor(out=rt[:, 0:c], in0=y, scalar=-0.5, in1=y,
                                                  op0=ALU.mult, op1=ALU.mult))
                    link(dve.tensor_tensor(rt[:, 0:c], rt[:, 0:c], rv[:, 0:c], ALU.mult))
                    link(dve.scalar_tensor_tensor(out=ry[:, 0:c], in0=rt[:, 0:c], scalar=1.5, in1=y,
                                                  op0=ALU.add, op1=ALU.mult))
                    y = ry[:, 0:c]
                dve.tensor_tensor(diag[:, 0:c], ident.unsqueeze(1).to_broadcast([P, c, P]),
                                  ry[:, 0:c].unsqueeze(2).to_broadcast([P, c, P]), ALU.mult).then_inc(diag_ready, 1)

            def norm_apply(name, bank, tiles, nt, src, dst_hi, dst_lo, context=None):
                base = NORM_BASE[name]
                dve.wait_ge(rstd_bc, CALL[name] + 1)
                for k in range(tiles + 1):
                    if k < tiles:
                        dve.tensor_tensor(xn[:, k % 2, 0:nt], src(k), ps[bank][:, 0:nt],
                                          ALU.mult).then_inc(xn_ready, 1)
                    if k >= 1:
                        e = k - 1
                        dve.wait_ge(nhi_ready, base + e + 1)
                        if context is not None:
                            count[0] += 1
                            dve.wait_ge(chain, count[0])
                        dve.tensor_tensor(dst_lo(e), full[:, e % 2, 0:nt], dst_hi(e).bitcast(F32),
                                          ALU.subtract).then_inc(normed, 1)
                    if context is not None and k < tiles:
                        dve.wait_ge(xn_ready, base + k + 1)
                        if k >= 2:
                            dve.wait_ge(normed, base + k - 1)
                        dve.tensor_scalar(full[:, k % 2, LAT:TOK], xn[:, k % 2, LAT:TOK], context[1](k),
                                          context[0](k), ALU.mult, ALU.add).then_inc(chain, 1)

            def residual_norm(name, nt, modulation=None):
                rsqrt(name, NORM_BANK, nt, 1.0 / D, NORM_EPS)
                if modulation is not None:
                    modulation()
                s = ("ffn0", "ab", "ffn1", "ffn2", "mla", "ffn3").index(name)
                norm_apply(name, NORM_BANK, DT, nt, lambda k: xT[:, k, 0:nt], lambda k: a_hi[:, k, 0:nt],
                           lambda k: a_lo[:, k, 0:nt],
                           [lambda k, x=x: x[:, s, 1, k:k + 1] for x in (shift, scale)] if nt == TOK else None)

            def out_tiles(s, b, w, j, nt, i=None):
                k = (lambda x: x) if i is None else (lambda x: i + x)
                for t in range(2):
                    dve.wait_ge(*((slab_done, k(w + j + 1)) if t else (tile0_done, k(b + j + 1))))
                    bank = ps[OUTB + 2 * ((b + j) % 2) + t]
                    m = 2 * j + t if i is None else i * 2 + (2 * j + t)
                    for v in range(nt // LAT):
                        c = slice(v * LAT, (v + 1) * LAT)
                        if i is None:
                            x, g = xT[:, m, c], gate[:, s, v, m:m + 1]
                        else:
                            x, g = xT[:, ds(m, 1), c].rearrange("p a n -> p (a n)"), gate[:, s, v, ds(m, 1)]
                        last = dve.scalar_tensor_tensor(out=x, in0=bank[:, c], scalar=g, in1=x,
                                                        op0=ALU.mult, op1=ALU.add)
                    last.then_inc(out_free[t], 1)

            def split_lo2(w, slot, i=None):
                dve.wait_ge(hi_ready, w + 1 if i is None else i + (w + 1))
                dve.tensor_tensor(w_lo[:, slot, HALF:SLAB], raw[:, slot, HALF:SLAB],
                                  w_hi[:, slot, HALF:SLAB].bitcast(F32), ALU.subtract).then_inc(lo2_ready, 1)

            def ffn(s, name, nt, next_norm, n0=0, modulation=None, finals=()):
                residual_norm(name, nt, modulation)
                mods = MOD_PHASES[s]
                if s == 0:
                    dve.wait_ge(cond_ready, 2)
                sub = (0, 2, 3, 5)[s]
                w, f, b = FFN_W[s], s * FFN_STEPS, B_FFN[s]
                phase = 0
                for g, size in enumerate(GROUPS):
                    with dve.Fori(0, size - 1, 2) as i:
                        for j in range(2):
                            slot = (f + j) % 2
                            if w >= W_FFN3:
                                split_lo2(w + j + 2, (w + j) % 2, i)
                            dve.wait_ge(sil_ready, i + (f + j + 1))
                            dve.tensor_tensor(prod[:, slot, 0:nt], sil[:, slot, 0:nt], ps[2 * slot + 1][:, 0:nt],
                                              ALU.mult).then_inc(pair_free, 1)
                            if phase in mods:
                                mod_dot(2 * j, i * 8 + 16 * (n0 // 4 + 1), i * 2 + (n0 + 2 * j))
                            dve.wait_ge(hhi_ready, i + (f + j + 1))
                            hi = h_hi[:, ds(i + j, 1), 0:nt].rearrange("p a n -> p (a n)").bitcast(F32)
                            lo = h_lo[:, ds(i + j, 1), 0:nt].rearrange("p a n -> p (a n)")
                            dve.tensor_tensor(lo, prod[:, slot, 0:nt], hi, ALU.subtract).then_inc(hid_ready, 1)
                            if phase in mods:
                                mod_dot(2 * j + 1, i * 8 + 16 * (n0 // 4 + 1), i * 2 + (n0 + 2 * j + 1))
                        if phase in mods:
                            mod_store(i * 2 + n0, i * 2 + (n0 + 4))
                    if phase in mods:
                        n0 += 2 * size
                    phase += 1
                    w, f = w + size, f + size
                    if g < len(finals) and finals[g]:
                        dve.wait_ge(mod_cols, n0)
                        finalize(*finals[g])
                    last = g == len(GROUPS) - 1
                    if last:
                        zero_sum(RES[next_norm])
                    if w + 4 == N_SLABS:
                        for j in range(4):
                            out_tiles(sub, b, w, j, nt)
                            if j < 2:
                                split_lo2(w + j + 2, (w + j) % 2)
                            add_square(RES[next_norm], j, 0, nt)
                            add_square(RES[next_norm], j, 1, nt)
                        continue
                    with dve.Fori(0, 3, 2) as i:
                        for j in range(2):
                            out_tiles(sub, b, w, j, nt, i)
                            if w >= W_FFN3:
                                split_lo2(w + j + 2, (w + j) % 2, i)
                            if phase in mods:
                                mod_dot(2 * j, i * 8 + 16 * (n0 // 4 + 1), i * 2 + (n0 + 2 * j))
                            if last:
                                add_square(RES[next_norm], j, 0, nt, i)
                                add_square(RES[next_norm], j, 1, nt, i)
                            if phase in mods:
                                mod_dot(2 * j + 1, i * 8 + 16 * (n0 // 4 + 1), i * 2 + (n0 + 2 * j + 1))
                        if phase in mods:
                            mod_store(i * 2 + n0, i * 2 + (n0 + 4))
                    if phase in mods:
                        n0 += 8
                    phase += 1
                    w, b = w + 4, b + 4
                return n0

            def rotate(src, dst):
                sw, t1, t2 = sq[:, 0, 0:LAT], sq[:, 0, LAT:TOK], sq[:, 1, 0:LAT]
                dve.stream_shuffle(sw, src, [(i + 16) % 32 for i in range(32)])
                link(dve.tensor_tensor(t1, src, cos, ALU.mult))
                link(dve.tensor_tensor(t2, sw, sin, ALU.mult))
                return dve.tensor_tensor(dst, t1, t2, ALU.add)

            def pieces(j, piece):
                src, hi, lo, runs, (s, value) = piece
                dve.wait_ge(s, value)
                if runs:
                    r = ROPE_INDEX[j]
                    if len(runs) == 1:
                        dve.wait_ge(rope_ctx, CTX_INDEX[j] + 1)
                    for n, (c0, c1) in enumerate(runs):
                        ins = rotate(src[:, c0:c1], full[:, r % 2, c0:c1])
                        if n == len(runs) - 1:
                            ins.then_inc(rope_full, 1)
                        else:
                            link(ins)
                    whole = full[:, r % 2]
                else:
                    whole = src[:]
                dve.wait_ge(piece_hi, j + 1)
                dve.tensor_tensor(lo, whole, hi.bitcast(F32), ALU.subtract).then_inc(piece_lo, 1)

            def conv_taps(first, last):
                for n in range(first, last):
                    c, tap = OWN[n]
                    x = ypad[:, c, :, tap:tap + LAT]
                    acc = conv[:, c].rearrange("p (v n) -> p v n", v=2)
                    col = vec[:, V_WDW + c * TAPS + tap:V_WDW + c * TAPS + tap + 1]
                    if tap == 0:
                        ins = dve.tensor_scalar(acc, x, col, vec[:, V_BDW + c:V_BDW + c + 1], ALU.mult, ALU.add)
                    else:
                        dve.wait_ge(conv_op, OWN_AFTER[n])
                        ins = dve.scalar_tensor_tensor(out=acc, in0=x, scalar=col, in1=acc,
                                                       op0=ALU.mult, op1=ALU.add)
                    ins.then_inc(conv_op, 1)

            def attention(units, u0, sink, factor, pt_hi_buf, pt_lo_buf, out_to, beside=None):
                for i in range(len(units) + 6):
                    if i < len(units):
                        h, qts, at = units[i]
                        b = slice(at, at + len(qts))
                        dve.wait_ge(scores_done, u0 + i + 1)
                        link(dve.tensor_reduce(smax[:, b], ps[S_BANK[i % 3]][:].rearrange("p (b n) -> p b n", b=len(qts)),
                                               AX.X, ALU.max))
                        if sink:
                            ins = dve.tensor_scalar(nmax[:, b], smax[:, b], -factor, nsink[:, h:h + 1],
                                                    ALU.mult, ALU.min)
                        else:
                            ins = dve.tensor_scalar(nmax[:, b], smax[:, b], -factor, None, ALU.mult)
                        ins.then_inc(nmax_ready, 1)
                    if 1 <= i < len(units) + 1:
                        e = i - 1
                        h, qts, at = units[e]
                        b = slice(at, at + len(qts))
                        dve.wait_ge(exp_done, u0 + e + 1)
                        if sink:
                            dve.wait_ge(sink_done, u0 + e + 1)
                            link(dve.tensor_tensor(den[:, b], den[:, b], esink[:, b], ALU.add))
                        link(dve.reciprocal(rinv[:, b], den[:, b]))
                        if e >= 2:
                            dve.wait_ge(pt_done, u0 + e - 1)
                        for n in range(len(qts)):
                            last = dve.tensor_scalar(rdiag[:, e % 2, n], ident, rinv[:, at + n:at + n + 1], None,
                                                     ALU.mult)
                        last.then_inc(rdiag_ready, 1)
                    if beside is not None and i < len(units):
                        beside(i)
                    if 3 <= i < len(units) + 3:
                        e = i - 3
                        qts = units[e][1]
                        dve.wait_ge(pt_hi, u0 + e + 1)
                        dve.tensor_tensor(pt_unit(pt_lo_buf, e, qts), pt_bank(e, qts),
                                          pt_unit(pt_hi_buf, e, qts).bitcast(F32), ALU.subtract).then_inc(pt_lo, 1)
                    if i >= 7 and i % 2:
                        p = (i - 7) // 2
                        dve.wait_ge(ot_hi, u0 // 2 + p + 1)
                        for (rows, c, lo), (_, _, hi) in zip(out_to(a_lo, p), out_to(a_hi, p)):
                            last = dve.tensor_tensor(lo, ps[O_BANK[p % 2]][rows, c], hi.bitcast(F32), ALU.subtract)
                        last.then_inc(ot_lo, 1)

            def mixer_out(s, w, b, nt, next_norm):
                zero_sum(RES[next_norm])
                for j in range(4):
                    out_tiles(s, b, w, j, nt)
                    if w + j + 2 >= W_FFN3:
                        split_lo2(w + j + 2, (w + j) % 2)
                    add_square(RES[next_norm], j, 0, nt)
                    add_square(RES[next_norm], j, 1, nt)

            dve.memset(rt[:], 0.0).then_inc(out_free[0], 2)
            dve.memset(mtmp[:], 0.0).then_inc(out_free[1], 2)
            dve.memset(rinv[:], 0.0).then_inc(pair_free, 2)
            dve.memset(unread[:], 0.0).then_inc(mod_first, MOD_FIRST + 1)
            zero_sum(0)
            for sl in range(4):
                add_square(0, sl, 0, TOK)
                add_square(0, sl, 1, TOK)

            def mod_to_rows(c):
                dve.wait_ge(mod_dots, DT * (c + 1))
                dve.tensor_copy(work[0:2, 2 * c], ps[2 * c][0:2, :])
                dve.tensor_copy(work[0:2, 2 * c + 1], ps[2 * c + 1][0:2, :]).then_inc(mod_rows, 1)

            mod_to_rows(0)

            def first_modulation():
                mod_to_rows(1)
                for c in range(2):
                    dve.wait_ge(mod_turned, c + 1)
                    dve.tensor_copy(modc[:, :, c * DT:(c + 1) * DT],
                                    ps[OUTB + c][:, 0:2 * DT].rearrange("p (m v) -> p v m", v=2)).then_inc(mod_cols, DT)
                dve.wait_ge(mod_cols, MOD_FIRST)
                dve.wait_ge(in_small, 32)
                finalize(0, 0, ("shift", "scale"))
                link(dve.tensor_scalar(nsink[:], vec[:, V_SINK:V_SINK + HEADS], -1.0, None, ALU.mult))

            n0 = ffn(0, "ffn0", TOK, "ab", MOD_FIRST, first_modulation, ((0, 0, ("gate",)), (0, 1)))
            dve.wait_ge(mod_cols, n0)

            residual_norm("ab", TOK)
            finalize(0, 2)
            dve.wait_ge(gp_const, 2)
            for c in range(CT):
                dve.wait_ge(glu_sig, c + 1)
                dve.tensor_tensor(ypad[:, c, :, PAD:PAD + LAT], ps[2 * (c % 2)][:].rearrange("p (v n) -> p v n", v=2),
                                  sil[:, c % 2].rearrange("p (v n) -> p v n", v=2), ALU.mult).then_inc(glu_done, 1)
                dve.wait_ge(glu_done, c + 1)
                conv_taps(TAPS_AFTER[c], TAPS_AFTER[c + 1])
            at = TAPS_AFTER[4]
            for j, taps in enumerate(TAPS_PIECE):
                pieces(j, AB_PIECES[j])
                conv_taps(at, at + taps)
                at += taps

            def ab_beside(i):
                if i < 2:
                    pieces(AB_EARLY + i, AB_PIECES[AB_EARLY + i])
                else:
                    conv_taps(min(at + 2 * i - 4, CONV_OPS), min(at + 2 * i - 2, CONV_OPS))
                if i == LN_UNIT:
                    dve.wait_ge(conv_op, CONV_OPS)
                    dve.wait_ge(tap_add, CONV_ADDS)
                    link(dve.tensor_tensor(ss[:, 0], conv[:, 0], conv[:, 1], ALU.add))
                    link(dve.tensor_tensor(ss[:, 1], conv[:, 2], conv[:, 3], ALU.add))
                    dve.tensor_tensor(ss[:, 0], ss[:, 0], ss[:, 1], ALU.add).then_inc(ln_sum, 1)
                if i in (LN_UNIT + 2, LN_UNIT + 3):
                    dve.wait_ge(ln_mean, 1)
                    for c in (0, 1) if i == LN_UNIT + 2 else (2, 3):
                        dve.scalar_tensor_tensor(out=conv[:, c], in0=ps[LN_BANK][:], scalar=-1.0 / B_CH,
                                                 in1=conv[:, c], op0=ALU.mult, op1=ALU.add).then_inc(ln_cent, 1)
                if i == LN_UNIT + 4:
                    dve.wait_ge(stat_sq, 2)
                    dve.tensor_tensor(ss[:, 0], sq[:, 0], sq[:, 1], ALU.add).then_inc(stat_add, 1)
                if i == LN_UNIT + 5:
                    dve.wait_ge(stat_sq, 4)
                    link(dve.tensor_tensor(ss[:, 1], sq[:, 0], sq[:, 1], ALU.add))
                    dve.wait_ge(stat_add, 1)
                    dve.tensor_tensor(ss[:, 0], ss[:, 0], ss[:, 1], ALU.add).then_inc(stat_add, 1)
                if i == LN_UNIT + 6:
                    rsqrt("ln", LN_BANK, TOK, 1.0 / B_CH, LN_EPS)
            attention(AB_UNITS, 0, True, A_DIM ** -0.5, *AB_PT, ab_out, ab_beside)
            norm_apply("ln", LN_BANK, CT, TOK, lambda k: conv[:, k], lambda k: a_hi[:, 4 + k], lambda k: a_lo[:, 4 + k])
            mixer_out(1, W_AB + 7, B_AB, TOK, "ffn1")

            n0 = ffn(1, "ffn1", TOK, "ffn2", n0, None, ((), (1, 0), (1, 1)))
            n0 = ffn(2, "ffn2", TOK, "mla", n0)
            assert n0 == 2 * MODT

            residual_norm("mla", TOK)
            dve.wait_ge(mod_cols, 2 * MODT)
            finalize(1, 2)
            for i, nt in ((0, LAT), (1, TOK)):
                dve.wait_ge(stat_sq, CT + 2 * i + 2)
                dve.tensor_tensor(ss[:, i, 0:nt], sq[:, 0, 0:nt], sq[:, 1, 0:nt], ALU.add).then_inc(stat_ready, 1)
            rsqrt("cq", NORM_BANK, LAT, 1.0 / LORA, NORM_EPS)
            dve.wait_ge(lat_copy, 2)
            norm_apply("cq", NORM_BANK, 2, LAT, lambda k: spare[:, k * LAT:(k + 1) * LAT],
                       lambda k: l_hi[:, 0, k * LAT:(k + 1) * LAT], lambda k: l_lo[:, 0, k * LAT:(k + 1) * LAT])
            rsqrt("ckv", NORM_BANK + 1, TOK, 1.0 / LORA, NORM_EPS)
            dve.wait_ge(lat_copy, 4)
            norm_apply("ckv", NORM_BANK + 1, 2, TOK, lambda k: spare[:, (1 + k) * TOK:(2 + k) * TOK],
                       lambda k: l_hi[:, 1 + k], lambda k: l_lo[:, 1 + k])
            for j in range(len(MLA_PIECES)):
                pieces(N_AB + j, MLA_PIECES[j])
            attention(MLA_UNITS, len(AB_UNITS), False, (NOPE + ROPE) ** -0.5, *MLA_PT, mla_out)
            mixer_out(4, W_MLA + 6, B_MLA, LAT, "ffn3")

            ffn(3, "ffn3", LAT, "final")
            rsqrt("final", NORM_BANK, LAT, 1.0 / D, NORM_EPS)
            dve.wait_ge(rstd_bc, CALL["final"] + 1)
            for k in range(DT):
                if k >= 2:
                    dve.wait_ge(y_ready, k - 1)
                dve.tensor_tensor(xn[:, k % 2, 0:LAT], xT[:, k, 0:LAT], ps[NORM_BANK][:, 0:LAT],
                                  ALU.mult).then_inc(xn_ready, 1)

        @block.tensor
        def _(pe):
            def passes(dst, lhs_hi, lhs_lo, rhs_hi, rhs_lo, start, stop):
                pe.matmul(dst, lhs_lo, rhs_hi, start=start, stop=False, skip_group_check=True)
                pe.matmul(dst, lhs_hi, rhs_lo, start=False, stop=False, skip_group_check=True)
                return pe.matmul(dst, lhs_hi, rhs_hi, start=False, stop=stop, skip_group_check=True)

            def weights(slot, c0, n=P):
                return w_hi[:, slot, c0:c0 + n], w_lo[:, slot, c0:c0 + n]

            def two_tiles(slot, banks, nt, name=None):
                for k in range(DT):
                    if name is not None:
                        pe.wait_ge(normed, NORM_BASE[name] + k + 1)
                    for t in range(2):
                        last = passes(ps[banks[t]][:, 0:nt], *weights(slot, t * HALF + k * P),
                                      a_hi[:, k, 0:nt], a_lo[:, k, 0:nt], k == 0, k == DT - 1)
                return last

            def token_colsum(bank, sums, nt):
                for c in range(nt // P):
                    last = pe.matmul(ps[bank][:, c:c + 1], sums[:, c * P:(c + 1) * P], ones[:, 0:1],
                                     start=True, stop=True)
                last.then_inc(colsum, 1)

            def token_spread(name, bank, nt):
                pe.wait_ge(diag_ready, CALL[name] + 1)
                pe.matmul(ps[bank][:, 0:nt], ones[:], diag[:].rearrange("p a n -> p (a n)")[:, 0:nt],
                          start=True, stop=True).then_inc(rstd_bc, 1)

            def token_sum(name, bank, sums, nt):
                token_colsum(bank, sums, nt)
                token_spread(name, bank, nt)

            def residual_norm(name, nt):
                n = RES[name]
                pe.wait_ge(ss_sum[1], 5 * n + 5)
                token_sum(name, NORM_BANK, ss[:, 0], nt)

            def out_slab(b, slot, j, kt, hi, lo, nt, w, i=None, waits=None):
                k0 = (lambda x: x) if i is None else (lambda x: i + x)
                pe.wait_ge(lo_ready, k0(w + j + 1))
                if w >= W_FFN3:
                    pe.wait_ge(lo2_ready, k0(w + j + 1 - W_FFN3))
                for t in range(2):
                    pe.wait_ge(out_free[t], k0(b + j + 1))
                    for k in range(kt):
                        if waits is not None and t == 0:
                            waits(k)
                        last = passes(ps[OUTB + 2 * ((b + j) % 2) + t][:, 0:nt],
                                      *weights(slot, (t * kt + k) * P), hi[:, k, 0:nt], lo[:, k, 0:nt],
                                      k == 0, k == kt - 1)
                    last.then_inc(slab_done if t else tile0_done, 1)

            def ffn(s, name, nt):
                if s:
                    residual_norm(name, nt)
                w, f, b = FFN_W[s], s * FFN_STEPS, B_FFN[s]
                for g, size in enumerate(GROUPS):
                    with pe.Fori(0, size - 1, 2) as i:
                        for j in range(2):
                            pe.wait_ge(lo_ready, i + (w + j + 1))
                            if w >= W_FFN3:
                                pe.wait_ge(lo2_ready, i + (w + j + 1 - W_FFN3))
                            pe.wait_ge(pair_free, i + (f + j + 1))
                            p = (f + j) % 2
                            two_tiles((w + j) % 2, (2 * p, 2 * p + 1), nt,
                                      name if g == 0 and j == 0 else None).then_inc(slab_done, 1)
                    w, f = w + size, f + size

                    def hidden(k, f=f, size=size):
                        if k >= size - 4:
                            pe.wait_ge(hid_ready, f - size + k + 1)
                    with pe.Fori(0, 3, 2) as i:
                        for j in range(2):
                            out_slab(b, (w + j) % 2, j, size, h_hi, h_lo, nt, w, i, hidden if j == 0 else None)
                    w, b = w + 4, b + 4

            def attention(units, u0, chunks, mask, v, pt_buf, beside=None):
                for i in range(len(units) + 5):
                    if i < len(units):
                        h, qts, _ = units[i]
                        bank = ps[S_BANK[i % 3]]
                        if i >= 3:
                            pe.wait_ge(exp_done, u0 + i - 2)
                        for qt, key0, c0, width in spans(qts):
                            parts = chunks(h, qt, key0)
                            for n, part in enumerate(parts):
                                last = passes(bank[:, c0:c0 + width], *part, n == 0, n == len(parts) - 1)
                            if mask and qt < 2:
                                m0 = P * (1 - qt)
                                last = pe.matmul(bank[:, m0:m0 + P], ident_r[:], mask_r[:, qt],
                                                 start=False, stop=True, skip_group_check=True)
                        last.then_inc(scores_done, 1)
                    if beside is not None and i < len(units):
                        beside(i)
                    if i >= 5 and i % 2:
                        p = (i - 5) // 2
                        h, qts, _ = units[2 * p]
                        n = len(qts) * P
                        pe.wait_ge(pt_lo, u0 + 2 * p + 2)
                        if p >= 2:
                            pe.wait_ge(ot_lo, u0 // 2 + p - 1)
                        tiles = TOK // n
                        for k in range(tiles):
                            at = [x[p % 2].rearrange("p a n -> p (a n)")[:, 2 * k * n:2 * (k + 1) * n]
                                  for x in pt_buf]
                            last = passes(ps[O_BANK[p % 2]][:, 0:2 * n], *v(h, qts[0][1] // P + k), *at,
                                          k == 0, k == tiles - 1)
                        last.then_inc(pv_done, 1)
                    if 2 <= i < len(units) + 2:
                        e = i - 2
                        qts = units[e][1]
                        pe.wait_ge(rdiag_ready, u0 + e + 1)
                        if e >= 2:
                            pe.wait_ge(pt_lo, u0 + e - 1)
                        for _, _, c0, width in spans(qts):
                            b = c0 // width
                            for k in range(width // P):
                                c = (k * len(qts) + b) * P
                                last = pe.matmul(ps[PT_BANK[e % 2]][:, c:c + P],
                                                 probs[:, e % 3, c0 + k * P:c0 + (k + 1) * P], rdiag[:, e % 2, b],
                                                 start=True, stop=True)
                        last.then_inc(pt_done, 1)

            pe.wait_ge(gp_const, 1)
            def turn_modulation(c):
                pe.wait_ge(mod_rows, c + 1)
                if c == 0:
                    pe.wait_ge(in_small, 16)
                for m in range(DT):
                    last = pe.transpose(ps[OUTB + c][:, 2 * m:2 * m + 2],
                                        work[0:2, 2 * c + m // 4, (m % 4) * P:(m % 4 + 1) * P], ident[0:2, 0:2])
                last.then_inc(mod_turned, 1)

            pe.wait_ge(cond_ready, 1)
            for n in range(MOD_FIRST):
                c, k = n // DT, n % DT
                pe.wait_ge(mod_loaded[n % 4], 16 * (n // 4 + 1))
                for m in range(2):
                    last = pe.matmul(ps[2 * c + m][0:2, :], ccol[:, k], mring[:, n % 4, m * 512:(m + 1) * 512],
                                     start=k == 0, stop=k == DT - 1)
                last.then_inc(mod_dots, 1)
                if n == MOD_FIRST - 5:
                    pe.wait_ge(ss_sum[1], 5)
                    token_colsum(NORM_BANK, ss[:, 0], TOK)
                if n == MOD_FIRST - 2:
                    token_spread("ffn0", NORM_BANK, TOK)
                if n in (DT + 2, MOD_FIRST - 1):
                    turn_modulation(0 if n < MOD_FIRST - 1 else 1)
            pe.wait_ge(act_const, 2)
            ffn(0, "ffn0", TOK)

            residual_norm("ab", TOK)
            w = W_AB
            for c in range(CT):
                pe.wait_ge(lo_ready, w + c + 1)
                if c >= 2:
                    pe.wait_ge(glu_done, c - 1)
                two_tiles((w + c) % 2, (2 * (c % 2), 2 * (c % 2) + 1), TOK,
                          "ab" if c == 0 else None).then_inc(slab_done, 1)
            pe.wait_ge(lo_ready, w + 5)
            pe.wait_ge(glu_done, 3)
            for t in range(2):
                for k in range(DT):
                    last = passes(ps[t][:], *weights((w + 4) % 2, t * HALF + k * P), a_hi[:, k], a_lo[:, k],
                                  k == 0, k == DT - 1)
                last.then_inc(slab_done if t else step_done, 1)
            pe.wait_ge(lo_ready, w + 6)
            pe.wait_ge(glu_done, 4)
            two_tiles((w + 5) % 2, (2, 3), TOK).then_inc(slab_done, 1)
            pe.wait_ge(v_copy, 1)
            for kt in range(4):
                last = pe.transpose(ps[6][:, kt * P:(kt + 1) * P], v_rows[:, kt * P:(kt + 1) * P], ident)
            last.then_inc(step_done, 1)
            pe.wait_ge(lo_ready, w + 7)
            pe.wait_ge(piece_lo, 1)
            two_tiles((w + 6) % 2, (0, 7), TOK).then_inc(slab_done, 1)
            pe.wait_ge(piece_lo, 3)

            def ab_chunks(h, qt, k0):
                r = slice(A_DIM * (h // 4), A_DIM * (h // 4 + 1))
                q = [x[r, h % 4, qt * P:(qt + 1) * P] for x in (h_hi, h_lo)]
                return [(*q, h_hi[r, 4, k0:TOK], h_lo[r, 4, k0:TOK])]

            def ab_v(h, kt):
                return h_hi[:, 5, kt * P:(kt + 1) * P], h_lo[:, 5, kt * P:(kt + 1) * P]
            def ab_beside(i):
                if i == 2:
                    pe.wait_ge(piece_lo, AB_EARLY)
                if i == 3:
                    pe.wait_ge(piece_lo, N_AB)
                if i == LN_UNIT + 1:
                    pe.wait_ge(ln_sum, 1)
                    pe.matmul(ps[LN_BANK][:], ones[:], ss[:, 0], start=True, stop=True).then_inc(ln_mean, 1)
                if i == LN_UNIT + 6:
                    pe.wait_ge(stat_add, 2)
                    token_colsum(LN_BANK, ss[:, 0], TOK)
            attention(AB_UNITS, 0, ab_chunks, True, ab_v, AB_PT, ab_beside)
            token_spread("ln", LN_BANK, TOK)

            def mixer_out(b, w, nt, inputs):
                for j in range(4):
                    out_slab(b, (w + j) % 2, j, DT, a_hi, a_lo, nt, w, None, inputs if j == 0 else None)

            def ab_inputs(k):
                if k < 4:
                    pe.wait_ge(ot_lo, 3 * (k + 1))
                else:
                    pe.wait_ge(normed, NORM_BASE["ln"] + k - 3)
            mixer_out(B_AB, W_AB + 7, TOK, ab_inputs)
            ffn(1, "ffn1", TOK)
            ffn(2, "ffn2", TOK)

            residual_norm("mla", TOK)
            w = W_MLA
            pe.wait_ge(lo_ready, w + 1)
            two_tiles(w % 2, (0, 1), LAT, "mla").then_inc(slab_done, 1)
            pe.wait_ge(lo_ready, w + 2)
            two_tiles((w + 1) % 2, (2, 3), TOK).then_inc(slab_done, 1)
            pe.wait_ge(lo_ready, w + 3)
            pe.wait_ge(stat_ready, 1)
            pe.wait_ge(lat_copy, 2)
            slot = (w + 2) % 2
            for k in range(DT):
                last = passes(ps[0][:], *weights(slot, k * P), a_hi[:, k], a_lo[:, k], k == 0, k == DT - 1)
            last.then_inc(step_done, 1)
            token_sum("cq", NORM_BANK, ss[:, 0], LAT)
            pe.wait_ge(stat_ready, 2)
            token_sum("ckv", NORM_BANK + 1, ss[:, 1], TOK)
            pe.wait_ge(normed, NORM_BASE["cq"] + 2)
            pe.wait_ge(lat_copy, 4)

            def queries(i, slot, c0):
                for t in range(4):
                    for k in range(2):
                        c = k * LAT
                        last = passes(ps[2 * (i % 2) + t // 2][:, (t % 2) * LAT:(t % 2 + 1) * LAT],
                                      *weights(slot, c0 + (2 * t + k) * P), l_hi[:, 0, c:c + LAT],
                                      l_lo[:, 0, c:c + LAT], k == 0, k == 1)
                return last

            def step(i, emit):
                if i >= 2:
                    pe.wait_ge(piece_lo, MLA_PIECES_BY[i - 2])
                emit().then_inc(MLA_SIGNAL[i][0], 1)

            step(1, lambda: queries(1, slot, HALF))
            pe.wait_ge(lo_ready, w + 4)
            step(2, lambda: queries(2, (w + 3) % 2, 0))
            step(3, lambda: queries(3, (w + 3) % 2, HALF))
            pe.wait_ge(normed, NORM_BASE["ckv"] + 2)
            pe.wait_ge(lo_ready, w + 5)

            def nope_keys(i):
                def emit():
                    for t in range(2):
                        m = 2 * (i - 4) + t
                        for k in range(2):
                            last = passes(ps[2 * (i % 2) + t][:], *weights((w + 4) % 2, (2 * m + k) * P),
                                          l_hi[:, 1 + k], l_lo[:, 1 + k], k == 0, k == 1)
                    return last
                return emit

            def values(i):
                def emit():
                    kt = i - 8
                    for t in range(2):
                        for k in range(2):
                            last = passes(ps[2 * (i % 2) + t][:], l_hi[:, 1 + k, kt * P:(kt + 1) * P],
                                          l_lo[:, 1 + k, kt * P:(kt + 1) * P],
                                          *weights((w + 5) % 2, k * D + t * 512, 512), k == 0, k == 1)
                    return last
                return emit
            for i in range(4, 8):
                step(i, nope_keys(i))
            pe.wait_ge(lo_ready, w + 6)
            for i in range(8, 12):
                step(i, values(i))
            pe.wait_ge(piece_lo, N_AB + len(MLA_PIECES))

            def mla_chunks(h, qt, k0):
                n, c = h // 2, (h % 2) * LAT + qt * P
                r = slice(ROPE * (h % 2), ROPE * (h % 2 + 1))
                tile = h // 2
                rn, rc = 4 + tile // 2, (tile % 2) * LAT + qt * P
                return [(q_hi[:, n, c:c + P], q_lo[:, n, c:c + P], a_hi[:, h], a_lo[:, h]),
                        (q_hi[r, rn, rc:rc + P], q_lo[r, rn, rc:rc + P], q_hi[r, 6], q_lo[r, 6])]

            def mla_v(h, kt):
                n, c = 2 * kt + h // 4, (h % 4) * C_V
                return h_hi[:, n, c:c + C_V], h_lo[:, n, c:c + C_V]
            attention(MLA_UNITS, len(AB_UNITS), mla_chunks, False, mla_v, MLA_PT)
            mixer_out(B_MLA, W_MLA + 6, LAT, lambda k: pe.wait_ge(ot_lo, AB_PAIRS + k + 1))
            ffn(3, "ffn3", LAT)
            residual_norm("final", LAT)


def _tiles(w, rows, width):
    k, m = w.shape
    return w.reshape(rows, P, m // width, width).transpose(2, 1, 0, 3)


def _ffn_slabs(w_in, w_out):
    n = D_FF // P
    gate_up = _tiles(w_in, DT, P).reshape(2, n, P, HALF)
    w_out = _tiles(w_out, n, P)
    slabs, at = [], 0
    for size in GROUPS:
        slabs.append(gate_up[:, at:at + size].transpose(1, 2, 0, 3).reshape(size, P, SLAB))
        part = w_out[:, :, at:at + size].reshape(4, 2, P, size * P).transpose(0, 2, 1, 3).reshape(4, P, 2 * size * P)
        if part.shape[2] < SLAB:
            part = np.concatenate([part, np.zeros((4, P, SLAB - part.shape[2]), part.dtype)], axis=2)
        slabs.append(part)
        at += size
    return slabs


def _pairs(w, rows):
    t = _tiles(w, rows, P)
    return t.reshape(t.shape[0] // 2, 2, P, rows * P).transpose(0, 2, 1, 3).reshape(-1, P, 2 * rows * P)


def _stream(ffn_w_in, ffn_w_out, ab_w_in, ab_w_out, c_w_dq, c_w_uq, c_w_dkv, c_w_uk, c_w_uv, c_w_o):
    aq, akv = HEADS * A_DIM, A_KV * A_DIM
    wq = ab_w_in[:, :aq].reshape(D, 2, 4, A_DIM).transpose(0, 2, 1, 3).reshape(D, aq)
    ab_w_out = np.concatenate([ab_w_out[:aq].reshape(2, 4, A_DIM, D).transpose(1, 0, 2, 3).reshape(aq, D),
                               ab_w_out[aq:]], axis=0)
    wa, wg = ab_w_in[:, aq + 2 * akv:aq + 2 * akv + B_CH], ab_w_in[:, aq + 2 * akv + B_CH:]
    wconv = np.concatenate([wa.reshape(D, CT, 1, P), wg.reshape(D, CT, 1, P)], axis=2).reshape(D, 2 * B_CH)
    wab = np.concatenate([wconv, ab_w_in[:, aq:aq + 2 * akv], wq], axis=1)
    uq = c_w_uq.reshape(LORA, HEADS, NOPE + ROPE)
    uq = np.concatenate([uq[:, :, :NOPE].reshape(LORA, -1), uq[:, :, NOPE:].reshape(LORA, -1)], axis=1)
    uq = _tiles(uq, 2, P).transpose(1, 0, 2, 3).reshape(P, 3 * HALF)
    kr = np.concatenate([c_w_dkv[:, LORA:], c_w_dkv[:, LORA:]], axis=1)
    kr = _tiles(kr, DT, P).reshape(P, HALF)
    mla = [_pairs(c_w_dq, DT), _pairs(c_w_dkv[:, :LORA], DT),
           np.concatenate([kr, uq[:, :HALF]], axis=1)[None], uq[:, HALF:][None],
           _tiles(c_w_uk, 2, P).transpose(1, 0, 2, 3).reshape(1, P, SLAB),
           c_w_uv.reshape(2, P, D).transpose(1, 0, 2).reshape(1, P, SLAB),
           _pairs(c_w_o, DT)]
    slabs = (_ffn_slabs(ffn_w_in[0, 0], ffn_w_out[0, 0]) + [_pairs(wab, DT), _pairs(ab_w_out, DT)]
             + _ffn_slabs(ffn_w_in[0, 1], ffn_w_out[0, 1]) + _ffn_slabs(ffn_w_in[1, 0], ffn_w_out[1, 0])
             + mla + _ffn_slabs(ffn_w_in[1, 1], ffn_w_out[1, 1]))
    return np.concatenate(slabs, axis=0)


def _columns(a):
    return a.reshape(-1, P).T


def _constants():
    q, k = np.arange(P)[:, None], np.arange(P)[None, :]
    mask0 = np.where(k <= q, 0.0, NEG)
    mask1 = np.where(q <= k, 0.0, NEG)
    t = np.arange(LAT)
    half = ROPE // 2
    inv = (np.float32(10000.0) ** (-np.arange(0, half, 2, dtype=np.float32) / np.float32(half))).astype(np.float32)
    row = (t // GRID_W).astype(np.float32)[:, None] * inv
    col = (t % GRID_W).astype(np.float32)[:, None] * inv
    ang = np.concatenate([row, row, col, col], axis=1).astype(np.float32)
    sign = np.tile(np.concatenate([-np.ones(half // 2), np.ones(half // 2)]), 2)
    cos, sin = np.cos(ang).T, (np.sin(ang) * sign).T
    c = np.concatenate([np.eye(P), mask0, mask1, np.tile(cos, (2, 1)), np.tile(sin, (2, 1))], axis=1)
    return np.ascontiguousarray(c, dtype=np.float32)


def kernel(x, c, ctx, c_ctx, w_mod, b_mod, g_norm, ffn_w_in, ffn_w_out, ab_w_in, a_sink, b_w_dw, b_b_dw,
           b_ln_g, b_ln_b, ab_w_out, c_w_dq, c_g_q, c_w_uq, c_w_dkv, c_g_kv, c_w_uk, c_w_uv, c_w_o, g_final):
    import concourse.bacc as bacc
    from concourse.bass_utils import run_bass_kernel_spmd

    (x, c, ctx, c_ctx, w_mod, b_mod, g_norm, ffn_w_in, ffn_w_out, ab_w_in, a_sink, b_w_dw, b_b_dw, b_ln_g, b_ln_b,
     ab_w_out, c_w_dq, c_g_q, c_w_uq, c_w_dkv, c_g_kv, c_w_uk, c_w_uv, c_w_o, g_final) = (
        np.asarray(a) for a in (x, c, ctx, c_ctx, w_mod, b_mod, g_norm, ffn_w_in, ffn_w_out, ab_w_in, a_sink, b_w_dw,
                                b_b_dw, b_ln_g, b_ln_b, ab_w_out, c_w_dq, c_g_q, c_w_uq, c_w_dkv, c_g_kv, c_w_uk,
                                c_w_uv, c_w_o, g_final))
    tokens = np.concatenate([x[0], ctx[0]], axis=0).T.reshape(DT, P, TOK).transpose(1, 0, 2)
    taps = b_w_dw[0].reshape(TAPS, CT, P).transpose(2, 1, 0).reshape(P, CT * TAPS)
    vecs = np.concatenate([_columns(g_norm), _columns(b_mod), _columns(g_final), _columns(b_b_dw), _columns(b_ln_g),
                           _columns(b_ln_b), _columns(c_g_q), _columns(c_g_kv),
                           np.broadcast_to(a_sink, (P, HEADS)), taps], axis=1)
    arrays = {
        "tokens": tokens,
        "cond": np.stack([c[0], c_ctx]),
        "cond_cols": np.stack([c[0], c_ctx]).reshape(2, DT, P).transpose(2, 1, 0),
        "vecs": vecs,
        "consts": _constants(),
        "wmod": np.concatenate([_tiles(w_mod[0][:, :MOD_FIRST * P], DT, D).transpose(0, 2, 1, 3).reshape(-1, P, D),
                                w_mod.transpose(0, 2, 1).reshape(2 * MODT, P, D)[MOD_FIRST:]], axis=0),
        "wstream": _stream(ffn_w_in, ffn_w_out, ab_w_in[0], ab_w_out[0], c_w_dq[0], c_w_uq[0], c_w_dkv[0], c_w_uk[0],
                           c_w_uv[0], c_w_o[0]),
    }
    arrays = {k: np.ascontiguousarray(a) for k, a in arrays.items()}
    nc = bacc.Bacc("TRN2", target_bir_lowering=False, num_devices=1)
    args = [nc.dram_tensor(k, a.shape, mybir.dt.from_np(a.dtype), kind="ExternalInput").ap()
            for k, a in arrays.items()]
    out = nc.dram_tensor("out", [P, DT, LAT], mybir.dt.float32, kind="ExternalOutput").ap()
    build(nc, *args, out)
    result = run_bass_kernel_spmd(nc, [arrays], core_ids=[0]).results[0]["out"]
    return np.ascontiguousarray(result.transpose(2, 1, 0).reshape(LAT, D))[None]
```
